# Optimizing a Trainium2 kernel written in Bass

```python
import math
import jax, jax.numpy as jnp
from jax import lax
import numpy as np

D_MODEL = 1024
BATCH = 1
SEQ = 1024
DEPTH = 1
DEC_BATCH = 8
DEC_SEQ = 4
PAST_LEN = 1024
PAGE_SIZE = 128

MLA_HEADS = 8
MLA_NOPE = 64
MLA_ROPE = 32
MLA_V = 64
MLA_Q_LORA = 256
MLA_KV_LORA = 128
MLA_SCALE = (MLA_NOPE + MLA_ROPE) ** -0.5
Q_BLOCK = 128
RET_HEADS = 4
RET_DK = 128
RET_DV = 128
RET_CHUNK = 128
N_EXPERTS = 64
N_GROUPS = 8
TOPK_GROUPS = 4
TOP_K = 6
EXPERT_FF = 256
SHARED_FF = 256
ROUTED_SCALE = 2.5
MOE_BLOCK = 128
ROPE_BASE = 10000.0
LN_EPS = 1e-5
RMS_EPS = 1e-6
DEEPNORM_ALPHA = (2 * DEPTH) ** 0.25
DEEPNORM_BETA = (8 * DEPTH) ** -0.25
IN_SPLITS = (MLA_Q_LORA, MLA_KV_LORA, MLA_ROPE, RET_HEADS * RET_DK, RET_HEADS * RET_DK,
             RET_HEADS * RET_DV, RET_HEADS * RET_DV, D_MODEL, D_MODEL)
IN_WIDTH = sum(IN_SPLITS)

kernel_name = 'hybrid_mla_retention_moe_deepnorm_step'

def layer_norm(x, g, b):
    xf = x.astype(jnp.float32)
    mu = jnp.mean(xf, axis=-1, keepdims=True)
    var = jnp.mean(jnp.square(xf - mu), axis=-1, keepdims=True)
    return ((xf - mu) * lax.rsqrt(var + LN_EPS)).astype(x.dtype) * g + b

def rms_norm(x, g):
    xf = x.astype(jnp.float32)
    inv = lax.rsqrt(jnp.mean(jnp.square(xf), axis=-1, keepdims=True) + RMS_EPS)
    return (xf * inv).astype(x.dtype) * g

def rope(x, pos):
    half = x.shape[-1] // 2
    inv = ROPE_BASE ** (-jnp.arange(half, dtype=jnp.float32) / half)
    ang = pos.astype(jnp.float32)[:, None] * inv[None, :]
    cos, sin = jnp.cos(ang), jnp.sin(ang)
    if x.ndim == 4:
        cos, sin = cos[:, None, :], sin[:, None, :]
    xf = x.astype(jnp.float32)
    x1, x2 = xf[..., :half], xf[..., half:]
    return jnp.concatenate([x1 * cos - x2 * sin, x2 * cos + x1 * sin], axis=-1).astype(x.dtype)

def mixer_inputs(x, pos, w_in, q_norm_g, w_q_up, kv_norm_g):
    B, L, _ = x.shape
    cuts = [int(c) for c in np.cumsum(IN_SPLITS)[:-1]]
    cq, ckv, kr, rq, rk, rv, rg, ga, gb = jnp.split(x @ w_in, cuts, axis=-1)
    q = (rms_norm(cq, q_norm_g) @ w_q_up).reshape(B, L, MLA_HEADS, MLA_NOPE + MLA_ROPE)
    q_nope = q[..., :MLA_NOPE]
    q_rope = rope(q[..., MLA_NOPE:], pos)
    c_kv = rms_norm(ckv, kv_norm_g)
    k_rope = rope(kr, pos)
    rq = rope(rq.reshape(B, L, RET_HEADS, RET_DK), pos)
    rk = rope(rk.reshape(B, L, RET_HEADS, RET_DK), pos) * (RET_DK ** -0.5)
    rv = rv.reshape(B, L, RET_HEADS, RET_DV)
    return q_nope, q_rope, c_kv, k_rope, rq, rk, rv, rg, ga, gb

def mla_prompt(q_nope, q_rope, k_nope, k_rope, v):
    B, S, H, _ = q_nope.shape
    kpos = jnp.arange(S)

    def one_block(i):
        qn = lax.dynamic_slice_in_dim(q_nope, i * Q_BLOCK, Q_BLOCK, axis=1)
        qr = lax.dynamic_slice_in_dim(q_rope, i * Q_BLOCK, Q_BLOCK, axis=1)
        s = (jnp.einsum('bqhd,bkhd->bhqk', qn, k_nope)
             + jnp.einsum('bqhr,bkr->bhqk', qr, k_rope)).astype(jnp.float32) * MLA_SCALE
        qpos = i * Q_BLOCK + jnp.arange(Q_BLOCK)
        s = jnp.where(kpos[None, :] <= qpos[:, None], s, -jnp.inf)
        p = jax.nn.softmax(s, axis=-1).astype(v.dtype)
        return jnp.einsum('bhqk,bkhd->bqhd', p, v)

    o = lax.map(one_block, jnp.arange(S // Q_BLOCK))
    return o.transpose(1, 0, 2, 3, 4).reshape(B, S, H * MLA_V)

def mla_sample(q_nope, q_rope, c_kv, k_rope, past_ckv, past_kr, w_uk, w_uv):
    B, Q, H, _ = q_nope.shape
    P = past_ckv.shape[1]
    q_lat = jnp.einsum('bqhn,chn->bqhc', q_nope, w_uk.reshape(MLA_KV_LORA, MLA_HEADS, MLA_NOPE))
    s_past = (jnp.einsum('bqhc,bkc->bhqk', q_lat, past_ckv)
              + jnp.einsum('bqhr,bkr->bhqk', q_rope, past_kr))
    s_new = (jnp.einsum('bqhc,bkc->bhqk', q_lat, c_kv)
             + jnp.einsum('bqhr,bkr->bhqk', q_rope, k_rope))
    causal = jnp.arange(Q)[None, :] <= jnp.arange(Q)[:, None]
    s_new = jnp.where(causal, s_new.astype(jnp.float32), -jnp.inf)
    s = jnp.concatenate([s_past.astype(jnp.float32), s_new], axis=-1) * MLA_SCALE
    p = jax.nn.softmax(s, axis=-1).astype(past_ckv.dtype)
    o_lat = (jnp.einsum('bhqk,bkc->bqhc', p[..., :P], past_ckv)
             + jnp.einsum('bhqk,bkc->bqhc', p[..., P:], c_kv))
    o = jnp.einsum('bqhc,chv->bqhv', o_lat, w_uv.reshape(MLA_KV_LORA, MLA_HEADS, MLA_V))
    return o.reshape(B, Q, H * MLA_V)

def retention_chunked(q, k, v, s0):
    B, L, H, _ = q.shape
    C = math.gcd(L, RET_CHUNK)
    n = L // C
    lg = jnp.log(1.0 - 2.0 ** (-5.0 - jnp.arange(H, dtype=jnp.float32)))
    idx = jnp.arange(C, dtype=jnp.float32)
    diff = idx[:, None] - idx[None, :]
    dmask = jnp.where(diff >= 0, jnp.exp(jnp.maximum(diff, 0.0)[None] * lg[:, None, None]), 0.0)
    q_dec = jnp.exp((idx[:, None] + 1.0) * lg[None, :])
    k_dec = jnp.exp((C - 1.0 - idx)[:, None] * lg[None, :])
    s_dec = jnp.exp(C * lg)

    def to_chunks(t):
        return t.astype(jnp.float32).reshape(B, n, C, H, t.shape[-1]).transpose(1, 0, 2, 3, 4)

    def step(S, xs):
        qc, kc, vc = xs
        att = jnp.einsum('bihd,bjhd->bhij', qc, kc) * dmask[None]
        o = (jnp.einsum('bhij,bjhv->bihv', att, vc)
             + jnp.einsum('bihd,bhdv->bihv', qc * q_dec[None, :, :, None], S))
        S = S * s_dec[None, :, None, None] + jnp.einsum('bjhd,bjhv->bhdv', kc * k_dec[None, :, :, None], vc)
        return S, o

    S, o = lax.scan(step, s0.astype(jnp.float32), (to_chunks(q), to_chunks(k), to_chunks(v)))
    o = o.transpose(1, 0, 2, 3, 4).reshape(B, L, H, v.shape[-1])
    return o, S.astype(s0.dtype)

def head_norm(o, g, dtype):
    mu = jnp.mean(o, axis=-1, keepdims=True)
    var = jnp.mean(jnp.square(o - mu), axis=-1, keepdims=True)
    n = (o - mu) * lax.rsqrt(var + LN_EPS)
    B, L = o.shape[:2]
    return n.reshape(B, L, -1).astype(dtype) * g

def swiglu(x, wg, wu, wd):
    return (jax.nn.silu(x @ wg) * (x @ wu)) @ wd

def route(h2d, w_router, router_bias):
    T = h2d.shape[0]
    scores = jax.nn.sigmoid(h2d.astype(jnp.float32) @ w_router.astype(jnp.float32))
    sel = scores + router_bias.astype(jnp.float32)[None, :]
    grp = sel.reshape(T, N_GROUPS, N_EXPERTS // N_GROUPS)
    grp_score = jnp.sum(lax.top_k(grp, 2)[0], axis=-1)
    _, gidx = lax.top_k(grp_score, TOPK_GROUPS)
    gmask = jnp.sum(jax.nn.one_hot(gidx, N_GROUPS, dtype=jnp.float32), axis=-2)
    emask = jnp.repeat(gmask, N_EXPERTS // N_GROUPS, axis=-1)
    _, eidx = lax.top_k(jnp.where(emask > 0, sel, -jnp.inf), TOP_K)
    w = jnp.take_along_axis(scores, eidx, axis=-1)
    w = w / jnp.sum(w, axis=-1, keepdims=True) * ROUTED_SCALE
    return eidx, w

def routed_experts(x2d, eidx, ew, w_gate, w_up, w_down):
    T, D = x2d.shape
    A = T * TOP_K
    flat_e = eidx.reshape(A)
    flat_w = ew.reshape(A).astype(x2d.dtype)
    flat_t = jnp.arange(A, dtype=jnp.int32) // TOP_K
    order = jnp.argsort(flat_e)
    se, st, sw = flat_e[order], flat_t[order], flat_w[order]
    counts = jnp.bincount(flat_e, length=N_EXPERTS)
    padded = (counts + MOE_BLOCK - 1) // MOE_BLOCK * MOE_BLOCK
    pad_end = jnp.cumsum(padded)
    pad_start = pad_end - padded
    start = jnp.cumsum(counts) - counts
    dest = pad_start[se] + jnp.arange(A, dtype=jnp.int32) - start[se]
    n_blocks = (A + N_EXPERTS * (MOE_BLOCK - 1) + MOE_BLOCK - 1) // MOE_BLOCK
    P = n_blocks * MOE_BLOCK
    row_tok = jnp.zeros((P,), jnp.int32).at[dest].set(st)
    row_w = jnp.zeros((P,), x2d.dtype).at[dest].set(sw)
    blk_e = jnp.minimum(jnp.searchsorted(pad_end, jnp.arange(n_blocks) * MOE_BLOCK, side='right'),
                        N_EXPERTS - 1)
    xb = x2d[row_tok].reshape(n_blocks, MOE_BLOCK, D)

    def expert_block(args):
        xblk, e = args
        return swiglu(xblk, w_gate[e], w_up[e], w_down[e])

    yb = lax.map(expert_block, (xb, blk_e)).reshape(P, D)
    return jax.ops.segment_sum(yb * row_w[:, None], row_tok, num_segments=T)

def merge_and_channel_mix(x, o_mla, o_ret, rg, ga, gb, ret_gn_g, w_mla_o, w_ret_o, w_out,
                          ln1_g, ln1_b, w_router, router_bias, w_exp_gate, w_exp_up, w_exp_down,
                          w_sh_gate, w_sh_up, w_sh_down, ln2_g, ln2_b):
    B, L, D = x.shape
    ret = jax.nn.silu(rg) * head_norm(o_ret, ret_gn_g, x.dtype)
    y_a = o_mla @ w_mla_o
    y_b = ret @ w_ret_o
    mixed = (jax.nn.sigmoid(ga) * y_a + jax.nn.sigmoid(gb) * y_b) @ w_out
    h = layer_norm(DEEPNORM_ALPHA * x + mixed, ln1_g, ln1_b)
    h2d = h.reshape(B * L, D)
    eidx, ew = route(h2d, w_router, router_bias)
    ffn = routed_experts(h2d, eidx, ew, w_exp_gate, w_exp_up, w_exp_down) + swiglu(h2d, w_sh_gate, w_sh_up, w_sh_down)
    return layer_norm(DEEPNORM_ALPHA * h + ffn.reshape(B, L, D), ln2_g, ln2_b)

def setup_inputs(seed: int = 0) -> dict:
    key = jax.random.key(seed)
    ks = jax.random.split(key, 28)
    f32 = jnp.float32

    def nrm(k, shape, scale):
        return jax.random.normal(k, shape, f32) * scale

    n_pages = PAST_LEN // PAGE_SIZE
    n_used = DEC_BATCH * n_pages
    n_phys = n_used + max(1, n_used // 4)
    page_table = jax.random.permutation(ks[0], n_phys)[:n_used].reshape(DEC_BATCH, n_pages).astype(jnp.int32)
    col_scale = jnp.concatenate([jnp.ones((sum(IN_SPLITS[:5]),), f32),
                                 jnp.full((IN_SPLITS[5],), DEEPNORM_BETA, f32),
                                 jnp.ones((sum(IN_SPLITS[6:]),), f32)])
    hv = MLA_HEADS * MLA_V
    rvw = RET_HEADS * RET_DV
    b = DEEPNORM_BETA
    return {
        'x_prompt': nrm(ks[1], (BATCH, SEQ, D_MODEL), 1.0),
        'x_sample': nrm(ks[2], (DEC_BATCH, DEC_SEQ, D_MODEL), 1.0),
        'cache_ckv': nrm(ks[3], (n_phys, PAGE_SIZE, MLA_KV_LORA), 1.0),
        'cache_krope': nrm(ks[4], (n_phys, PAGE_SIZE, MLA_ROPE), 1.0),
        'state_ret': nrm(ks[5], (DEC_BATCH, RET_HEADS, RET_DK, RET_DV), 0.5),
        'page_table': page_table,
        'w_in': nrm(ks[6], (D_MODEL, IN_WIDTH), D_MODEL ** -0.5) * col_scale[None, :],
        'q_norm_g': 1.0 + nrm(ks[7], (MLA_Q_LORA,), 0.02),
        'w_q_up': nrm(ks[8], (MLA_Q_LORA, MLA_HEADS * (MLA_NOPE + MLA_ROPE)), MLA_Q_LORA ** -0.5),
        'kv_norm_g': 1.0 + nrm(ks[9], (MLA_KV_LORA,), 0.02),
        'w_uk': nrm(ks[10], (MLA_KV_LORA, MLA_HEADS * MLA_NOPE), MLA_KV_LORA ** -0.5),
        'w_uv': nrm(ks[11], (MLA_KV_LORA, hv), MLA_KV_LORA ** -0.5 * b),
        'ret_gn_g': 1.0 + nrm(ks[12], (rvw,), 0.02),
        'w_mla_o': nrm(ks[13], (hv, D_MODEL), hv ** -0.5 * b),
        'w_ret_o': nrm(ks[14], (rvw, D_MODEL), rvw ** -0.5 * b),
        'w_out': nrm(ks[15], (D_MODEL, D_MODEL), D_MODEL ** -0.5 * b),
        'ln1_g': 1.0 + nrm(ks[16], (D_MODEL,), 0.02),
        'ln1_b': nrm(ks[17], (D_MODEL,), 0.02),
        'w_router': nrm(ks[18], (D_MODEL, N_EXPERTS), D_MODEL ** -0.5),
        'router_bias': nrm(ks[19], (N_EXPERTS,), 0.01),
        'w_exp_gate': nrm(ks[20], (N_EXPERTS, D_MODEL, EXPERT_FF), D_MODEL ** -0.5 * b),
        'w_exp_up': nrm(ks[21], (N_EXPERTS, D_MODEL, EXPERT_FF), D_MODEL ** -0.5 * b),
        'w_exp_down': nrm(ks[22], (N_EXPERTS, EXPERT_FF, D_MODEL), EXPERT_FF ** -0.5 * b),
        'w_sh_gate': nrm(ks[23], (D_MODEL, SHARED_FF), D_MODEL ** -0.5 * b),
        'w_sh_up': nrm(ks[24], (D_MODEL, SHARED_FF), D_MODEL ** -0.5 * b),
        'w_sh_down': nrm(ks[25], (SHARED_FF, D_MODEL), SHARED_FF ** -0.5 * b),
        'ln2_g': 1.0 + nrm(ks[26], (D_MODEL,), 0.02),
        'ln2_b': nrm(ks[27], (D_MODEL,), 0.02),
    }

def reference(x_prompt, x_sample, cache_ckv, cache_krope, state_ret, page_table,
              w_in, q_norm_g, w_q_up, kv_norm_g, w_uk, w_uv, ret_gn_g, w_mla_o, w_ret_o, w_out,
              ln1_g, ln1_b, w_router, router_bias, w_exp_gate, w_exp_up, w_exp_down,
              w_sh_gate, w_sh_up, w_sh_down, ln2_g, ln2_b):
    y_p, y_s = x_prompt, x_sample
    for _ in range(DEPTH):
        B, S = y_p.shape[:2]
        pos_p = jnp.arange(S)
        qn, qr, ckv_p, kr_p, rq, rk, rv, rg, ga, gb = mixer_inputs(y_p, pos_p, w_in, q_norm_g, w_q_up, kv_norm_g)
        k_nope = (ckv_p @ w_uk).reshape(B, S, MLA_HEADS, MLA_NOPE)
        v = (ckv_p @ w_uv).reshape(B, S, MLA_HEADS, MLA_V)
        o_mla = mla_prompt(qn, qr, k_nope, kr_p, v)
        s0 = jnp.zeros((B, RET_HEADS, RET_DK, RET_DV), y_p.dtype)
        o_ret, ret_p = retention_chunked(rq, rk, rv, s0)
        y_p_new = merge_and_channel_mix(y_p, o_mla, o_ret, rg, ga, gb, ret_gn_g, w_mla_o, w_ret_o, w_out,
                                        ln1_g, ln1_b, w_router, router_bias, w_exp_gate, w_exp_up, w_exp_down,
                                        w_sh_gate, w_sh_up, w_sh_down, ln2_g, ln2_b)
        DB, Q = y_s.shape[:2]
        pos_s = PAST_LEN + jnp.arange(Q)
        qn_s, qr_s, ckv_s, kr_s, rq_s, rk_s, rv_s, rg_s, ga_s, gb_s = mixer_inputs(y_s, pos_s, w_in, q_norm_g, w_q_up, kv_norm_g)
        past_ckv = cache_ckv[page_table].reshape(DB, -1, MLA_KV_LORA)
        past_kr = cache_krope[page_table].reshape(DB, -1, MLA_ROPE)
        o_mla_s = mla_sample(qn_s, qr_s, ckv_s, kr_s, past_ckv, past_kr, w_uk, w_uv)
        o_ret_s, ret_s = retention_chunked(rq_s, rk_s, rv_s, state_ret)
        y_s_new = merge_and_channel_mix(y_s, o_mla_s, o_ret_s, rg_s, ga_s, gb_s, ret_gn_g, w_mla_o, w_ret_o, w_out,
                                        ln1_g, ln1_b, w_router, router_bias, w_exp_gate, w_exp_up, w_exp_down,
                                        w_sh_gate, w_sh_up, w_sh_down, ln2_g, ln2_b)
        y_p, y_s = y_p_new, y_s_new
    return (y_p, y_s, ckv_p, kr_p, ret_p, ckv_s, kr_s, ret_s)


_drawn_inputs = setup_inputs


def setup_inputs(seed=0):
    import zlib

    import numpy as np

    out = dict(_drawn_inputs(seed))
    spreads = {}
    factors = {'cache_ckv': 4.92,
     'cache_krope': 8.0,
     'q_norm_g': 8.0,
     'w_q_up': 3.607,
     'w_uk': 3.827,
     'w_uv': 3.15,
     'ret_gn_g': 30.43,
     'w_mla_o': 3.07,
     'ln2_g': 7.807,
     'ln2_b': 8.742}
    for name, (base, spread) in spreads.items():
        noise = np.random.default_rng([zlib.crc32(name.encode()), seed]).standard_normal(out[name].shape)
        drawn = base * np.exp(spread * noise) if base else spread * noise
        out[name] = __import__('jax').numpy.asarray(drawn.astype(out[name].dtype))
    for name, factor in factors.items():
        out[name] = (out[name] * factor).astype(out[name].dtype)
    return out
```

```python
from contextlib import ExitStack
import concourse.bass as bass
from concourse import mybir

ALU = mybir.AluOpType
ACT = mybir.ActivationFunctionType
F32 = mybir.dt.float32
I32 = mybir.dt.int32
U32 = mybir.dt.uint32
AX = mybir.AxisListType
P = 128
D = 1024
KD = D // P
NT = 9
TOK = NT * P
IN_W = 4512
CW = 376
NCHUNK = IN_W // CW


QL, KVL, ROPE, NOPE, VD, HEADS = 256, 128, 32, 64, 64, 8
HALF = ROPE // 2
S = 1024
DB, DQ = 8, 4
N_PHYS = 80
PAST = 1024
NE, TOPK = 64, 6
LIST = (NE + 1) * TOK
BLOCKS = (S + DB * DQ) * TOPK // P + NE
BK_STEPS = 34
ALPHA = 2.0 ** 0.25
ROUTED_SCALE = 2.5
RMS_EPS, LN_EPS = 1e-6, 1e-5
SCALE = (NOPE + ROPE) ** -0.5
QCH = ((0, 512), (512, 512), (1024, 128))


def groups(i):
    return [i] if i < 4 else [2 * i - 4, 2 * i - 3]


def gw(i, gi):
    done = 4 * (gi - groups(i)[0])
    return P * min(4, i + 1 - done)

def project(nc, xT, w_in, proj):
    with ExitStack() as ctx:
        sb = lambda n, s, d=F32: ctx.enter_context(nc.sbuf_tensor(n, s, d))
        sem = lambda n: ctx.enter_context(nc.semaphore(n))
        x_sb = sb("x_sb", [P, KD, TOK])
        w_sb = sb("w_sb", [P, 2, KD, CW])
        o_sb = sb("o_sb", [P, 2, NT, CW])
        ps = ctx.enter_context(nc.psum_tensor("ps", [P, 6, 512], F32))
        x_in = sem("x_in")
        w_in_sem = [sem(f"w_ready{c}") for c in range(2)]
        tile_done = sem("tile_done")
        free_by_dve = sem("free_by_dve")
        free_by_act = sem("free_by_act")
        dve_out = sem("dve_out")
        act_out = sem("act_out")
        stored = [sem(f"stored{c}") for c in range(2)]
        passed = sem("passed")
        block = ctx.enter_context(nc.Block())
        wv = w_in.rearrange("(k p) n -> p k n", p=P)
        pv = proj.rearrange("(t p) n -> p t n", p=P)

        @block.sync
        def _(sp):
            sp.dma_start(x_sb[:], xT.rearrange("(k p) t -> p k t", p=P)).then_inc(x_in, 16)
            for c in range(2):
                sp.dma_start(w_sb[:, c], wv[:, :, c * CW:(c + 1) * CW]).then_inc(w_in_sem[c], 16)
            with sp.Fori(0, NCHUNK // 2 - 1) as r:
                for c in range(2):
                    done, by_dve, by_act = sp.snap(r * 18 + 9 * c + 9), sp.snap(r * 9 + (5 if c == 0 else 9)), sp.snap(r * 9 + (4 if c == 0 else 9))
                    src_at, dst_at = sp.snap(r * (2 * CW) + (2 + c) * CW), sp.snap(r * (2 * CW) + c * CW)
                    sp.wait_ge(tile_done, done)
                    sp.sem_inc(passed, 1)
                    sp.dma_start(w_sb[:, c], wv[:, :, bass.ds(src_at, CW)]).then_inc(w_in_sem[c], 16)
                    sp.wait_ge(dve_out, by_dve)
                    sp.sem_inc(passed, 1)
                    sp.wait_ge(act_out, by_act)
                    sp.sem_inc(passed, 1)
                    sp.dma_start(pv[:, :, bass.ds(dst_at, CW)], o_sb[:, c]).then_inc(stored[c], 16)
            r = NCHUNK // 2 - 1
            for c in range(2):
                sp.wait_ge(dve_out, r * 9 + (5 if c == 0 else 9))
                sp.wait_ge(act_out, r * 9 + (4 if c == 0 else 9))
                sp.dma_start(pv[:, :, r * 2 * CW + c * CW:r * 2 * CW + (c + 1) * CW], o_sb[:, c]).then_inc(stored[c], 16)
            for c in range(2):
                sp.wait_ge(stored[c], 16 * (NCHUNK // 2))

        @block.tensor
        def _(pe):
            pe.wait_ge(x_in, 16)
            with pe.Fori(0, NCHUNK // 2) as r:
                for j in range(18):
                    c, t = j // 9, j % 9
                    if t == 0:
                        pe.wait_ge(w_in_sem[c], r * 16 + 16)
                    pe.wait_ge(free_by_dve if j % 2 == 0 else free_by_act, r * 9 + j // 2 + 1)
                    for k in range(KD):
                        mm = nc.tensor.matmul(ps[:, j % 6, 0:CW], x_sb[:, k, t * P:(t + 1) * P], w_sb[:, c, k, :], start=k == 0, stop=k == KD - 1)
                    mm.then_inc(tile_done, 1)

        def evac(eng, op, par, free, out):
            eng.sem_inc(free, 3)
            with eng.Fori(0, NCHUNK // 2) as r:
                for j in range(par, 18, 2):
                    c, t = j // 9, j % 9
                    if t < 2:
                        eng.wait_ge(stored[c], r * 16)
                    eng.wait_ge(tile_done, r * 18 + j + 1)
                    op(o_sb[:, c, t, :], ps[:, j % 6, 0:CW]).then_inc(out, 1)
                    eng.wait_ge(out, r * 9 + j // 2 + 1)
                    eng.sem_inc(free, 1)

        @block.vector
        def _(dve):
            evac(dve, nc.vector.tensor_copy, 0, free_by_dve, dve_out)

        @block.scalar
        def _(act):
            evac(act, nc.scalar.copy, 1, free_by_act, act_out)


def attention(nc, a, proj, o_mla, out_ckv_p, out_ckv_s, out_kr_p, out_kr_s):
    with ExitStack() as ctx:
        sb = lambda n, s, d=F32: ctx.enter_context(nc.sbuf_tensor(n, s, d))
        sem = lambda n: ctx.enter_context(nc.semaphore(n))
        ident = sb("ident", [P, P])
        cq = sb("cq", [P, NT, QL])
        sq = sb("sq", [P, NT, QL])
        ckv = sb("ckv", [P, NT, KVL])
        kr = sb("kr", [P, NT, ROPE])
        krp = sb("krp", [P, NT, NOPE + ROPE])
        t16 = sb("t16", [P, 4, NT, HALF])
        rot = sb("rot", [P, 2, NT, HALF])
        stat = sb("stat", [P, 4, NT])
        mhalf = sb("mhalf", [P, NT])
        kvg = sb("kvg", [P, KVL])
        qg = sb("qg", [P, 2])
        cqT = sb("cqT", [P, 2, TOK])
        ckvT = sb("ckvT", [P, TOK])
        qtab = sb("qtab", [P, TOK])
        wq_h = sb("wq_h", [P, 2, P])
        wuk_h = sb("wuk_h", [P, NOPE])
        wukT_h = sb("wukT_h", [NOPE, KVL])
        wuv = sb("wuv", [P, HEADS * VD])
        qT = sb("qT", [P, TOK])
        kT = sb("kT", [P, S])
        krsT = sb("krsT", [P, P])
        rt = sb("rt", [P, 2, 512])
        v_h = sb("v_h", [P, 8, VD])
        mask = sb("mask", [P, P])
        nmax = sb("nmax", [P, 8])
        sums = sb("sums", [P, 8])
        rinv = sb("rinv", [P, 8])
        prob = sb("prob", [P, 2, S])
        pT = sb("pT", [P, 4, 512])
        o_all = sb("o_all", [P, NT, HEADS * VD])
        qlat = sb("qlat", [P, DB, HEADS, DQ])
        qrs = sb("qrs", [P, DB, HEADS, DQ])
        pS = ctx.enter_context(nc.psum_tensor("pS", [P, 4, 512], F32))
        pT_ps = ctx.enter_context(nc.psum_tensor("pT_ps", [P, 2, 512], F32))
        pO = ctx.enter_context(nc.psum_tensor("pO", [P, 512], F32))

        page_kv = sb("page_kv", [P, 2, 8, KVL])
        page_kvT = sb("page_kvT", [P, 2, S])
        page_krT = sb("page_krT", [P, 2, S])
        new_kv = sb("new_kv", [DQ, 2, KVL])
        qlat_b = sb("qlat_b", [P, HEADS * DQ])
        qrs_b = sb("qrs_b", [P, HEADS * DQ])
        krs_b = sb("krs_b", [ROPE, DQ])
        smask = sb("smask", [HEADS * DQ, DQ])
        prob_s = sb("prob_s", [HEADS * DQ, S + DQ])
        st_s = sb("st_s", [HEADS * DQ, 4])
        pTs = sb("pTs", [P, 9 * HEADS * DQ])
        olat = sb("olat", [P, HEADS, DB, DQ])

        const_in = sem("const_in")
        lat_in = sem("lat_in")
        w_ready = sem("w_ready")
        dv = sem("dv")
        pl = sem("pl")
        lat_ready = sem("lat_ready")
        lat_T = sem("lat_T")
        lat_ev = sem("lat_ev")
        lat_out = sem("lat_out")
        pro_mm = sem("pro_mm")
        pro_act = sem("pro_act")
        pro_dve = sem("pro_dve")
        s_done = sem("s_done")
        max_done = sem("max_done")
        masked = sem("masked")
        exp_done = sem("exp_done")
        pt_done = sem("pt_done")
        pt_act = sem("pt_act")
        pt_dve = sem("pt_dve")
        o_done = sem("o_done")
        o_ev = sem("o_ev")
        rv = sem("rv")
        rv2 = sem("rv2")
        page_in = [sem(f"page_in{c}") for c in range(2)]
        q_b = sem("q_b")
        ss_done = sem("ss_done")
        smax = sem("smax")
        sexp = sem("sexp")
        snorm = sem("snorm")
        st_done = sem("st_done")
        st_ev = sem("st_ev")
        ol_done = sem("ol_done")
        ol_ev = sem("ol_ev")
        os_done = sem("os_done")
        os_ev = sem("os_ev")
        o_out = sem("o_out")
        passed = sem("passed")
        block = ctx.enter_context(nc.Block())
        pv = proj.rearrange("(t p) n -> p t n", p=P)
        HQ = HEADS * DQ
        CONSTS = 8

        @block.sync
        def _(sp):
            sp.dma_start(ckv[:], pv[:, :, QL:QL + KVL]).then_inc(lat_in, 16)
            sp.dma_start(cq[:], pv[:, :, 0:QL]).then_inc(lat_in, 16)
            sp.dma_start(kr[:], pv[:, :, QL + KVL:QL + KVL + ROPE]).then_inc(lat_in, 16)
            sp.dma_start(ident[:], a["ident"]).then_inc(const_in, 16)
            sp.dma_start(kvg[:], a["kv_norm_g"].partition_broadcast(P)).then_inc(const_in, 16)
            sp.dma_start(qg[:], a["q_norm_gT"]).then_inc(const_in, 16)
            sp.dma_start(rot[:], a["rope16"].rearrange("s (t p) c -> p s t c", p=P)).then_inc(const_in, 16)
            sp.dma_start(qtab[NOPE:P, :], a["rope_q"]).then_inc(const_in, 16)
            sp.dma_start(mask[:], a["causal"]).then_inc(const_in, 16)
            sp.dma_start(smask[:], a["causal_s"]).then_inc(const_in, 16)
            sp.dma_start(wuv[:], a["w_uv"]).then_inc(const_in, 16)

            def head_weights(h):
                if isinstance(h, int):
                    h = slice(h, h + 1)
                else:
                    h = bass.ds(h, 1)
                sp.dma_start(wq_h[:], a["w_q_ext"][h].rearrange("a (k p) n -> p (a k) n", p=P)).then_inc(w_ready, 16)
                sp.dma_start(wuk_h[:], a["w_uk_h"][h].rearrange("a p n -> p (a n)")).then_inc(w_ready, 16)
                sp.dma_start(wukT_h[:], a["w_ukT_h"][h].rearrange("a p n -> p (a n)")).then_inc(w_ready, 16)

            head_weights(0)
            sp.wait_ge(lat_ready, 2)
            sp.dma_start(out_ckv_p.rearrange("(t p) c -> p t c", p=P), ckv[:, 0:8, :]).then_inc(lat_out, 16)
            sp.dma_start(out_ckv_s, ckv[0:DB * DQ, 8, :]).then_inc(lat_out, 16)
            sp.wait_ge(lat_ready, 3)
            sp.dma_start(out_kr_p.rearrange("(t p) c -> p t c", p=P), krp[:, 0:8, NOPE:]).then_inc(lat_out, 16)
            sp.dma_start(out_kr_s, krp[0:DB * DQ, 8, NOPE:]).then_inc(lat_out, 16)
            with sp.Fori(0, HEADS - 1) as h:
                nxt, used_up = sp.snap(h + 1), sp.snap(h * 7 + 7)
                sp.wait_ge(pro_mm, used_up)
                sp.sem_inc(passed, 1)
                head_weights(nxt)
            sp.wait_ge(lat_out, 64)

            def pages(b, c, used=None):
                pgs = []
                for j in range(8):
                    pg = sp.value_load(a["page_table"][bass.ds(b, 1), j:j + 1] if not isinstance(b, int) else a["page_table"][b:b + 1, j:j + 1], min_val=0, max_val=N_PHYS - 1)
                    pgs.append(pg)
                src = out_ckv_s.rearrange("(b q) c -> b q c", q=DQ)
                src = src[b:b + 1] if isinstance(b, int) else src[bass.ds(b, 1)]
                if used is not None:
                    sp.wait_ge(ol_done, used)
                    sp.sem_inc(passed, 1)
                sp.dma_start(new_kv[:, c, :], src.rearrange("a q c -> q (a c)")).then_inc(page_in[c], 16)
                for j in range(8):
                    one = bass.ds(pgs[j], 1)
                    sp.dma_start(page_kv[:, c, j, :], a["cache_ckv"][one].rearrange("a p c -> p (a c)")).then_inc(page_in[c], 16)
                    sp.dma_start(page_kvT[:, c, j * P:(j + 1) * P], a["cache_ckvT"][one].rearrange("a p c -> p (a c)")).then_inc(page_in[c], 16)
                    sp.dma_start(page_krT[0:ROPE, c, j * P:(j + 1) * P], a["cache_kropeT"][one].rearrange("a p c -> p (a c)")).then_inc(page_in[c], 16)

            for c in range(2):
                pages(c, c)
            with sp.Fori(0, DB // 2 - 1) as r:
                for c in range(2):
                    used, nxt = sp.snap(r * 2 + (c + 1)), sp.snap(r * 2 + (c + 2))
                    pages(nxt, c, used)
            sp.wait_ge(os_ev, 1)
            sp.dma_start(o_mla.rearrange("(t p) c -> p t c", p=P), o_all[:]).then_inc(o_out, 16)
            sp.wait_ge(o_out, 16)

        @block.gpsimd
        def _(pool):
            pool.memset(mhalf[:], -0.5).then_inc(pl, 1)
            pool.memset(krp[:], 0.0).then_inc(pl, 1)
            pool.memset(o_all[:, 8, :], 0.0).then_inc(pl, 1)
            pool.wait_ge(pl, 1)
            for n in range(2):
                pool.wait_ge(dv, 3 * (n + 1))
                pool.tensor_tensor(stat[:, 2 + n, :], stat[:, n, :], mhalf[:], ALU.pow).then_inc(pl, 1)

        @block.vector
        def _(dve):
            v = nc.vector
            n = 0
            dve.wait_ge(lat_in, 48)
            dve.wait_ge(const_in, 16 * CONSTS)
            for i, (x, w) in enumerate(((cq, QL), (ckv, KVL))):
                v.tensor_tensor(sq[:, :, 0:w], x[:], x[:], ALU.mult).then_inc(dv, 1)
                dve.wait_ge(dv, 3 * i + 1)
                v.tensor_reduce(stat[:, i, :], sq[:, :, 0:w], AX.X, ALU.add).then_inc(dv, 1)
                dve.wait_ge(dv, 3 * i + 2)
                v.tensor_scalar(stat[:, i, :], stat[:, i, :], 1.0 / w, RMS_EPS, ALU.mult, ALU.add).then_inc(dv, 1)
                dve.wait_ge(dv, 3 * i + 3)
            dve.wait_ge(pl, 4)
            v.tensor_tensor(cq[:], cq[:], stat[:, 2, :].unsqueeze(2).broadcast_to([P, NT, QL]), ALU.mult).then_inc(lat_ready, 1)
            dve.wait_ge(pl, 5)
            v.tensor_tensor(ckv[:], ckv[:], stat[:, 3, :].unsqueeze(2).broadcast_to([P, NT, KVL]), ALU.mult).then_inc(dv, 1)
            dve.wait_ge(dv, 7)
            v.tensor_tensor(ckv[:], ckv[:], kvg[:].unsqueeze(1).broadcast_to([P, NT, KVL]), ALU.mult).then_inc(lat_ready, 1)
            cos, sin = rot[:, 0], rot[:, 1]
            x1, x2 = kr[:, :, 0:HALF], kr[:, :, HALF:ROPE]
            v.tensor_tensor(t16[:, 0], x1, cos, ALU.mult).then_inc(dv, 1)
            v.tensor_tensor(t16[:, 1], x2, sin, ALU.mult).then_inc(dv, 1)
            v.tensor_tensor(t16[:, 2], x2, cos, ALU.mult).then_inc(dv, 1)
            v.tensor_tensor(t16[:, 3], x1, sin, ALU.mult).then_inc(dv, 1)
            dve.wait_ge(dv, 11)
            v.tensor_tensor(krp[:, :, NOPE:NOPE + HALF], t16[:, 0], t16[:, 1], ALU.subtract).then_inc(dv, 1)
            v.tensor_tensor(krp[:, :, NOPE + HALF:], t16[:, 2], t16[:, 3], ALU.add).then_inc(dv, 1)
            dve.wait_ge(dv, 13)
            v.engine_nop().then_inc(lat_ready, 1)

            with dve.Fori(0, HEADS) as h:
                for g, (lo, w) in enumerate(QCH):
                    dve.wait_ge(pro_mm, h * 7 + g + 1)
                    v.tensor_tensor(rt[64:96, 0, 0:w], pS[64:96, g, 0:w], qtab[64:96, lo:lo + w], ALU.mult).then_inc(rv, 1)
                    v.tensor_tensor(rt[64:96, 1, 0:w], pS[96:128, g, 0:w], qtab[96:128, lo:lo + w], ALU.mult).then_inc(rv, 1)
                    dve.wait_ge(rv, h * 6 + 2 * g + 2)
                    v.tensor_tensor(qT[64:96, lo:lo + w], rt[64:96, 0, 0:w], rt[64:96, 1, 0:w], ALU.add).then_inc(pro_dve, 1)
                    dve.wait_ge(pro_dve, h * 5 + g + 1)
                dve.wait_ge(pro_mm, h * 7 + 6)
                v.tensor_copy(v_h[:], pS[:, 1, :]).then_inc(pro_dve, 1)
                v.tensor_copy(qrs[0:32, :, bass.ds(h, 1), :], qT[64:96, S:S + DB * DQ].rearrange("p (b a q) -> p b a q", b=DB, a=1)).then_inc(pro_dve, 1)
                def softmax_max(i):
                    s = pS[:, 2 * (i % 2):2 * (i % 2) + 2, :].rearrange("p a b -> p (a b)")
                    dve.wait_ge(s_done, h * 8 + i + 1)
                    v.tensor_tensor(s[:, i * P:(i + 1) * P], s[:, i * P:(i + 1) * P], mask[:], ALU.add).then_inc(masked, 1)
                    dve.wait_ge(masked, h * 8 + i + 1)
                    v.tensor_reduce(nmax[:, i:i + 1], s[:, 0:(i + 1) * P], AX.X, ALU.max, negate=True).then_inc(max_done, 1)

                def evac_odd(i):
                    for gi in groups(i):
                        if gi % 2:
                            dve.wait_ge(pt_done, h * 12 + gi + 1)
                            w = gw(i, gi)
                            v.tensor_copy(pT[:, gi % 4, 0:w], pT_ps[:, 1, 0:w]).then_inc(pt_dve, 1)
                softmax_max(0)
                softmax_max(1)
                for i in range(8):
                    evac_odd(i)
                    if i + 2 < 8:
                        softmax_max(i + 2)
                v.reciprocal(rinv[:], sums[:]).then_inc(rv2, 1)
                dve.wait_ge(rv2, h + 1)
                dve.wait_ge(o_done, h + 1)
                if True:
                    dve.wait_ge(pl, 3)
                v.tensor_tensor(o_all[:, 0:8, bass.ds(h * VD, VD)], pO[:].rearrange("p (t c) -> p t c", c=VD), rinv[:].unsqueeze(2).broadcast_to([P, 8, VD]), ALU.mult).then_inc(o_ev, 1)

            dve.wait_ge(pro_act, 6 * HEADS)
            with dve.Fori(0, DB) as b:
                v.tensor_copy(qlat_b[:], qlat[:, bass.ds(b, 1)].rearrange("p a h q -> p (a h q)")).then_inc(q_b, 1)
                v.tensor_copy(qrs_b[0:32, :], qrs[0:32, bass.ds(b, 1)].rearrange("p a h q -> p (a h q)")).then_inc(q_b, 1)
                v.tensor_copy(krs_b[:], krsT[0:32, bass.ds(b * DQ, DQ)]).then_inc(q_b, 1)
                s = pS[0:HQ].rearrange("p a b -> p (a b)")
                dve.wait_ge(ss_done, b + 1)
                v.tensor_tensor(s[:, S:S + DQ], s[:, S:S + DQ], smask[:], ALU.add).then_inc(smax, 1)
                dve.wait_ge(smax, b * 2 + 1)
                v.tensor_reduce(st_s[:, 0:1], s[:, 0:S + DQ], AX.X, ALU.max, negate=True).then_inc(smax, 1)
                dve.wait_ge(sexp, b + 1)
                v.reciprocal(st_s[:, 2:3], st_s[:, 1:2]).then_inc(snorm, 1)
                dve.wait_ge(snorm, b * 2 + 1)
                v.tensor_scalar(prob_s[:], prob_s[:], st_s[:, 2:3], None, ALU.mult).then_inc(snorm, 1)
                dve.wait_ge(st_done, b + 1)
                v.tensor_copy(pTs[:, 0:8 * HQ], pT_ps[:, 0, 0:8 * HQ]).then_inc(st_ev, 1)
                v.tensor_copy(pTs[0:DQ, 8 * HQ:], pT_ps[0:DQ, 0, 8 * HQ:9 * HQ]).then_inc(st_ev, 1)
                dve.wait_ge(ol_done, b + 1)
                v.tensor_copy(olat[:, :, bass.ds(b, 1), :], pO[:, 0:HQ].rearrange("p (h a q) -> p h a q", h=HEADS, a=1)).then_inc(ol_ev, 1)
            dve.wait_ge(os_done, 1)
            v.tensor_copy(o_all[0:DB * DQ, 8, :], pS[0:DB * DQ, 0, :]).then_inc(os_ev, 1)

        @block.scalar
        def _(act):
            s_ = nc.scalar
            act.wait_ge(const_in, 16 * CONSTS)
            for g in range(12):
                arr, part = g // 3, g % 3
                w = 512 if part < 2 else P
                lo = part * 512
                act.wait_ge(lat_T, g + 1)
                src = pS[:, g % 4, 0:w]
                if arr < 2:
                    s_.activation(cqT[:, arr, lo:lo + w], src, ACT.Copy, scale=qg[:, arr:arr + 1]).then_inc(lat_ev, 1)
                elif arr == 2:
                    s_.copy(ckvT[:, lo:lo + w], src).then_inc(lat_ev, 1)
                elif part < 2:
                    s_.copy(kT[64:96, lo:lo + w], pS[64:96, g % 4, 0:w]).then_inc(lat_ev, 1)
                else:
                    s_.copy(krsT[0:32, :], pS[64:96, g % 4, 0:w]).then_inc(lat_ev, 1)

            with act.Fori(0, HEADS) as h:
                for g, (lo, w) in enumerate(QCH):
                    act.wait_ge(pro_mm, h * 7 + g + 1)
                    s_.activation(qT[0:64, lo:lo + w], pS[0:64, g, 0:w], ACT.Copy, scale=SCALE).then_inc(pro_act, 1)
                for g in range(2):
                    act.wait_ge(pro_mm, h * 7 + 4 + g)
                    s_.copy(kT[0:64, g * 512:(g + 1) * 512], pS[0:64, (3 + g) % 4, :]).then_inc(pro_act, 1)
                act.wait_ge(pro_mm, h * 7 + 7)
                s_.copy(qlat[:, :, bass.ds(h, 1), :], pS[:, 2, 0:DB * DQ].rearrange("p (b a q) -> p b a q", b=DB, a=1)).then_inc(pro_act, 1)

                def expo(i):
                    act.wait_ge(max_done, h * 8 + i + 1)
                    s = pS[:, 2 * (i % 2):2 * (i % 2) + 2, :].rearrange("p a b -> p (a b)")
                    s_.activation(prob[:, i % 2, 0:(i + 1) * P], s[:, 0:(i + 1) * P], ACT.Exp, bias=nmax[:, i:i + 1], accum_out=sums[:, i:i + 1]).then_inc(exp_done, 1)

                def evac_even(i):
                    for gi in groups(i):
                        if gi % 2 == 0:
                            act.wait_ge(pt_done, h * 12 + gi + 1)
                            w = gw(i, gi)
                            s_.copy(pT[:, gi % 4, 0:w], pT_ps[:, 0, 0:w]).then_inc(pt_act, 1)
                expo(0)
                for i in range(8):
                    if i + 1 < 8:
                        if i >= 1:
                            act.wait_ge(pt_done, h * 12 + groups(i - 1)[-1] + 1)
                        expo(i + 1)
                    evac_even(i)

            with act.Fori(0, DB) as b:
                act.wait_ge(smax, b * 2 + 2)
                s_.activation(prob_s[:], pS[0:HQ].rearrange("p a b -> p (a b)")[:, 0:S + DQ], ACT.Exp, bias=st_s[:, 0:1], accum_out=st_s[:, 1:2]).then_inc(sexp, 1)

        @block.tensor
        def _(pe):
            t_ = nc.tensor
            pe.wait_ge(const_in, 16 * CONSTS)
            for g in range(12):
                arr, part = g // 3, g % 3
                if part == 0:
                    pe.wait_ge(lat_ready, (1, 1, 2, 3)[arr])
                if g >= 4:
                    pe.wait_ge(lat_ev, g - 3)
                for t in range(4 * part, min(4 * part + 4, NT)):
                    lo = (t - 4 * part) * P
                    src = cq[:, t, arr * P:(arr + 1) * P] if arr < 2 else ckv[:, t, :] if arr == 2 else krp[:, t, :]
                    rows = P if arr < 3 else 96
                    mm = t_.transpose(pS[0:rows, g % 4, lo:lo + P], src, ident[:])
                mm.then_inc(lat_T, 1)
            pe.wait_ge(lat_ev, 12)

            with pe.Fori(0, HEADS) as h:
                pe.wait_ge(w_ready, h * 48 + 48)
                pe.wait_ge(exp_done, h * 8)
                for g, (lo, w) in enumerate(QCH):
                    for k in range(2):
                        mm = t_.matmul(pS[:, g, 0:w], wq_h[:, k, :], cqT[:, k, lo:lo + w], start=k == 0, stop=k == 1)
                    mm.then_inc(pro_mm, 1)
                t_.matmul(pS[0:64, 3, :], wuk_h[:], ckvT[:, 0:512], start=True, stop=True).then_inc(pro_mm, 1)
                pe.wait_ge(pro_act, h * 6 + 1)
                pe.wait_ge(pro_dve, h * 5 + 1)
                t_.matmul(pS[0:64, 0, :], wuk_h[:], ckvT[:, 512:1024], start=True, stop=True).then_inc(pro_mm, 1)
                pe.wait_ge(pro_act, h * 6 + 2)
                pe.wait_ge(pro_dve, h * 5 + 2)
                for t in range(8):
                    mm = t_.matmul(pS[:, 1, t * VD:(t + 1) * VD], ckvT[:, t * P:(t + 1) * P], wuv[:, bass.ds(h * VD, VD)], start=True, stop=True)
                mm.then_inc(pro_mm, 1)
                pe.wait_ge(pro_act, h * 6 + 3)
                pe.wait_ge(pro_dve, h * 5 + 3)
                t_.matmul(pS[:, 2, 0:DB * DQ], wukT_h[:], qT[0:64, S:S + DB * DQ], start=True, stop=True).then_inc(pro_mm, 1)
                pe.wait_ge(pro_act, h * 6 + 6)
                pe.wait_ge(pro_dve, h * 5 + 5)

                def scores(i):
                    if i >= 2:
                        pe.wait_ge(exp_done, h * 8 + i - 1)
                    kw = (i + 1) * P
                    for c in range(0, kw, 512):
                        w = min(512, kw - c)
                        mm = t_.matmul(pS[:, 2 * (i % 2) + c // 512, 0:w], qT[0:96, i * P:(i + 1) * P], kT[0:96, c:c + w], start=True, stop=True)
                    mm.then_inc(s_done, 1)

                def turn(i):
                    pe.wait_ge(exp_done, h * 8 + i + 1)
                    for gi in groups(i):
                        pe.wait_ge(pt_dve if gi % 2 else pt_act, h * 6 + gi // 2)
                        b0 = 4 * (gi - groups(i)[0])
                        for b in range(gw(i, gi) // P):
                            mm = t_.transpose(pT_ps[:, gi % 2, b * P:(b + 1) * P], prob[:, i % 2, (b0 + b) * P:(b0 + b + 1) * P], ident[:])
                        mm.then_inc(pt_done, 1)

                def values(i):
                    if i == 0:
                        pe.wait_ge(o_ev, h)
                    for gi in groups(i):
                        pe.wait_ge(pt_dve if gi % 2 else pt_act, h * 6 + gi // 2 + 1)
                        b0 = 4 * (gi - groups(i)[0])
                        for b in range(gw(i, gi) // P):
                            mm = t_.matmul(pO[:, i * VD:(i + 1) * VD], pT[:, gi % 4, b * P:(b + 1) * P], v_h[:, b0 + b, :], start=b0 + b == 0, stop=b0 + b == i)
                    if i == 7:
                        mm.then_inc(o_done, 1)
                scores(0)
                scores(1)
                for i in range(8):
                    turn(i)
                    if i + 2 < 8:
                        scores(i + 2)
                    values(i)

            pe.wait_ge(exp_done, 64)
            pe.wait_ge(o_ev, 8)
            with pe.Fori(0, DB // 2) as r:
                for c in range(2):
                    b = r * 2 + c
                    s = pS[0:HQ]
                    pe.wait_ge(q_b, b * 3 + 3)
                    pe.wait_ge(sexp, b)
                    pe.wait_ge(page_in[c], r * 400 + 400)
                    for k in range(2):
                        t_.matmul(s[:, k, :], qlat_b[:], page_kvT[:, c, k * 512:(k + 1) * 512], start=True, stop=False)
                        t_.matmul(s[:, k, :], qrs_b[0:32, :], page_krT[0:32, c, k * 512:(k + 1) * 512], start=False, stop=True)
                    t_.matmul(s[:, 2, 0:DQ], qlat_b[:], ckvT[:, bass.ds(b * DQ + S, DQ)], start=True, stop=False)
                    t_.matmul(s[:, 2, 0:DQ], qrs_b[0:32, :], krs_b[0:32, :], start=False, stop=True).then_inc(ss_done, 1)
                    pe.wait_ge(snorm, b * 2 + 2)
                    pe.sem_inc(passed, 1)
                    for j in range(8):
                        t_.transpose(pT_ps[:, 0, j * HQ:(j + 1) * HQ], prob_s[:, j * P:(j + 1) * P], ident[0:HQ, 0:HQ])
                    t_.transpose(pT_ps[0:DQ, 0, 8 * HQ:9 * HQ], prob_s[:, S:S + DQ], ident[0:HQ, 0:HQ]).then_inc(st_done, 1)
                    pe.wait_ge(st_ev, b * 2 + 2)
                    pe.wait_ge(ol_ev, b)
                    for j in range(8):
                        t_.matmul(pO[:, 0:HQ], page_kv[:, c, j, :], pTs[:, j * HQ:(j + 1) * HQ], start=j == 0, stop=False)
                    mm = t_.matmul(pO[:, 0:HQ], new_kv[:, c, :], pTs[0:DQ, 8 * HQ:9 * HQ], start=False, stop=True)
                    mm.then_inc(ol_done, 1)
                    
            pe.wait_ge(ol_ev, DB)
            pe.wait_ge(sexp, DB)
            for h in range(HEADS):
                mm = t_.matmul(pS[0:DB * DQ, 0, h * VD:(h + 1) * VD], olat[:, h].rearrange("p b q -> p (b q)"), wuv[:, h * VD:(h + 1) * VD], start=True, stop=True)
            mm.then_inc(os_done, 1)


def retention(nc, a, proj, retn, out_ret_p, out_ret_s):
    with ExitStack() as ctx:
        sb = lambda n, s, d=F32: ctx.enter_context(nc.sbuf_tensor("r_" + n, s, d))
        sem = lambda n: ctx.enter_context(nc.semaphore("r_" + n))
        NS = DB * DQ
        ident = sb("ident", [P, P])
        raw_q = sb("raw_q", [P, NT, 512])
        raw_k = sb("raw_k", [P, NT, 512])
        raw_v = sb("raw_v", [P, NT, 512])
        rot = sb("rot", [P, 4, NT, 64])
        dmask = sb("dmask", [P, P])
        dmask_s = sb("dmask_s", [NS, NS])
        qdec = sb("qdec", [P, TOK])
        cols = sb("cols", [P, 11])
        st_in = sb("st_in", [P, DB, P])
        st_out = sb("st_out", [P, DB, P])
        tq = sb("tq", [P, 2, NT, 64])
        tk = sb("tk", [P, 2, NT, 64])
        qr = sb("qr", [P, NT, P])
        kr = sb("kr", [P, NT, P])
        kd = sb("kd", [P, 8, P])
        kds = sb("kds", [NS, DB, P])
        v_s = sb("v_s", [NS, P])
        qT = sb("qT", [P, TOK])
        kT = sb("kT", [P, TOK])
        qd = sb("qd", [P, TOK])
        attT = sb("attT", [P, 8, P])
        attT_s = sb("attT_s", [NS, NS])
        state = sb("state", [P, 9, P])
        oT_s = sb("oT_s", [P, NS])
        bst = sb("bst", [P, NT, 6])
        mv = sb("mv", [P, NT, 2])
        vare = sb("vare", [P, NT])
        mhalf = sb("mhalf", [P, NT])
        rstd = sb("rstd", [P, NT])
        nbias = sb("nbias", [P, NT])
        on = sb("on", [P, NT, P])
        ps = [ctx.enter_context(nc.psum_tensor(f"r_ps{i}", [P, 512], F32)) for i in range(8)]
        const_in, raw_in, head_in, pl, dv, q_rot, k_rot, k_dec, turned, ev, qd_ok, att_mm, att_ok, kv_mm, kv_ok, o_mm, \
            os_mm, os_ev, os_T, var_ok, rstd_ok, nb_ok, norm_ok, out_s, state_out = [sem(n) for n in (
                "const_in raw_in head_in pl dv q_rot k_rot k_dec turned ev qd_ok att_mm att_ok kv_mm kv_ok o_mm "
                "os_mm os_ev os_T var_ok rstd_ok nb_ok norm_ok out_s state_out").split()]
        passed = sem("passed")
        block = ctx.enter_context(nc.Block())
        pv = proj.rearrange("(t p) n -> p t n", p=P)
        rn = retn.rearrange("(t p) n -> p t n", p=P)
        R0 = QL + KVL + ROPE

        @block.sync
        def _(sp):
            for i, x in enumerate((raw_q, raw_k, raw_v)):
                sp.dma_start(x[:], pv[:, :, R0 + 512 * i:R0 + 512 * (i + 1)]).then_inc(raw_in, 16)
            sp.dma_start(rot[:], a["rope64"].rearrange("s (t p) c -> p s t c", p=P)).then_inc(const_in, 16)
            sp.dma_start(ident[:], a["ident"]).then_inc(const_in, 16)

            def head_consts(h):
                one = slice(h, h + 1) if isinstance(h, int) else bass.ds(h, 1)
                sp.dma_start(dmask[:], a["dmask"][one].rearrange("a p n -> p (a n)")).then_inc(head_in, 16)
                sp.dma_start(dmask_s[:], a["dmask_s"][one].rearrange("a p n -> p (a n)")).then_inc(head_in, 16)
                sp.dma_start(qdec[:], a["qdec"][one].rearrange("a p n -> p (a n)")).then_inc(head_in, 16)
                sp.dma_start(cols[:], a["ret_cols"][one].rearrange("a p n -> p (a n)")).then_inc(head_in, 16)
                sp.dma_start(st_in[:], a["state_ret"][:, one].rearrange("b a d v -> d b (a v)")).then_inc(head_in, 16)

            head_consts(0)

            def stores(h, kv_n, norm_n, hc):
                sp.wait_ge(kv_ok, kv_n)
                sp.sem_inc(passed, 1)
                sp.dma_start(out_ret_p[bass.ds(h, 1)].rearrange("a d v -> d (a v)"), state[:, 8, :]).then_inc(state_out, 16)
                sp.dma_start(out_ret_s[:, bass.ds(h, 1)].rearrange("b a d v -> d b (a v)"), st_out[:]).then_inc(state_out, 16)
                sp.wait_ge(norm_ok, norm_n)
                sp.sem_inc(passed, 1)
                sp.dma_start(rn[:, :, bass.ds(hc, P)], on[:]).then_inc(out_s, 16)
            with sp.Fori(0, 3) as h:
                nxt, n9, hc = sp.snap(h + 1), sp.snap(h * 9 + 9), sp.snap(h * P)
                stores(h, n9, n9, hc)
                head_consts(nxt)
            stores(3, 36, 36, 3 * P)
            sp.wait_ge(state_out, 128)
            sp.wait_ge(out_s, 64)

        @block.gpsimd
        def _(pool):
            pool.memset(mhalf[:], -0.5).then_inc(pl, 1)
            pool.memset(on[:, 8, :], 0.0).then_inc(pl, 1)
            pool.memset(mv[:], 1.0).then_inc(pl, 1)
            pool.wait_ge(const_in, 32)
            pool.wait_ge(raw_in, 48)
            pool.wait_ge(pl, 3)
            cos, sin = rot[:, 2], rot[:, 3]
            with pool.Fori(0, 4) as h:
                x1, x2 = raw_k[:, :, bass.ds(h * P, 64)], raw_k[:, :, bass.ds(h * P + 64, 64)]
                g = nc.gpsimd
                pool.wait_ge(head_in, h * 80 + 80)
                pool.sem_inc(passed, 1)
                g.tensor_tensor(tk[:, 0], x1, cos, ALU.mult).then_inc(k_rot, 1)
                g.tensor_tensor(tk[:, 1], x2, sin, ALU.mult).then_inc(k_rot, 1)
                pool.wait_ge(k_rot, h * 6 + 2)
                g.tensor_tensor(kr[:, :, 0:64], tk[:, 0], tk[:, 1], ALU.subtract).then_inc(k_rot, 1)
                pool.wait_ge(k_rot, h * 6 + 3)
                pool.sem_inc(passed, 1)
                g.tensor_tensor(tk[:, 0], x2, cos, ALU.mult).then_inc(k_rot, 1)
                g.tensor_tensor(tk[:, 1], x1, sin, ALU.mult).then_inc(k_rot, 1)
                pool.wait_ge(k_rot, h * 6 + 5)
                g.tensor_tensor(kr[:, :, 64:P], tk[:, 0], tk[:, 1], ALU.add).then_inc(k_rot, 1)
                pool.wait_ge(k_rot, h * 6 + 6)
                pool.sem_inc(passed, 1)
                g.tensor_scalar(kd[:], kr[:, 0:8, :], cols[:, 0:1], None, ALU.mult).then_inc(k_dec, 1)
                for b in range(DB):
                    g.tensor_scalar(kds[:, b, :], kr[0:NS, 8, :], cols[0:NS, 1 + b:2 + b], None, ALU.mult).then_inc(k_dec, 1)
                g.tensor_copy(v_s[:], raw_v[0:NS, 8, bass.ds(h * P, P)]).then_inc(k_dec, 1)
                pool.wait_ge(var_ok, h + 1)
                g.tensor_tensor(rstd[:], vare[:], mhalf[:], ALU.pow).then_inc(rstd_ok, 1)

        @block.vector
        def _(dve):
            v = nc.vector
            dve.wait_ge(const_in, 32)
            dve.wait_ge(raw_in, 48)
            dve.wait_ge(pl, 3)
            cos, sin = rot[:, 0], rot[:, 1]
            with dve.Fori(0, 4) as h:
                x1, x2 = raw_q[:, :, bass.ds(h * P, 64)], raw_q[:, :, bass.ds(h * P + 64, 64)]
                v.tensor_tensor(tq[:, 0], x1, cos, ALU.mult).then_inc(q_rot, 1)
                v.tensor_tensor(tq[:, 1], x2, sin, ALU.mult).then_inc(q_rot, 1)
                dve.wait_ge(q_rot, h * 6 + 2)
                v.tensor_tensor(qr[:, :, 0:64], tq[:, 0], tq[:, 1], ALU.subtract).then_inc(q_rot, 1)
                dve.wait_ge(q_rot, h * 6 + 3)
                v.tensor_tensor(tq[:, 0], x2, cos, ALU.mult).then_inc(q_rot, 1)
                v.tensor_tensor(tq[:, 1], x1, sin, ALU.mult).then_inc(q_rot, 1)
                dve.wait_ge(q_rot, h * 6 + 5)
                v.tensor_tensor(qr[:, :, 64:P], tq[:, 0], tq[:, 1], ALU.add).then_inc(q_rot, 1)
                dve.wait_ge(head_in, h * 80 + 80)
                dve.wait_ge(ev, h * 6 + 3)
                v.tensor_tensor(qd[:], qT[:], qdec[:], ALU.mult).then_inc(qd_ok, 1)
                for g in range(2):
                    dve.wait_ge(att_mm, h * 3 + g + 1)
                    v.tensor_tensor(attT[:, 4 * g:4 * g + 4, :], ps[3 + g][:].rearrange("p (c n) -> p c n", n=P), dmask[:].unsqueeze(1).broadcast_to([P, 4, P]), ALU.mult).then_inc(att_ok, 1)
                dve.wait_ge(att_mm, h * 3 + 3)
                v.tensor_tensor(attT_s[:], ps[5][0:NS, 0:NS], dmask_s[:], ALU.mult).then_inc(att_ok, 1)
                dve.wait_ge(state_out, h * 32)
                for n in range(8):
                    if n % 4 == 0:
                        dve.wait_ge(kv_mm, h * 4 + n // 4 + 1)
                    kv = ps[6 + n // 4][:, (n % 4) * P:(n % 4 + 1) * P]
                    if n == 0:
                        v.tensor_copy(state[:, 1, :], kv).then_inc(kv_ok, 1)
                    else:
                        dve.wait_ge(kv_ok, h * 9 + n)
                        v.scalar_tensor_tensor(state[:, n + 1, :], state[:, n, :], cols[:, 9:10], kv, ALU.mult, ALU.add).then_inc(kv_ok, 1)
                for g in range(2):
                    dve.wait_ge(kv_mm, h * 4 + 3 + g)
                    ins = v.scalar_tensor_tensor(st_out[:, 4 * g:4 * g + 4, :].rearrange("p b n -> p (b n)"), st_in[:, 4 * g:4 * g + 4, :].rearrange("p b n -> p (b n)"), cols[:, 10:11], ps[g][:], ALU.mult, ALU.add)
                ins.then_inc(kv_ok, 1)
                dve.wait_ge(os_mm, h + 1)
                v.tensor_copy(oT_s[:], ps[5][:, 64:64 + NS]).then_inc(os_ev, 1)
                for n in range(NT):
                    if n < 8:
                        if n % 4 == 0:
                            dve.wait_ge(o_mm, h * 2 + n // 4 + 1)
                        v.bn_stats(bst[:, n, :], ps[3 + n // 4][:, (n % 4) * P:(n % 4 + 1) * P]).then_inc(dv, 1)
                    else:
                        dve.wait_ge(os_T, h + 1)
                        v.bn_stats(bst[0:NS, n, :], ps[2][0:NS, 0:P]).then_inc(dv, 1)
                for n in range(NT):
                    rows = P if n < 8 else NS
                    dve.wait_ge(dv, h * 18 + n + 1)
                    dve.sem_inc(passed, 1)
                    v.bn_aggr(mv[0:rows, n, :], bst[0:rows, n, :]).then_inc(dv, 1)
                dve.wait_ge(dv, h * 18 + 18)
                v.tensor_scalar(vare[:], mv[:, :, 1], LN_EPS, None, ALU.add).then_inc(var_ok, 1)
                dve.wait_ge(rstd_ok, h + 1)
                v.scalar_tensor_tensor(nbias[:], mv[:, :, 0], -1.0, rstd[:], ALU.mult, ALU.mult).then_inc(nb_ok, 1)

        @block.scalar
        def _(act):
            s_ = nc.scalar
            with act.Fori(0, 4) as h:
                for g in range(6):
                    dst, part = (qT, kT)[g // 3], g % 3
                    w = 512 if part < 2 else P
                    act.wait_ge(turned, h * 6 + g + 1)
                    s_.copy(dst[:, part * 512:part * 512 + w], ps[g % 3][:, 0:w]).then_inc(ev, 1)
                act.wait_ge(nb_ok, h + 1)
                act.wait_ge(out_s, h * 16)
                for n in range(NT):
                    rows = P if n < 8 else NS
                    src = ps[3 + n // 4][:, (n % 4) * P:(n % 4 + 1) * P] if n < 8 else ps[2][0:NS, 0:P]
                    s_.activation(on[0:rows, n, :], src, ACT.Identity, bias=nbias[0:rows, n:n + 1], scale=rstd[0:rows, n:n + 1]).then_inc(norm_ok, 1)

        @block.tensor
        def _(pe):
            t_ = nc.tensor
            pe.wait_ge(const_in, 32)
            with pe.Fori(0, 4) as h:
                for g in range(6):
                    src, part = (qr, kr)[g // 3], g % 3
                    if g == 0:
                        pe.wait_ge(q_rot, h * 6 + 6)
                        pe.wait_ge(norm_ok, h * 9)
                    if g == 3:
                        pe.wait_ge(k_rot, h * 6 + 6)
                    if g >= 3:
                        pe.wait_ge(ev, h * 6 + g - 2)
                    for t in range(4 * part, min(4 * part + 4, NT)):
                        mm = t_.transpose(ps[g % 3][:, (t - 4 * part) * P:(t - 4 * part + 1) * P], src[:, t, :], ident[:])
                    mm.then_inc(turned, 1)
                pe.wait_ge(k_dec, h * 10 + 10)
                for g in range(2):
                    for c in range(4):
                        n = 4 * g + c
                        mm = t_.matmul(ps[6 + g][:, c * P:(c + 1) * P], kd[:, n, :], raw_v[:, n, bass.ds(h * P, P)], start=True, stop=True)
                    mm.then_inc(kv_mm, 1)
                pe.wait_ge(ev, h * 6 + 6)
                for g in range(2):
                    for c in range(4):
                        at = slice((4 * g + c) * P, (4 * g + c + 1) * P)
                        mm = t_.matmul(ps[3 + g][:, c * P:(c + 1) * P], kT[:, at], qT[:, at], start=True, stop=True)
                    mm.then_inc(att_mm, 1)
                t_.matmul(ps[5][0:NS, 0:NS], kT[:, S:S + NS], qT[:, S:S + NS], start=True, stop=True).then_inc(att_mm, 1)
                for g in range(2):
                    for c in range(4):
                        mm = t_.matmul(ps[g][:, c * P:(c + 1) * P], kds[:, 4 * g + c, :], raw_v[0:NS, 8, bass.ds(h * P, P)], start=True, stop=True)
                    mm.then_inc(kv_mm, 1)
                pe.wait_ge(att_ok, h * 3 + 3)
                pe.wait_ge(qd_ok, h + 1)
                for b in range(DB):
                    out = ps[5][:, 64 + DQ * b:64 + DQ * (b + 1)]
                    t_.matmul(out, st_in[:, b, :], qd[:, S + DQ * b:S + DQ * (b + 1)], start=True, stop=False)
                    mm = t_.matmul(out, v_s[:], attT_s[:, DQ * b:DQ * (b + 1)], start=False, stop=True)
                mm.then_inc(os_mm, 1)
                for n in range(8):
                    if n:
                        pe.wait_ge(kv_ok, h * 9 + n)
                    out = ps[3 + n // 4][:, (n % 4) * P:(n % 4 + 1) * P]
                    mm = t_.matmul(out, attT[:, n, :], raw_v[:, n, bass.ds(h * P, P)], start=True, stop=n == 0)
                    if n:
                        mm = t_.matmul(out, qd[:, n * P:(n + 1) * P], state[:, n, :], start=False, stop=True)
                    if n % 4 == 3:
                        mm.then_inc(o_mm, 1)
                pe.wait_ge(os_ev, h + 1)
                pe.sem_inc(passed, 1)
                t_.transpose(ps[2][0:NS, 0:P], oT_s[:], ident[:]).then_inc(os_T, 1)


def merge(nc, a, proj, o_mla, retn, h_perm, base, tok_list, meta):
    with ExitStack() as ctx:
        sb = lambda n, s, d=F32: ctx.enter_context(nc.sbuf_tensor("m_" + n, s, d))
        sem = lambda n: ctx.enter_context(nc.semaphore("m_" + n))
        ident = sb("ident", [P, P])
        w_mo = sb("w_mo", [P, 4, D])
        w_ro = sb("w_ro", [P, 4, D])
        w_o = sb("w_o", [P, KD, D])
        w_gu = sb("w_gu", [P, KD, 512])
        w_sd = sb("w_sd", [P, 2, D])
        w_r = sb("w_r", [P, KD, NE])
        gn_g = sb("gn_g", [P, 512])
        g1 = sb("g1", [P, D])
        b1 = sb("b1", [P, D])
        gates = sb("gates", [P, 2560])
        o_in = sb("o_in", [P, 512])
        ret = sb("ret", [P, 512])
        srg = sb("srg", [P, 512])
        x_in = sb("x_in", [P, D])
        sg = sb("sg", [P, 2048])
        oT = sb("oT", [P, KD, P])
        mix = sb("mix", [P, D])
        tmp = sb("tmp", [P, D])
        mT = sb("mT", [P, KD, P])
        z = sb("z", [P, D])
        hp = sb("hp", [P, D])
        hT = sb("hT", [P, KD, P])
        sgg = sb("sgg", [P, 256])
        act_s = sb("act_s", [P, 256])
        aT = sb("aT", [P, 2, P])
        base_sb = sb("base_sb", [P, D])
        bst = sb("bst", [P, 2, 6])
        mv = sb("mv", [P, 2])
        col = sb("col", [P, 4])
        bias = sb("bias", [P, NE])
        tri = sb("tri", [P, P])
        ones = sb("ones", [P, P])
        iota = sb("iota", [P, NE + 1])
        ebase = sb("ebase", [P, NE])
        pid = sb("pid", [P, 1])
        valid = sb("valid", [P, NT])
        dump = sb("dump", [P, NT, TOPK])
        tid = sb("tid", [P, NT], U32)
        sc = sb("sc", [P, NE])
        sel = sb("sel", [P, NE])
        top2 = sb("top2", [P, 8, 8])
        gs = sb("gs", [P, 8])
        m8 = sb("m8", [P, 8])
        i8 = sb("i8", [P, 8], U32)
        f8 = sb("f8", [P, 8])
        gm = sb("gm", [P, 8])
        oh = sb("oh", [P, TOPK, NE])
        prod = sb("prod", [P, TOPK, NE])
        cnt = sb("cnt", [P, NE])
        carry = sb("carry", [P, NE])
        rank = sb("rank", [P, NE])
        w6 = sb("w6", [P, TOPK])
        wsum = sb("wsum", [P, 2])
        slot = sb("slot", [P, TOPK])
        slot_c = sb("slot_c", [P, TOPK], U32)
        entry = sb("entry", [P, TOPK, 2], U32)
        nb_i = sb("nb_i", [P, NE], I32)
        pre = sb("pre", [P, 2, NE + 1])
        eqk = sb("eqk", [P, NE])
        bt = sb("bt", [P, 8])
        meta_i = sb("meta_i", [P, 2], I32)
        nblk_i = sb("nblk_i", [P, 1], I32)

        T = [ctx.enter_context(nc.psum_tensor(f"m_T{i}", [P, 512], F32)) for i in range(2)]
        Y = ctx.enter_context(nc.psum_tensor("m_Y", [P, 4, 512], F32))
        GU = ctx.enter_context(nc.psum_tensor("m_GU", [P, 512], F32))
        R = ctx.enter_context(nc.psum_tensor("m_R", [P, 512], F32))
        (w_in_s, c_in, gates_in, o_in_s, ret_in, x_in_s, pl, sig_ok, ret_ok, turned, tev, y_done, m_ok, w_done, z_ok,
         st, var_ok, rstd_ok, zn_ok, hg, h_ok, h_out, gu_done, sgg_ok, a1_ok, act_ok, r_done, sc_ok, cnt_ok, p_done,
         rank_ok, d_done, base_ok, base_out, slot_ok, listed, rt, t12, t12b, filled, bk, meta_out, passed) = [sem(n) for n in (
            "w_in_s c_in gates_in o_in_s ret_in x_in_s pl sig_ok ret_ok turned tev y_done m_ok w_done z_ok "
            "st var_ok rstd_ok zn_ok hg h_ok h_out gu_done sgg_ok a1_ok act_ok r_done sc_ok cnt_ok p_done "
            "rank_ok d_done base_ok base_out slot_ok listed rt t12 t12b filled bk meta_out passed").split()]
        block = ctx.enter_context(nc.Block())
        G0 = QL + KVL + ROPE + 3 * 512
        NCONST = 13

        def rows(t, dram):
            return dram[t * P:(t + 1) * P, :] if isinstance(t, int) else dram[bass.ds(t * P, P), :]

        def wait_alone(eng, s, value):
            eng.wait_ge(s, value)
            eng.sem_inc(passed, 1)

        @block.sync
        def _(sp):
            def loads(t):
                n = [t, t, t, t] if isinstance(t, int) else [sp.snap(t) for _ in range(4)]
                r0 = t * P if isinstance(t, int) else sp.snap(t * P)
                t3 = t * 3 if isinstance(t, int) else sp.snap(t * 3)
                turned_by = t * 2 - 1 if isinstance(t, int) else sp.snap(t * 2 - 1)
                later = not isinstance(t, int) or t > 0
                at = bass.ds(r0, P)
                if later:
                    wait_alone(sp, sig_ok, n[0])
                    wait_alone(sp, ret_ok, t3)
                sp.dma_start(gates[:], proj[at, G0:G0 + 2560]).then_inc(gates_in, 16)
                if later:
                    wait_alone(sp, y_done, turned_by)
                sp.dma_start(o_in[:], o_mla[at, :]).then_inc(o_in_s, 16)
                sp.dma_start(ret[:], retn[at, :]).then_inc(ret_in, 16)
                if later:
                    wait_alone(sp, z_ok, n[0])
                sp.dma_start(x_in[:], a["x"][at, :]).then_inc(x_in_s, 16)

            for dst, src in ((ident[:], a["ident"]), (gn_g[:], a["ret_gn_g"].partition_broadcast(P)), (g1[:], a["ln1_g"].partition_broadcast(P)),
                             (b1[:], a["ln1_b"].partition_broadcast(P)), (bias[:], a["router_bias"].partition_broadcast(P)),
                             (tri[:], a["tri"]), (iota[:], a["iota"]), (ebase[:], a["ebase"]), (pid[:], a["pid"]),
                             (valid[:], a["valid"]), (dump[:], a["dump"]), (tid[:], a["tid"]), (ones[:], a["ones"])):
                sp.dma_start(dst, src).then_inc(c_in, 16)
            loads(0)
            for dst, src in ((w_mo[:], a["w_mla_o"].rearrange("(k p) n -> p k n", p=P)), (w_ro[:], a["w_ret_o"].rearrange("(k p) n -> p k n", p=P)),
                             (w_o[:], a["w_out"].rearrange("(k p) n -> p k n", p=P)),
                             (w_gu[:, :, 0:256], a["w_sh_gate"].rearrange("(p k) n -> p k n", p=P)),
                             (w_gu[:, :, 256:512], a["w_sh_up"].rearrange("(p k) n -> p k n", p=P)),
                             (w_sd[:], a["w_sh_down"].rearrange("(k p) n -> p k n", p=P)),
                             (w_r[:], a["w_router"].rearrange("(p k) n -> p k n", p=P))):
                sp.dma_start(dst, src).then_inc(w_in_s, 16)
            loads(1)
            with sp.Fori(2, NT) as t:
                loads(t)
            sp.wait_ge(bk, BK_STEPS)
            sp.dma_start(meta[0:P, :], meta_i[:]).then_inc(meta_out, 16)
            sp.dma_start(meta[P:P + 1, 0:1], nblk_i[0:1, :]).then_inc(meta_out, 16)
            sp.wait_ge(meta_out, 32)

        @block.gpsimd
        def _(pool):
            g = nc.gpsimd
            g.memset(col[:, 3:4], -0.5).then_inc(pl, 1)
            g.memset(carry[:], 0.0).then_inc(pl, 1)
            pool.dma_start(tok_list, a["list_fill"]).then_inc(filled, 16)
            pool.dma_start(h_perm[TOK:TOK + P, :], a["zero_rows"]).then_inc(filled, 16)
            pool.dma_start(base[TOK:TOK + P, :], a["zero_rows"]).then_inc(filled, 16)
            pool.wait_ge(c_in, 16 * NCONST)
            pool.wait_ge(filled, 48)

            def branch(t):
                pool.wait_ge(sig_ok, t + 1)
                pool.wait_ge(ret_in, t * 16 + 16)
                g.tensor_tensor(srg[:], srg[:], gates[:, 0:512], ALU.mult).then_inc(ret_ok, 1)
                g.tensor_tensor(ret[:], ret[:], gn_g[:], ALU.mult).then_inc(ret_ok, 1)
                pool.wait_ge(ret_ok, t * 3 + 2)
                g.tensor_tensor(ret[:], ret[:], srg[:], ALU.mult).then_inc(ret_ok, 1)

            def norm(t):
                pool.wait_ge(var_ok, t + 1)
                g.tensor_tensor(col[:, 1:2], col[:, 0:1], col[:, 3:4], ALU.pow).then_inc(rstd_ok, 1)
                pool.wait_ge(zn_ok, t + 1)
                g.tensor_tensor(z[:], z[:], g1[:], ALU.mult).then_inc(hg, 1)
                pool.wait_ge(hg, t + 1)
                pool.wait_ge(h_out, t * 16)
                pool.wait_ge(base_ok, t)
                g.tensor_tensor(hp[:].rearrange("p (k q) -> p q k", k=KD), z[:].rearrange("p (q k) -> p q k", k=KD), b1[:].rearrange("p (q k) -> p q k", k=KD), ALU.add).then_inc(h_ok, 1)
                wait_alone(pool, h_ok, t + 1)
                pool.dma_start(rows(t, h_perm), hp[:]).then_inc(h_out, 16)

            def scatter(t):
                wait_alone(pool, slot_ok, t + 1)
                for k in range(TOPK):
                    idx = slot_c[:, k:k + 1]
                    g.indirect_dma_start(tok_list, bass.IndirectOffsetOnAxis(ap=idx, axis=0), entry[:, k, :], None).then_inc(listed, 16)

            def body(t, first=False):
                branch(t)
                norm(t)
                if not first:
                    scatter(t - 1)
            body(0, first=True)
            with pool.Fori(1, NT) as t:
                body(t)
            scatter(NT - 1)
            pool.wait_ge(listed, 16 * TOPK * NT)
            pool.wait_ge(h_out, 16 * NT)

        @block.scalar
        def _(act):
            s_ = nc.scalar

            def sigmoids(t):
                act.wait_ge(gates_in, t * 16 + 16)
                act.wait_ge(ret_ok, t * 3)
                act.wait_ge(m_ok, t)
                s_.activation(srg[:], gates[:, 0:512], ACT.Sigmoid).then_inc(t12, 1)
                s_.activation(sg[:], gates[:, 512:2560], ACT.Sigmoid).then_inc(sig_ok, 1)

            def evac(dst, bank, n):
                act.wait_ge(turned, n + 1)
                s_.copy(dst, T[bank][:, 0:dst.free_size()]).then_inc(tev, 1)

            def body(t, first=False, last=False):
                n0 = 0 if first else t * 7 - 3
                evac(oT[:, 0:4, :].rearrange("p k n -> p (k n)"), 0, n0)
                evac(oT[:, 4:8, :].rearrange("p k n -> p (k n)"), 1, n0 + 1)
                if not first:
                    evac(hT[:, 0:4, :].rearrange("p k n -> p (k n)"), 0, n0 + 2)
                    evac(hT[:, 4:8, :].rearrange("p k n -> p (k n)"), 1, n0 + 3)
                    act.wait_ge(gu_done, t)
                    s_.activation(sgg[:], GU[:, 0:256], ACT.Sigmoid).then_inc(sgg_ok, 1)
                nm = n0 + (2 if first else 4)
                evac(mT[:, 0:4, :].rearrange("p k n -> p (k n)"), 0, nm)
                evac(mT[:, 4:8, :].rearrange("p k n -> p (k n)"), 1, nm + 1)
                if not first:
                    act.wait_ge(r_done, t)
                    act.wait_ge(rank_ok, t - 1)
                    s_.activation(sc[:], R[:, 0:NE], ACT.Sigmoid).then_inc(sc_ok, 1)
                if not last:
                    sigmoids(t + 1)
                if not first:
                    evac(aT[:].rearrange("p k n -> p (k n)"), 0, n0 + 6)
                    wait_alone(act, base_ok, t)
                    act.dma_start(rows(t - 1, base), base_sb[:]).then_inc(base_out, 16)
            sigmoids(0)
            body(0, first=True)
            with act.Fori(1, NT - 1) as t:
                body(t)
            body(NT - 1, last=True)
            n0 = NT * 7 - 3
            evac(hT[:, 0:4, :].rearrange("p k n -> p (k n)"), 0, n0)
            evac(hT[:, 4:8, :].rearrange("p k n -> p (k n)"), 1, n0 + 1)
            act.wait_ge(gu_done, NT)
            s_.activation(sgg[:], GU[:, 0:256], ACT.Sigmoid).then_inc(sgg_ok, 1)
            act.wait_ge(r_done, NT)
            act.wait_ge(rank_ok, NT - 1)
            s_.activation(sc[:], R[:, 0:NE], ACT.Sigmoid).then_inc(sc_ok, 1)
            evac(aT[:].rearrange("p k n -> p (k n)"), 0, n0 + 2)
            act.wait_ge(base_ok, NT)
            act.dma_start(rows(NT - 1, base), base_sb[:]).then_inc(base_out, 16)
            act.wait_ge(base_out, 16 * NT)

        @block.vector
        def _(dve):
            v = nc.vector

            def mixing(t):
                dve.wait_ge(y_done, t * 2 + 1)
                dve.wait_ge(sig_ok, t + 1)
                v.tensor_tensor(mix[:], sg[:, 0:D], Y[:, 0:2, :].rearrange("p a b -> p (a b)"), ALU.mult).then_inc(t12b, 1)
                dve.wait_ge(y_done, t * 2 + 2)
                v.tensor_tensor(tmp[:], sg[:, D:2 * D], Y[:, 2:4, :].rearrange("p a b -> p (a b)"), ALU.mult).then_inc(t12b, 1)
                dve.wait_ge(t12b, t * 2 + 2)
                v.tensor_tensor(mix[:], mix[:], tmp[:], ALU.add).then_inc(m_ok, 1)

            def shared_act(u):
                dve.wait_ge(sgg_ok, u + 1)
                v.tensor_tensor(act_s[:], sgg[:], GU[:, 0:256], ALU.mult).then_inc(a1_ok, 1)
                dve.wait_ge(a1_ok, u + 1)
                v.tensor_tensor(act_s[:], act_s[:], GU[:, 256:512], ALU.mult).then_inc(act_ok, 1)

            def layer_norm_1(t):
                dve.wait_ge(w_done, t + 1)
                dve.wait_ge(x_in_s, t * 16 + 16)
                dve.wait_ge(h_ok, t)
                v.scalar_tensor_tensor(z[:], x_in[:], ALPHA, Y[:, 0:2, :].rearrange("p a b -> p (a b)"), ALU.mult, ALU.add).then_inc(z_ok, 1)
                dve.wait_ge(z_ok, t + 1)
                v.bn_stats(bst[:, 0, :], z[:, 0:512]).then_inc(st, 1)
                v.bn_stats(bst[:, 1, :], z[:, 512:D]).then_inc(st, 1)
                wait_alone(dve, st, t * 3 + 2)
                v.bn_aggr(mv[:], bst[:].rearrange("p a b -> p (a b)")).then_inc(st, 1)
                dve.wait_ge(st, t * 3 + 3)
                v.tensor_scalar(col[:, 0:1], mv[:, 1:2], LN_EPS, None, ALU.add).then_inc(var_ok, 1)
                dve.wait_ge(rstd_ok, t + 1)
                v.tensor_scalar(z[:], z[:], mv[:, 0:1], col[:, 1:2], ALU.subtract, ALU.mult).then_inc(zn_ok, 1)

            def shared_out(u):
                dve.wait_ge(d_done, u + 1)
                dve.wait_ge(base_out, u * 16)
                v.scalar_tensor_tensor(base_sb[:].rearrange("p (q k) -> p q k", k=KD), hp[:].rearrange("p (k q) -> p q k", k=KD), ALPHA,
                                       Y[:, 2:4, :].rearrange("p a (q k) -> p (a q) k", k=KD), ALU.mult, ALU.add).then_inc(base_ok, 1)

            RSTEPS = 29

            def choose(u):
                n = [0]

                def link(ins, alone=False):
                    n[0] += 1
                    ins.then_inc(rt, 1)
                    dve.wait_ge(rt, u * RSTEPS + n[0])
                    if alone:
                        dve.sem_inc(passed, 1)
                dve.wait_ge(sc_ok, u + 1)
                link(v.tensor_tensor(sel[:], sc[:], bias[:], ALU.add), True)
                for q in range(8):
                    ins = v.max(top2[:, q, :], sel[:, 8 * q:8 * q + 8])
                link(ins)
                link(v.tensor_tensor(gs[:], top2[:, :, 0], top2[:, :, 1], ALU.add), True)
                link(v.max(m8[:], gs[:]), True)
                link(v.max_index(i8[:], m8[:], gs[:]))
                link(v.tensor_copy(f8[:], i8[:]))
                link(v.tensor_tensor(prod[:, 0, 0:32].rearrange("p (g k) -> p g k", k=4), iota[:, 0:8].unsqueeze(2).broadcast_to([P, 8, 4]),
                                     f8[:, 0:4].unsqueeze(1).broadcast_to([P, 8, 4]), ALU.is_equal))
                link(v.tensor_reduce(gm[:], prod[:, 0, 0:32].rearrange("p (g k) -> p g k", k=4), AX.X, ALU.add))
                sel3 = sel[:].rearrange("p (g k) -> p g k", k=8)
                link(v.tensor_tensor(sel3, sel3, gm[:].unsqueeze(2).broadcast_to([P, 8, 8]), ALU.mult))
                link(v.tensor_scalar(gm[:], gm[:], 1.0, 1e30, ALU.subtract, ALU.mult))
                link(v.tensor_tensor(sel3, sel3, gm[:].unsqueeze(2).broadcast_to([P, 8, 8]), ALU.add), True)
                link(v.max(m8[:], sel[:]), True)
                link(v.max_index(i8[:], m8[:], sel[:]))
                link(v.tensor_copy(f8[:], i8[:]))
                link(v.tensor_tensor(oh[:], iota[:, 0:NE].unsqueeze(1).broadcast_to([P, TOPK, NE]),
                                     f8[:, 0:TOPK].unsqueeze(2).broadcast_to([P, TOPK, NE]), ALU.is_equal))
                link(v.tensor_reduce(cnt[:], oh[:].rearrange("p k e -> p e k"), AX.X, ALU.add))
                link(v.tensor_scalar(cnt[:], cnt[:], at(valid, u), None, ALU.mult))
                link(v.tensor_tensor(prod[:], oh[:], sc[:].unsqueeze(1).broadcast_to([P, TOPK, NE]), ALU.mult))
                link(v.tensor_reduce(w6[:], prod[:], AX.X, ALU.add))
                link(v.tensor_reduce(wsum[:, 0:1], w6[:], AX.X, ALU.add))
                link(v.reciprocal(wsum[:, 1:2], wsum[:, 0:1]))
                link(v.tensor_scalar(w6[:], w6[:], wsum[:, 1:2], ROUTED_SCALE, ALU.mult, ALU.mult))
                assert n[0] == 22, n

            def place(u):
                n = [22]

                def link(ins):
                    n[0] += 1
                    ins.then_inc(rt, 1)
                    dve.wait_ge(rt, u * RSTEPS + n[0])
                dve.wait_ge(p_done, u + 1)
                link(v.tensor_tensor(rank[:], carry[:], R[:, 64:128], ALU.add))
                v.tensor_tensor(carry[:], carry[:], R[:, 128:192], ALU.add).then_inc(rank_ok, 1)
                link(v.tensor_tensor(rank[:], rank[:], ebase[:], ALU.add))
                link(v.tensor_tensor(prod[:], oh[:], rank[:].unsqueeze(1).broadcast_to([P, TOPK, NE]), ALU.mult))
                link(v.tensor_reduce(slot[:], prod[:], AX.X, ALU.add))
                link(v.scalar_tensor_tensor(slot[:].unsqueeze(1), slot[:].unsqueeze(1), at(valid, u), at(dump, u), ALU.mult, ALU.add))
                dve.wait_ge(listed, u * (16 * TOPK))
                link(v.tensor_copy(entry[:, :, 0], at(tid, u).broadcast_to([P, TOPK])))
                link(v.tensor_copy(entry[:, :, 1].bitcast(F32), w6[:]))
                v.tensor_copy(slot_c[:], slot[:]).then_inc(slot_ok, 1)
                assert n[0] == RSTEPS, n

            def at(x, u):
                return x[:, u:u + 1] if isinstance(u, int) else x[:, bass.ds(u, 1)]

            dve.wait_ge(c_in, 16 * NCONST)
            dve.wait_ge(pl, 2)
            mixing(0)
            layer_norm_1(0)
            with dve.Fori(1, NT) as t:
                mixing(t)
                shared_act(t - 1)
                choose(t - 1)
                layer_norm_1(t)
                shared_out(t - 1)
                place(t - 1)
            shared_act(NT - 1)
            choose(NT - 1)
            shared_out(NT - 1)
            place(NT - 1)

            n = [0]

            def link(ins):
                n[0] += 1
                ins.then_inc(bk, 1)
                dve.wait_ge(bk, n[0])
            dve.wait_ge(rank_ok, NT)
            link(v.tensor_scalar(rank[:], carry[:], P - 1.0, None, ALU.add))
            link(v.tensor_copy(nb_i[:], rank[:]))
            link(v.tensor_scalar(nb_i[:], nb_i[:], 7, None, ALU.logical_shift_right))
            link(v.memset(pre[:], 0.0))
            link(v.tensor_copy(pre[:, 0, 1:], nb_i[:]))
            s, c = 1, 0
            while s <= NE:
                link(v.tensor_copy(pre[:, 1 - c, 0:s], pre[:, c, 0:s]))
                link(v.tensor_tensor(pre[:, 1 - c, s:], pre[:, c, s:], pre[:, c, 0:NE + 1 - s], ALU.add))
                s, c = 2 * s, 1 - c
            start = pre[:, c, :]
            link(v.tensor_scalar(eqk[:], start[:, 1:], pid[:, 0:1], None, ALU.is_le))
            link(v.tensor_reduce(bt[:, 0:1], eqk[:], AX.X, ALU.add))
            other = pre[:, 1 - c, :]
            link(v.tensor_scalar(other, iota[:], bt[:, 0:1], None, ALU.is_equal))
            link(v.tensor_tensor(other, other, start, ALU.mult))
            link(v.tensor_reduce(bt[:, 1:2], other, AX.X, ALU.add))
            link(v.tensor_tensor(bt[:, 2:3], pid[:], bt[:, 1:2], ALU.subtract))
            link(v.tensor_scalar(bt[:, 3:4], bt[:, 0:1], float(TOK), None, ALU.mult))
            link(v.scalar_tensor_tensor(bt[:, 4:5], bt[:, 2:3], float(P), bt[:, 3:4], ALU.mult, ALU.add))
            link(v.tensor_scalar(bt[:, 5:6], bt[:, 0:1], NE - 1.0, None, ALU.min))
            link(v.tensor_scalar(bt[:, 4:5], bt[:, 4:5], float(LIST - P), None, ALU.min))
            link(v.tensor_copy(meta_i[:, 0:1], bt[:, 5:6]))
            link(v.tensor_copy(meta_i[:, 1:2], bt[:, 4:5]))
            link(v.tensor_scalar(bt[:, 6:7], start[:, NE:], 1.0, None, ALU.subtract))
            link(v.tensor_copy(nblk_i[:], bt[:, 6:7]))
            link(v.tensor_scalar(nblk_i[:], nblk_i[:], 1, None, ALU.logical_shift_right))
            assert n[0] == BK_STEPS, n

        @block.tensor
        def _(pe):
            t_ = nc.tensor

            def turn(srcs, bank, n, free):
                pe.wait_ge(tev, free)
                for i, src in enumerate(srcs):
                    mm = t_.transpose(T[bank][:, i * P:(i + 1) * P], src, ident[:])
                mm.then_inc(turned, 1)

            def project_out(out, xT_, w, k0, nk):
                for c in range(2):
                    for k in range(nk):
                        mm = t_.matmul(out[:, c, :], xT_[:, k0 + k, :], w[:, k, c * 512:(c + 1) * 512], start=k == 0, stop=k == nk - 1)
                return mm

            def cols_of(x, lo=0, n=4):
                return [x[:, (lo + i) * P:(lo + i + 1) * P] for i in range(n)]

            def front(t, n0):
                pe.wait_ge(o_in_s, t * 16 + 16)
                turn(cols_of(o_in), 0, n0, n0)
                pe.wait_ge(ret_ok, t * 3 + 3)
                turn(cols_of(ret), 1, n0 + 1, n0)
                pe.wait_ge(tev, n0 + 1)
                pe.wait_ge(z_ok, t)
                project_out(Y[:, 0:2, :], oT, w_mo, 0, 4).then_inc(y_done, 1)
                pe.wait_ge(tev, n0 + 2)
                if not isinstance(t, int) or t > 0:
                    pe.wait_ge(base_ok, t - 1)
                project_out(Y[:, 2:4, :], oT, w_ro, 4, 4).then_inc(y_done, 1)

            def shared_up(u, n):
                pe.wait_ge(h_ok, u + 1)
                turn(cols_of(hp), 0, n, n - 1)
                turn(cols_of(hp, 4), 1, n + 1, n)
                pe.wait_ge(tev, n + 2)
                pe.wait_ge(act_ok, u)
                for k in range(KD):
                    mm = t_.matmul(GU[:], hT[:, k, :], w_gu[:, k, :], start=k == 0, stop=k == KD - 1)
                mm.then_inc(gu_done, 1)

            def mixed_out(t, n):
                pe.wait_ge(m_ok, t + 1)
                turn(cols_of(mix), 0, n, n - 1)
                turn(cols_of(mix, 4), 1, n + 1, n)

            def router(u):
                pe.wait_ge(rank_ok, u)
                for k in range(KD):
                    mm = t_.matmul(R[:, 0:NE], hT[:, k, :], w_r[:, k, :], start=k == 0, stop=k == KD - 1)
                mm.then_inc(r_done, 1)

            def out_proj(t, n):
                pe.wait_ge(tev, n)
                project_out(Y[:, 0:2, :], mT, w_o, 0, KD).then_inc(w_done, 1)

            def shared_down(u, n):
                pe.wait_ge(act_ok, u + 1)
                turn(cols_of(act_s, 0, 2), 0, n, n - 1)
                pe.wait_ge(tev, n + 1)
                project_out(Y[:, 2:4, :], aT, w_sd, 0, 2).then_inc(d_done, 1)

            def prefix(u):
                pe.wait_ge(rt, u * 29 + 17)
                pe.wait_ge(sc_ok, u + 1)
                t_.matmul(R[:, 64:128], tri[:], cnt[:], start=True, stop=True)
                t_.matmul(R[:, 128:192], ones[:], cnt[:], start=True, stop=True).then_inc(p_done, 1)

            pe.wait_ge(c_in, 16 * NCONST)
            pe.wait_ge(w_in_s, 16 * 7)
            front(0, 0)
            mixed_out(0, 2)
            out_proj(0, 4)
            with pe.Fori(1, NT) as t:
                n0 = t * 7 - 3
                front(t, n0)
                shared_up(t - 1, n0 + 2)
                mixed_out(t, n0 + 4)
                router(t - 1)
                out_proj(t, n0 + 6)
                shared_down(t - 1, n0 + 6)
                prefix(t - 1)
            n0 = NT * 7 - 3
            shared_up(NT - 1, n0)
            router(NT - 1)
            shared_down(NT - 1, n0 + 2)
            prefix(NT - 1)


def experts(nc, a, h_perm, tok_list, meta, base):
    with ExitStack() as ctx:
        sb = lambda n, s, d=F32: ctx.enter_context(nc.sbuf_tensor("e_" + n, s, d))
        sem = lambda n: ctx.enter_context(nc.semaphore("e_" + n))
        ident = sb("ident", [P, P])
        w_g = sb("w_g", [P, 2, KD, 256])
        w_u = sb("w_u", [P, 2, KD, 256])
        w_d = sb("w_d", [P, 2, 2, D])
        idx = [sb(f"idx{c}", [P, 2], U32) for c in range(2)]
        s_idx = [sb(f"s_idx{c}", [P, 1], U32) for c in range(2)]
        s_w = sb("s_w", [P, 2])
        xg = [sb(f"xg{c}", [P, D]) for c in range(2)]
        xT = sb("xT", [P, 2, KD, P])
        sig = sb("sig", [P, 2, 256])
        act_s = sb("act_s", [P, 2, 256])
        aT = sb("aT", [P, 2, 2, P])
        y_sb = sb("y_sb", [P, 2, D])
        T = [ctx.enter_context(nc.psum_tensor(f"e_T{i}", [P, 512], F32)) for i in range(2)]
        G = [ctx.enter_context(nc.psum_tensor(f"e_G{i}", [P, 512], F32)) for i in range(2)]
        A = ctx.enter_context(nc.psum_tensor("e_A", [P, 512], F32))
        Y = [ctx.enter_context(nc.psum_tensor(f"e_Y{i}", [P, 512], F32)) for i in range(2)]
        c_in = sem("c_in")
        w_in = [sem(f"w_in{c}") for c in range(2)]
        idx_in = sem("idx_in")
        x_in = [sem(f"x_in{c}") for c in range(2)]
        y_out = [sem(f"y_out{c}") for c in range(2)]
        (x_turned, xT_act, xT_dve, gu_done, sig_ok, a1_ok, act_ok, a_turned, aT_ok, d_done, y_act, y_dve, passed, kept) = [sem(n) for n in
            "x_turned xT_act xT_dve gu_done sig_ok a1_ok act_ok a_turned aT_ok d_done y_act y_dve passed kept".split()]
        block = ctx.enter_context(nc.Block())

        def wait_alone(eng, s, value):
            eng.wait_ge(s, value)
            eng.sem_inc(passed, 1)

        def pairs(eng):
            return eng.value_load(meta[P:P + 1, 0:1], min_val=1, max_val=BLOCKS // 2)

        def number(eng, b, field, top):
            src = meta[b:b + 1, field:field + 1] if isinstance(b, int) else meta[bass.ds(b, 1), field:field + 1]
            return eng.value_load(src, min_val=0, max_val=top)

        @block.sync
        def _(sp):
            sp.dma_start(ident[:], a["ident"]).then_inc(c_in, 16)
            more = pairs(sp)

            def weights(b, c, free=None):
                e = number(sp, b, 0, NE - 1)
                if free is not None:
                    wait_alone(sp, d_done, free)
                one = bass.ds(e, 1)
                sp.dma_start(w_g[:, c], a["w_exp_gate"][one].rearrange("a (p k) n -> p (a k) n", p=P)).then_inc(w_in[c], 16)
                sp.dma_start(w_u[:, c], a["w_exp_up"][one].rearrange("a (p k) n -> p (a k) n", p=P)).then_inc(w_in[c], 16)
                sp.dma_start(w_d[:, c], a["w_exp_down"][one].rearrange("a (p k) n -> p (a k) n", p=P)).then_inc(w_in[c], 16)
            for c in range(2):
                weights(c, c)
            with sp.Fori(1, more + 1) as r:
                for c in range(2):
                    weights(sp.snap(r * 2 + c), c, sp.snap(r * 2 + (c - 1)))
            sp.wait_ge(c_in, 16)

        @block.gpsimd
        def _(pool):
            g = nc.gpsimd
            more = pairs(pool)

            def keep(c, n):
                wait_alone(pool, idx_in, n)
                g.tensor_copy(s_idx[c][:], idx[c][:, 0:1]).then_inc(kept, 1)
                g.tensor_copy(s_w[:, c:c + 1], idx[c][:, 1:2].bitcast(F32)).then_inc(kept, 1)

            def add_rows(b, c, n_kept, n_out):
                pool.wait_ge(kept, n_kept)
                pool.wait_ge(y_act, b + 1)
                wait_alone(pool, y_dve, b + 1)
                g.indirect_dma_start(base, bass.IndirectOffsetOnAxis(ap=s_idx[c][:], axis=0), y_sb[:, c, :], None, compute_op=ALU.add).then_inc(y_out[c], 16)
                pool.wait_ge(y_out[c], n_out)

            def gather(b, c, n_idx, free=None):
                lb = number(pool, b, 1, LIST - P)
                if free is not None:
                    wait_alone(pool, x_turned, free)
                    wait_alone(pool, kept, free)
                pool.dma_start(idx[c][:], tok_list[bass.ds(lb, P), :]).then_inc(idx_in, 16)
                wait_alone(pool, idx_in, n_idx)
                g.indirect_dma_start(xg[c][:], None, h_perm, bass.IndirectOffsetOnAxis(ap=idx[c][:, 0:1], axis=0)).then_inc(x_in[c], 16)
            for c in range(2):
                gather(c, c, 16 * (c + 1))
                keep(c, 16 * (c + 1))
            with pool.Fori(1, more + 1) as r:
                for c in range(2):
                    n_idx = pool.snap(r * 32 + 16 * (c + 1))
                    gather(pool.snap(r * 2 + c), c, n_idx, pool.snap(r * 4 + 2 * (c - 1)))
                    add_rows(r * 2 + (c - 2), c, r * 4 + 2 * (c - 1), r * 16)
                    keep(c, n_idx)
            for c in range(2):
                add_rows(pool.snap(more * 2 + c), c, pool.snap(more * 4 + 2 * (c + 1)), pool.snap(more * 16 + 16))

        @block.scalar
        def _(act):
            s_ = nc.scalar
            more = pairs(act)

            def first_half(b, c):
                act.wait_ge(x_turned, b * 2 + 1)
                s_.copy(xT[:, c, 0:4, :].rearrange("p k n -> p (k n)"), T[0][:]).then_inc(xT_act, 1)
                act.wait_ge(gu_done, b + 1)
                s_.activation(sig[:, c, :], G[c][:, 0:256], ACT.Sigmoid).then_inc(sig_ok, 1)

            def second_half(b, c, r):
                act.wait_ge(a_turned, b + 1)
                s_.copy(aT[:, c].rearrange("p k n -> p (k n)"), A[:, 0:256]).then_inc(aT_ok, 1)
                act.wait_ge(d_done, b + 1)
                act.wait_ge(y_out[c], r * 16)
                act.wait_ge(kept, b * 2 + 2)
                s_.activation(y_sb[:, c, 0:512], Y[0][:], ACT.Copy, scale=s_w[:, c:c + 1]).then_inc(y_act, 1)
            first_half(0, 0)
            first_half(1, 1)
            second_half(0, 0, 0)
            with act.Fori(1, more + 1) as r:
                first_half(r * 2, 0)
                second_half(r * 2 - 1, 1, r - 1)
                first_half(r * 2 + 1, 1)
                second_half(r * 2, 0, r)
            second_half(act.snap(more * 2 + 1), 1, act.snap(more + 0))

        @block.vector
        def _(dve):
            v = nc.vector
            more = pairs(dve)

            def first_half(b, c):
                dve.wait_ge(x_turned, b * 2 + 2)
                v.tensor_copy(xT[:, c, 4:8, :].rearrange("p k n -> p (k n)"), T[1][:]).then_inc(xT_dve, 1)
                dve.wait_ge(sig_ok, b + 1)
                v.tensor_tensor(sig[:, c, :], sig[:, c, :], G[c][:, 0:256], ALU.mult).then_inc(a1_ok, 1)
                dve.wait_ge(a1_ok, b + 1)
                v.tensor_tensor(act_s[:, c, :].rearrange("p (k q) -> p q k", k=2), sig[:, c, :].rearrange("p (q k) -> p q k", k=2),
                                G[c][:, 256:512].rearrange("p (q k) -> p q k", k=2), ALU.mult).then_inc(act_ok, 1)

            def second_half(b, c, r):
                dve.wait_ge(d_done, b + 1)
                dve.wait_ge(y_out[c], r * 16)
                dve.wait_ge(kept, b * 2 + 2)
                v.tensor_scalar(y_sb[:, c, 512:D], Y[1][:], s_w[:, c:c + 1], None, ALU.mult).then_inc(y_dve, 1)
            first_half(0, 0)
            first_half(1, 1)
            second_half(0, 0, 0)
            with dve.Fori(1, more + 1) as r:
                first_half(r * 2, 0)
                second_half(r * 2 - 1, 1, r - 1)
                first_half(r * 2 + 1, 1)
                second_half(r * 2, 0, r)
            second_half(dve.snap(more * 2 + 1), 1, dve.snap(more + 0))

        @block.tensor
        def _(pe):
            t_ = nc.tensor
            more = pairs(pe)

            def up(b, c, r):
                pe.wait_ge(x_in[c], r * 16 + 16)
                for q in range(2):
                    pe.wait_ge((xT_act, xT_dve)[q], b)
                    for k in range(4):
                        mm = t_.transpose(T[q][:, k * P:(k + 1) * P], xg[c][:, (4 * q + k) * P:(4 * q + k + 1) * P], ident[:])
                    mm.then_inc(x_turned, 1)
                pe.wait_ge(w_in[c], r * 48 + 48)
                pe.wait_ge(xT_act, b + 1)
                for k in range(KD):
                    if k == 4:
                        pe.wait_ge(xT_dve, b + 1)
                    for q, w in enumerate((w_g, w_u)):
                        mm = t_.matmul(G[c][:, q * 256:(q + 1) * 256], xT[:, c, k, :], w[:, c, k, :], start=k == 0 and q == 0, stop=k == KD - 1, skip_group_check=True)
                mm.then_inc(gu_done, 1)

            def down(b, c):
                pe.wait_ge(act_ok, b + 1)
                for k in range(2):
                    mm = t_.transpose(A[:, k * P:(k + 1) * P], act_s[:, c, k * P:(k + 1) * P], ident[:])
                mm.then_inc(a_turned, 1)
                pe.wait_ge(aT_ok, b + 1)
                pe.wait_ge(y_act, b)
                pe.wait_ge(y_dve, b)
                for q in range(2):
                    for k in range(2):
                        mm = t_.matmul(Y[q][:], aT[:, c, k, :], w_d[:, c, k, q * 512:(q + 1) * 512], start=k == 0, stop=k == 1)
                mm.then_inc(d_done, 1)
            pe.wait_ge(c_in, 16)
            up(0, 0, 0)
            up(1, 1, 0)
            down(0, 0)
            with pe.Fori(1, more + 1) as r:
                up(r * 2, 0, r)
                down(r * 2 - 1, 1)
                up(r * 2 + 1, 1, r)
                down(r * 2, 0)
            down(pe.snap(more * 2 + 1), 1)


def finish(nc, a, base, out_p, out_s):
    with ExitStack() as ctx:
        sb = lambda n, s, d=F32: ctx.enter_context(nc.sbuf_tensor("c_" + n, s, d))
        sem = lambda n: ctx.enter_context(nc.semaphore("c_" + n))
        g2 = sb("g2", [P, D])
        b2 = sb("b2", [P, D])
        acc = sb("acc", [P, NT, D])
        bst = sb("bst", [P, NT, 12])
        mv = sb("mv", [P, NT, 2])
        col = sb("col", [P, NT, 2])
        mhalf = sb("mhalf", [P, 1])
        c_in, pl, st, var_ok, rstd_ok, zn, out_ok, o_out = [sem(n) for n in "c_in pl st var_ok rstd_ok zn out_ok o_out".split()]
        acc_in = [sem(f"acc_in{t}") for t in range(NT)]
        block = ctx.enter_context(nc.Block())

        @block.sync
        def _(sp):
            for t in range(NT):
                sp.dma_start(acc[:, t, :], base[t * P:(t + 1) * P, :]).then_inc(acc_in[t], 16)
                if t == 1:
                    sp.dma_start(g2[:], a["ln2_g"].partition_broadcast(P)).then_inc(c_in, 16)
                    sp.dma_start(b2[:], a["ln2_b"].partition_broadcast(P)).then_inc(c_in, 16)
            for t in range(NT):
                sp.wait_ge(out_ok, t + 1)
                if t < NT - 1:
                    sp.dma_start(out_p[t * P:(t + 1) * P, :], acc[:, t, :]).then_inc(o_out, 16)
                else:
                    sp.dma_start(out_s, acc[0:DB * DQ, t, :]).then_inc(o_out, 16)
            sp.wait_ge(o_out, 16 * NT)

        @block.gpsimd
        def _(pool):
            nc.gpsimd.memset(mhalf[:], -0.5).then_inc(pl, 1)
            pool.wait_ge(pl, 1)
            for t in range(NT):
                pool.wait_ge(var_ok, t + 1)
                nc.gpsimd.tensor_tensor(col[:, t, 1:2], col[:, t, 0:1], mhalf[:], ALU.pow).then_inc(rstd_ok, 1)

        @block.vector
        def _(dve):
            v = nc.vector

            def statistics(t):
                x = acc[:, t, :]
                dve.wait_ge(acc_in[t], 16)
                v.bn_stats(bst[:, t, 0:6], x[:, 0:512]).then_inc(st, 1)
                v.bn_stats(bst[:, t, 6:12], x[:, 512:D]).then_inc(st, 1)
                dve.wait_ge(st, 3 * t + 2)
                v.bn_aggr(mv[:, t, :], bst[:, t, :]).then_inc(st, 1)
                dve.wait_ge(st, 3 * t + 3)
                v.tensor_scalar(col[:, t, 0:1], mv[:, t, 1:2], LN_EPS, None, ALU.add).then_inc(var_ok, 1)

            statistics(0)
            dve.wait_ge(c_in, 32)
            for t in range(NT):
                if t + 1 < NT:
                    statistics(t + 1)
                x = acc[:, t, :]
                dve.wait_ge(rstd_ok, t + 1)
                v.tensor_scalar(x, x, mv[:, t, 0:1], col[:, t, 1:2], ALU.subtract, ALU.mult).then_inc(zn, 1)
                dve.wait_ge(zn, 2 * t + 1)
                v.tensor_tensor(x, x, g2[:], ALU.mult).then_inc(zn, 1)
                dve.wait_ge(zn, 2 * t + 2)
                v.tensor_tensor(x, x, b2[:], ALU.add).then_inc(out_ok, 1)


def program(nc, a, o):
    def dram(name, shape, dt=F32):
        return nc.dram_tensor("d_" + name, shape, dt).ap()
    proj = dram("proj", (TOK, IN_W))
    retn = dram("retn", (TOK, 512))
    o_mla = dram("o_mla", (TOK, 512))
    h_perm = dram("h_perm", (TOK + P, D))
    base = dram("base", (TOK + P, D))
    tok_list = dram("tok_list", (LIST, 2), U32)
    meta = dram("meta", (P + 1, 2), I32)
    project(nc, a["xT"], a["w_in"], proj)
    retention(nc, a, proj, retn, o["ret_p"], o["ret_s"])
    attention(nc, a, proj, o_mla, o["ckv_p"], o["ckv_s"], o["kr_p"], o["kr_s"])
    merge(nc, a, proj, o_mla, retn, h_perm, base, tok_list, meta)
    experts(nc, a, h_perm, tok_list, meta, base)
    finish(nc, a, base, o["y_p"], o["y_s"])


def host_arrays(i):
    import numpy as np
    f = np.float32
    x = np.concatenate([i["x_prompt"].reshape(1024, D), i["x_sample"].reshape(32, D), np.zeros((96, D), f)])
    pos = np.concatenate([np.arange(S), np.tile(PAST + np.arange(DQ), DB), np.zeros(96)]).astype(f)

    def angles(half):
        inv = f(10000.0) ** (-np.arange(half, dtype=f) / f(half))
        ang = pos[:, None] * inv[None, :]
        return np.cos(ang).astype(f), np.sin(ang).astype(f)
    c16, s16 = angles(HALF)
    wq = i["w_q_up"].reshape(QL, HEADS, NOPE + ROPE)
    wq = np.concatenate([wq, wq[:, :, NOPE + HALF:], wq[:, :, NOPE:NOPE + HALF]], axis=2)
    c64, s64 = angles(64)
    kscale = f(128 ** -0.5)
    lg = np.log(f(1.0) - f(2.0) ** (-5 - np.arange(4, dtype=f)))
    idx = np.arange(P, dtype=f)
    diff = idx[None, :] - idx[:, None]

    def decay_mask(m):
        return np.where(m >= 0, np.exp(np.maximum(m, 0)[None] * lg[:, None, None]), 0).astype(f)
    same = np.kron(np.eye(DB), np.ones((DQ, DQ)))
    d_s = np.where(same > 0, np.tile(diff[0:DQ, 0:DQ], (DB, DB)), -1)
    q_idx = np.concatenate([np.tile(idx, 8), np.tile(idx[0:DQ], DB), np.zeros(96, f)])
    qdec = np.exp((q_idx[None, :] + 1) * lg[:, None]).astype(f)
    cols = np.zeros((4, P, 11), f)
    cols[:, :, 0] = np.exp((P - 1 - idx)[None, :] * lg[:, None])
    for b in range(DB):
        cols[:, DQ * b:DQ * (b + 1), 1 + b] = np.exp((DQ - 1 - idx[0:DQ])[None, :] * lg[:, None])
    cols[:, :, 9] = np.exp(P * lg)[:, None]
    cols[:, :, 10] = np.exp(DQ * lg)[:, None]
    real = (np.arange(TOK) < S + DB * DQ).astype(f).reshape(NT, P).T
    tri = np.where(np.arange(P)[None, :] <= np.arange(P)[:, None], 0, -1e30).astype(f)
    h = {
        "xT": x.T, "x": x, "w_in": i["w_in"], "ident": np.eye(P, dtype=f),
        "kv_norm_g": i["kv_norm_g"], "q_norm_gT": i["q_norm_g"].reshape(2, P).T,
        "rope16": np.stack([c16, s16]),
        "rope_q": np.concatenate([c16.T, c16.T, -s16.T, s16.T]) * f(SCALE),
        "causal": tri, "causal_s": np.tile(tri[0:DQ, 0:DQ], (HEADS, 1)),
        "w_uv": i["w_uv"],
        "rope64": np.stack([c64, s64, c64 * kscale, s64 * kscale]),
        "dmask": decay_mask(diff), "dmask_s": decay_mask(d_s),
        "qdec": np.repeat(qdec[:, None, :], P, axis=1), "ret_cols": cols,
        "state_ret": i["state_ret"],
        "tri": (np.arange(P)[:, None] < np.arange(P)[None, :]).astype(f), "ones": np.ones((P, P), f),
        "iota": np.tile(np.arange(NE + 1, dtype=f), (P, 1)), "ebase": np.tile(np.arange(NE, dtype=f) * TOK, (P, 1)),
        "pid": np.arange(P, dtype=f)[:, None], "valid": real,
        "dump": ((1 - real)[:, :, None] * (NE * TOK + P * np.arange(TOPK)[None, None, :] + np.arange(P)[:, None, None])).astype(f),
        "list_fill": np.stack([TOK + np.arange(LIST) % P, np.zeros(LIST)], axis=1).astype(np.uint32), "zero_rows": np.zeros((P, D), f),
        "tid": (np.arange(NT)[None, :] * P + np.arange(P)[:, None]).astype(np.uint32),
        **{k: i[k] for k in ("ret_gn_g", "ln1_g", "ln1_b", "ln2_g", "ln2_b", "router_bias", "w_mla_o", "w_ret_o", "w_out", "w_router",
                             "w_sh_gate", "w_sh_up", "w_sh_down", "w_exp_gate", "w_exp_up", "w_exp_down")},
        "w_q_ext": wq.transpose(1, 0, 2),
        "w_uk_h": i["w_uk"].reshape(KVL, HEADS, NOPE).transpose(1, 0, 2),
        "w_ukT_h": i["w_uk"].reshape(KVL, HEADS, NOPE).transpose(1, 2, 0),
        "page_table": i["page_table"], "cache_ckv": i["cache_ckv"],
        "cache_ckvT": i["cache_ckv"].transpose(0, 2, 1), "cache_kropeT": i["cache_krope"].transpose(0, 2, 1),
    }
    return {k: np.ascontiguousarray(v) for k, v in h.items()}


OUTS = {"y_p": (1024, 1024), "y_s": (32, 1024), "ckv_p": (1024, 128), "ckv_s": (32, 128), "kr_p": (1024, 32), "kr_s": (32, 32), "ret_p": (4, 128, 128), "ret_s": (8, 4, 128, 128)}


RETURNED = {"y_p": (1, S, D), "y_s": (DB, DQ, D), "ckv_p": (1, S, KVL), "kr_p": (1, S, ROPE), "ret_p": (1, 4, 128, 128),
            "ckv_s": (DB, DQ, KVL), "kr_s": (DB, DQ, ROPE), "ret_s": (DB, 4, 128, 128)}


def kernel(**inputs):
    import concourse.bacc as bacc
    from concourse.bass_utils import run_bass_kernel_spmd as run
    nc = bacc.Bacc("TRN2", target_bir_lowering=False, num_devices=1)
    host = host_arrays(inputs)
    a = {k: nc.dram_tensor("in_" + k, v.shape, mybir.dt.from_np(v.dtype), kind="ExternalInput").ap() for k, v in host.items()}
    o = {k: nc.dram_tensor("out_" + k, s, F32, kind="ExternalOutput").ap() for k, s in OUTS.items()}
    program(nc, a, o)
    r = run(nc, [{"in_" + k: v for k, v in host.items()}], core_ids=[0])
    got = r.results[0]
    return tuple(got["out_" + k].reshape(s) for k, s in RETURNED.items())
```

```python
from contextlib import ExitStack
import concourse.bass as bass
from concourse import mybir

ALU = mybir.AluOpType
ACT = mybir.ActivationFunctionType
F32 = mybir.dt.float32
F32R = mybir.dt.float32r
I32 = mybir.dt.int32
U32 = mybir.dt.uint32
AX = mybir.AxisListType
P = 128
D = 1024
KD = D // P
NT = 9
TOK = NT * P
IN_W = 4512
GATE_W = 2560
CW = 244
NCHUNK = (IN_W - GATE_W) // CW
FW = GATE_W // 8


QL, KVL, ROPE, NOPE, VD, HEADS = 256, 128, 32, 64, 64, 8
HALF = ROPE // 2
S = 1024
DB, DQ = 8, 4
N_PHYS = 80
PAST = 1024
NE, TOPK, FF = 64, 6, 256
LIST = (NE + 1) * TOK
BLOCKS = (S + DB * DQ) * TOPK // P + NE
BK_STEPS = 34
ALPHA = 2.0 ** 0.25
ROUTED_SCALE = 2.5
RMS_EPS, LN_EPS = 1e-6, 1e-5
SCALE = (NOPE + ROPE) ** -0.5
QCH = ((0, 512), (512, 512), (1024, 128))


def groups(i):
    return [i] if i < 4 else [2 * i - 4, 2 * i - 3]


def gw(i, gi):
    done = 4 * (gi - groups(i)[0])
    return P * min(4, i + 1 - done)


def project(nc, passed, x_sb, gw_sb, gw_in, xT, w_in, proj):
    with ExitStack() as ctx:
        sb = lambda n, s, d=F32: ctx.enter_context(nc.sbuf_tensor(n, s, d))
        sem = lambda n: ctx.enter_context(nc.semaphore(n))
        w_sb = sb("w_sb", [P, 2, KD, CW])
        w_hi = sb("w_hi", [P, 2, KD, CW], F32R)
        w_lo = sb("w_lo", [P, 2, KD, CW], F32R)
        upper = sb("upper", [P, KD, CW])
        x_hi = sb("x_hi", [P, KD, TOK], F32R)
        x_lo = sb("x_lo", [P, KD, TOK], F32R)
        o_sb = sb("o_sb", [P, 2, NT, CW])
        x_split = sem("x_split")
        w_split = sem("w_split")
        ps = ctx.enter_context(nc.psum_tensor("ps", [P, 6, 512], F32))
        x_in = [sem(f"x_in{i}") for i in range(3)]
        w_in_sem = [sem(f"w_ready{c}") for c in range(2)]
        tile_done = sem("tile_done")
        free_by_dve = sem("free_by_dve")
        free_by_act = sem("free_by_act")
        dve_out = sem("dve_out")
        act_out = sem("act_out")
        stored = [sem(f"stored{c}") for c in range(2)]
        block = ctx.enter_context(nc.Block())
        wv = w_in.rearrange("(k p) n -> p k n", p=P)
        pv = proj.rearrange("(t p) n -> p t n", p=P)

        @block.sync
        def _(sp):
            xv = xT.rearrange("(k p) t -> p k t", p=P)
            sp.dma_start(w_sb[:, 0], wv[:, :, 0:CW]).then_inc(w_in_sem[0], 16)
            for i, tiles in enumerate(((0, 1), (1, 3), (3, NT))):
                at = slice(tiles[0] * P, tiles[1] * P)
                sp.dma_start(x_sb[:, :, at], xv[:, :, at]).then_inc(x_in[i], 16)
            sp.dma_start(w_sb[:, 1], wv[:, :, CW:2 * CW]).then_inc(w_in_sem[1], 16)
            for q in range(2):
                sp.dma_start(gw_sb[:, q], wv[:, :, IN_W - GATE_W + q * FW:IN_W - GATE_W + (q + 1) * FW]).then_inc(gw_in[q], 16)
            with sp.Fori(0, NCHUNK // 2 - 1) as r:
                for c in range(2):
                    done, by_dve, by_act = sp.snap(r * 18 + 9 * c + 9), sp.snap(r * 9 + (5 if c == 0 else 9)), sp.snap(r * 9 + (4 if c == 0 else 9))
                    src_at, dst_at = sp.snap(r * (2 * CW) + (2 + c) * CW), sp.snap(r * (2 * CW) + c * CW)
                    sp.wait_ge(tile_done, done)
                    sp.sem_inc(passed, 1)
                    sp.dma_start(w_sb[:, c], wv[:, :, bass.ds(src_at, CW)]).then_inc(w_in_sem[c], 16)
                    sp.wait_ge(dve_out, by_dve)
                    sp.sem_inc(passed, 1)
                    sp.wait_ge(act_out, by_act)
                    sp.sem_inc(passed, 1)
                    sp.dma_start(pv[:, :, bass.ds(dst_at, CW)], o_sb[:, c]).then_inc(stored[c], 16)
            r = NCHUNK // 2 - 1
            for c in range(2):
                sp.wait_ge(dve_out, r * 9 + (5 if c == 0 else 9))
                sp.wait_ge(act_out, r * 9 + (4 if c == 0 else 9))
                sp.dma_start(pv[:, :, r * 2 * CW + c * CW:r * 2 * CW + (c + 1) * CW], o_sb[:, c]).then_inc(stored[c], 16)
            for c in range(2):
                sp.wait_ge(stored[c], 16 * (NCHUNK // 2))

        @block.tensor
        def _(pe):
            with pe.Fori(0, NCHUNK // 2) as r:
                for j in range(18):
                    c, t = j // 9, j % 9
                    if t == 0:
                        pe.wait_ge(w_split, r * 6 + 3 * c + 3)
                    pe.wait_ge(free_by_dve if j % 2 == 0 else free_by_act, r * 9 + j // 2 + 1)
                    if j < NT:
                        pe.wait_ge(x_split, 3 * j + 3)
                    for k in range(KD):
                        for i, (x, w) in enumerate(((x_hi, w_hi), (x_hi, w_lo), (x_lo, w_hi))):
                            mm = nc.tensor.matmul(ps[:, j % 6, 0:CW], x[:, k, t * P:(t + 1) * P], w[:, c, k, :],
                                                  start=k == 0 and i == 0, stop=k == KD - 1 and i == 2)
                    mm.then_inc(tile_done, 1)

        def evac(eng, op, par, free, out, r, between=None):
            for j in range(par, 18, 2):
                c, t = j // 9, j % 9
                if t < 2:
                    eng.wait_ge(stored[c], r * 16)
                eng.wait_ge(tile_done, r * 18 + j + 1)
                op(o_sb[:, c, t, :], ps[:, j % 6, 0:CW]).then_inc(out, 1)
                eng.wait_ge(out, r * 9 + j // 2 + 1)
                eng.sem_inc(free, 1)
                if between:
                    between(j)

        @block.vector
        def _(dve):
            v = nc.vector

            def split(src, hi, lo, done, n):
                up = upper[:, :, 0:src.shape[2]]
                v.tensor_scalar(up.bitcast(I32), src.bitcast(I32), 12, 12, ALU.logical_shift_right, ALU.logical_shift_left).then_inc(done, 1)
                dve.wait_ge(done, n)
                v.tensor_copy(hi, up).then_inc(done, 1)
                v.tensor_tensor(lo, src, up, ALU.subtract).then_inc(done, 1)
                dve.wait_ge(done, n + 2)
                dve.sem_inc(passed, 1)

            def split_weights(c, n_in, n):
                dve.wait_ge(w_in_sem[c], n_in)
                dve.sem_inc(passed, 1)
                split(w_sb[:, c], w_hi[:, c], w_lo[:, c], w_split, n)

            dve.sem_inc(free_by_dve, 3)
            split_weights(0, 16, 1)
            for t in range(NT):
                if t in (0, 1, 3):
                    dve.wait_ge(x_in[(0, 1, 3).index(t)], 16)
                at = slice(t * P, (t + 1) * P)
                split(x_sb[:, :, at], x_hi[:, :, at], x_lo[:, :, at], x_split, 3 * t + 1)

            def body(r, last=False):
                def between(j):
                    if j == 4:
                        split_weights(1, r * 16 + 16, r * 6 + 4)
                    elif j == 14 and not last:
                        split_weights(0, r * 16 + 32, r * 6 + 7)
                evac(dve, v.tensor_copy, 0, free_by_dve, dve_out, r, between)
            with dve.Fori(0, NCHUNK // 2 - 1) as r:
                body(r)
            body(NCHUNK // 2 - 1, last=True)

        @block.scalar
        def _(act):
            act.sem_inc(free_by_act, 3)
            with act.Fori(0, NCHUNK // 2) as r:
                evac(act, nc.scalar.copy, 1, free_by_act, act_out, r)


def attention(nc, passed, a, proj, o_mla, out_ckv_p, out_ckv_s, out_kr_p, out_kr_s):
    with ExitStack() as ctx:
        sb = lambda n, s, d=F32: ctx.enter_context(nc.sbuf_tensor(n, s, d))
        sem = lambda n: ctx.enter_context(nc.semaphore(n))
        ident = sb("ident", [P, P])
        cq = sb("cq", [P, NT, QL])
        sq = sb("sq", [P, NT, QL])
        sq_q = sb("sq_q", [P, QL])
        sq_ok = sem("sq_ok")
        ckv = sb("ckv", [P, NT, KVL])
        kr = sb("kr", [P, NT, ROPE])
        krp = sb("krp", [P, NT, NOPE + ROPE])
        t16 = sb("t16", [P, 4, NT, HALF])
        rot = sb("rot", [P, 2, NT, HALF])
        stat = sb("stat", [P, 4, NT])
        mhalf = sb("mhalf", [P, NT])
        kvg = sb("kvg", [P, KVL])
        qg = sb("qg", [P, 2])
        cqT = sb("cqT", [P, 2, TOK])
        ckvT = sb("ckvT", [P, TOK])
        qtab = sb("qtab", [P, TOK])
        wq_h = sb("wq_h", [P, 2, P])
        wuk_h = sb("wuk_h", [P, NOPE])
        wukT_h = sb("wukT_h", [NOPE, KVL])
        wuv = sb("wuv", [P, HEADS * VD])
        qT = sb("qT", [P, TOK])
        kT = sb("kT", [P, S])
        krsT = sb("krsT", [P, P])
        rt = sb("rt", [P, 2, 512])
        v_h = sb("v_h", [P, 8, VD])
        mask = sb("mask", [P, P])
        nmax = sb("nmax", [P, 8])
        sums = sb("sums", [P, 8])
        rinv = sb("rinv", [P, 8])
        prob = sb("prob", [P, 2, S])
        pT = sb("pT", [P, 4, 512])
        o_all = sb("o_all", [P, NT, HEADS * VD])
        qlat = sb("qlat", [P, DB, HEADS, DQ])
        qrs = sb("qrs", [P, DB, HEADS, DQ])
        pS = ctx.enter_context(nc.psum_tensor("pS", [P, 4, 512], F32))
        pT_ps = ctx.enter_context(nc.psum_tensor("pT_ps", [P, 2, 512], F32))
        pO = ctx.enter_context(nc.psum_tensor("pO", [P, 512], F32))

        pN = ctx.enter_context(nc.psum_tensor("pN", [P, 512], F32))
        s_new_ps = (pT_ps[0:HEADS * DQ, 1, 0:DQ], pN[0:HEADS * DQ, 0:DQ])

        ptab = sb("ptab", [1, DB * 8], I32)
        ptab_in = sem("ptab_in")
        page_kv = sb("page_kv", [P, 2, 8, KVL])
        page_kvT = sb("page_kvT", [P, 2, S])
        page_krT = sb("page_krT", [P, 2, S])
        new_kv = sb("new_kv", [DQ, 2, KVL])
        qlat_b = sb("qlat_b", [P, 2, HEADS * DQ])
        qrs_b = sb("qrs_b", [P, 2, HEADS * DQ])
        krs_b = sb("krs_b", [ROPE, 2, DQ])
        smask = sb("smask", [HEADS * DQ, DQ])
        prob_s = sb("prob_s", [HEADS * DQ, 2, S + DQ])
        st_s = sb("st_s", [HEADS * DQ, 2, 8])
        s_new = sb("s_new", [HEADS * DQ, 2, DQ])
        pTs = sb("pTs", [P, 9 * HEADS * DQ])
        olat = sb("olat", [P, HEADS, DB, DQ])

        const_in = sem("const_in")
        lat_in = sem("lat_in")
        w_ready = sem("w_ready")
        dv = sem("dv")
        pl = sem("pl")
        lat_ready = sem("lat_ready")
        lat_T = sem("lat_T")
        lat_ev = sem("lat_ev")
        lat_out = sem("lat_out")
        pro_mm = sem("pro_mm")
        pro_act = sem("pro_act")
        pro_dve = sem("pro_dve")
        s_done = sem("s_done")
        max_done = sem("max_done")
        masked = sem("masked")
        exp_done = sem("exp_done")
        pt_done = sem("pt_done")
        pt_act = sem("pt_act")
        pt_dve = sem("pt_dve")
        o_done = sem("o_done")
        o_ev = sem("o_ev")
        rv = sem("rv")
        rv2 = sem("rv2")
        page_in = [sem(f"page_in{c}") for c in range(2)]
        page_T_in = [sem(f"page_T_in{c}") for c in range(2)]
        q_b = sem("q_b")
        ss_done = sem("ss_done")
        smax = sem("smax")
        sexp = sem("sexp")
        snorm = sem("snorm")
        st_done = sem("st_done")
        st_ev = sem("st_ev")
        ol_done = sem("ol_done")
        ol_ev = sem("ol_ev")
        os_done = sem("os_done")
        os_ev = sem("os_ev")
        o_out = sem("o_out")
        block = ctx.enter_context(nc.Block())
        pv = proj.rearrange("(t p) n -> p t n", p=P)
        HQ = HEADS * DQ
        CONSTS = 8

        def page_numbers(eng, b):
            at = [bass.ds(b * 8 + j, 1) if not isinstance(b, int) else slice(b * 8 + j, b * 8 + j + 1) for j in range(8)]
            return [eng.value_load(ptab[0:1, x], min_val=0, max_val=N_PHYS - 1) for x in at]

        @block.sync
        def _(sp):
            sp.dma_start(ckv[:], pv[:, :, QL:QL + KVL]).then_inc(lat_in, 16)
            sp.dma_start(cq[:], pv[:, :, 0:QL]).then_inc(lat_in, 16)
            sp.dma_start(kr[:], pv[:, :, QL + KVL:QL + KVL + ROPE]).then_inc(lat_in, 16)
            sp.dma_start(ident[:], a["ident"]).then_inc(const_in, 16)
            sp.dma_start(kvg[:], a["kv_norm_g"].partition_broadcast(P)).then_inc(const_in, 16)
            sp.dma_start(qg[:], a["q_norm_gT"]).then_inc(const_in, 16)
            sp.dma_start(rot[:], a["rope16"].rearrange("s (t p) c -> p s t c", p=P)).then_inc(const_in, 16)
            sp.dma_start(qtab[NOPE:P, :], a["rope_q"]).then_inc(const_in, 16)
            sp.dma_start(mask[:], a["causal"]).then_inc(const_in, 16)
            sp.dma_start(smask[:], a["causal_s"]).then_inc(const_in, 16)
            sp.dma_start(wuv[:], a["w_uv"]).then_inc(const_in, 16)

            def head_weights(h):
                if isinstance(h, int):
                    h = slice(h, h + 1)
                else:
                    h = bass.ds(h, 1)
                sp.dma_start(wq_h[:], a["w_q_ext"][h].rearrange("a (k p) n -> p (a k) n", p=P)).then_inc(w_ready, 16)
                sp.dma_start(wuk_h[:], a["w_uk_h"][h].rearrange("a p n -> p (a n)")).then_inc(w_ready, 16)
                sp.dma_start(wukT_h[:], a["w_ukT_h"][h].rearrange("a p n -> p (a n)")).then_inc(w_ready, 16)

            head_weights(0)
            sp.dma_start(ptab[:], a["page_table"].rearrange("(o b) j -> o (b j)", o=1)).then_inc(ptab_in, 16)
            sp.wait_ge(lat_ready, 2)
            sp.dma_start(out_ckv_p.rearrange("(t p) c -> p t c", p=P), ckv[:, 0:8, :]).then_inc(lat_out, 16)
            sp.dma_start(out_ckv_s, ckv[0:DB * DQ, 8, :]).then_inc(lat_out, 16)
            sp.wait_ge(lat_ready, 3)
            sp.dma_start(out_kr_p.rearrange("(t p) c -> p t c", p=P), krp[:, 0:8, NOPE:]).then_inc(lat_out, 16)
            sp.dma_start(out_kr_s, krp[0:DB * DQ, 8, NOPE:]).then_inc(lat_out, 16)
            with sp.Fori(0, HEADS - 1) as h:
                nxt, used_up = sp.snap(h + 1), sp.snap(h * 7 + 7)
                sp.wait_ge(pro_mm, used_up)
                sp.sem_inc(passed, 1)
                head_weights(nxt)
            sp.wait_ge(lat_out, 64)

            def pages_turned(b, c, used=None):
                pgs = page_numbers(sp, b)
                if used is not None:
                    sp.wait_ge(ss_done, used)
                    sp.sem_inc(passed, 1)
                for j in range(8):
                    one = bass.ds(pgs[j], 1)
                    sp.dma_start(page_kvT[:, c, j * P:(j + 1) * P], a["cache_ckvT"][one].rearrange("a p c -> p (a c)")).then_inc(page_T_in[c], 16)
                    sp.dma_start(page_krT[0:ROPE, c, j * P:(j + 1) * P], a["cache_kropeT"][one].rearrange("a p c -> p (a c)")).then_inc(page_T_in[c], 16)

            sp.wait_ge(ptab_in, 16)
            for c in range(2):
                pages_turned(c, c)
            with sp.Fori(0, DB // 2 - 1) as r:
                for c in range(2):
                    used, nxt = sp.snap(r * 2 + (c + 1)), sp.snap(r * 2 + (c + 2))
                    pages_turned(nxt, c, used)
            sp.wait_ge(os_ev, 1)
            sp.dma_start(o_mla[S:TOK], o_all[:, 8]).then_inc(o_out, 16)
            sp.wait_ge(o_out, 32)

        @block.gpsimd
        def _(pool):
            def pages(b, c, used=None):
                pgs = page_numbers(pool, b)
                src = out_ckv_s.rearrange("(b q) c -> b q c", q=DQ)[bass.ds(b, 1)]
                if used is not None:
                    pool.wait_ge(ol_done, used)
                    pool.sem_inc(passed, 1)
                pool.dma_start(new_kv[:, c, :], src.rearrange("a q c -> q (a c)")).then_inc(page_in[c], 16)
                for j in range(8):
                    pool.dma_start(page_kv[:, c, j, :], a["cache_ckv"][bass.ds(pgs[j], 1)].rearrange("a p c -> p (a c)")).then_inc(page_in[c], 16)
            pool.memset(mhalf[:], -0.5).then_inc(pl, 1)
            pool.memset(krp[:], 0.0).then_inc(pl, 1)
            pool.memset(o_all[:, 8, :], 0.0).then_inc(pl, 1)
            pool.wait_ge(pl, 1)
            for n in (1, 0):
                pool.wait_ge(dv, 4 - n)
                pool.tensor_tensor(stat[:, 2 + n, :], stat[:, n, :], mhalf[:], ALU.pow).then_inc(pl, 1)
            pool.wait_ge(lat_out, 64)
            pool.wait_ge(ptab_in, 16)
            for c in range(2):
                pages(c, c)
            with pool.Fori(0, DB // 2 - 1) as r:
                for c in range(2):
                    used, nxt = pool.snap(r * 2 + (c + 1)), pool.snap(r * 2 + (c + 2))
                    pages(nxt, c, used)

        @block.vector
        def _(dve):
            v = nc.vector
            dve.wait_ge(lat_in, 48)
            dve.wait_ge(const_in, 16 * CONSTS)
            v.tensor_tensor(sq[:, :, 0:KVL], ckv[:], ckv[:], ALU.mult).then_inc(dv, 1)
            dve.wait_ge(dv, 1)
            v.tensor_reduce(stat[:, 1, :], sq[:, :, 0:KVL], AX.X, ALU.add).then_inc(dv, 1)
            dve.wait_ge(dv, 2)
            v.tensor_scalar(stat[:, 1, :], stat[:, 1, :], 1.0 / KVL, RMS_EPS, ALU.mult, ALU.add).then_inc(dv, 1)
            dve.wait_ge(sq_ok, NT)
            v.tensor_scalar(stat[:, 0, :], stat[:, 0, :], 1.0 / QL, RMS_EPS, ALU.mult, ALU.add).then_inc(dv, 1)
            dve.wait_ge(pl, 4)
            v.tensor_tensor(ckv[:], ckv[:], stat[:, 3, :].unsqueeze(2).broadcast_to([P, NT, KVL]), ALU.mult).then_inc(dv, 1)
            dve.wait_ge(pl, 5)
            v.tensor_tensor(cq[:], cq[:], stat[:, 2, :].unsqueeze(2).broadcast_to([P, NT, QL]), ALU.mult).then_inc(lat_ready, 1)
            dve.wait_ge(dv, 5)
            v.tensor_tensor(ckv[:], ckv[:], kvg[:].unsqueeze(1).broadcast_to([P, NT, KVL]), ALU.mult).then_inc(lat_ready, 1)
            cos, sin = rot[:, 0], rot[:, 1]
            x1, x2 = kr[:, :, 0:HALF], kr[:, :, HALF:ROPE]
            v.tensor_tensor(t16[:, 0], x1, cos, ALU.mult).then_inc(dv, 1)
            v.tensor_tensor(t16[:, 1], x2, sin, ALU.mult).then_inc(dv, 1)
            v.tensor_tensor(t16[:, 2], x2, cos, ALU.mult).then_inc(dv, 1)
            v.tensor_tensor(t16[:, 3], x1, sin, ALU.mult).then_inc(dv, 1)
            dve.wait_ge(dv, 9)
            v.tensor_tensor(krp[:, :, NOPE:NOPE + HALF], t16[:, 0], t16[:, 1], ALU.subtract).then_inc(dv, 1)
            v.tensor_tensor(krp[:, :, NOPE + HALF:], t16[:, 2], t16[:, 3], ALU.add).then_inc(dv, 1)
            dve.wait_ge(dv, 11)
            v.engine_nop().then_inc(lat_ready, 1)

            with dve.Fori(0, HEADS) as h:
                for g, (lo, w) in enumerate(QCH):
                    dve.wait_ge(pro_mm, h * 7 + g + 1)
                    v.tensor_tensor(rt[64:96, 0, 0:w], pS[64:96, g, 0:w], qtab[64:96, lo:lo + w], ALU.mult).then_inc(rv, 1)
                    v.tensor_tensor(rt[64:96, 1, 0:w], pS[96:128, g, 0:w], qtab[96:128, lo:lo + w], ALU.mult).then_inc(rv, 1)
                    dve.wait_ge(rv, h * 6 + 2 * g + 2)
                    v.tensor_tensor(qT[64:96, lo:lo + w], rt[64:96, 0, 0:w], rt[64:96, 1, 0:w], ALU.add).then_inc(pro_dve, 1)
                    dve.wait_ge(pro_dve, h * 5 + g + 1)
                dve.wait_ge(pro_mm, h * 7 + 6)
                v.tensor_copy(v_h[:], pS[:, 1, :]).then_inc(pro_dve, 1)
                v.tensor_copy(qrs[0:32, :, bass.ds(h, 1), :], qT[64:96, S:S + DB * DQ].rearrange("p (b a q) -> p b a q", b=DB, a=1)).then_inc(pro_dve, 1)
                def softmax_max(i):
                    s = pS[:, 2 * (i % 2):2 * (i % 2) + 2, :].rearrange("p a b -> p (a b)")
                    dve.wait_ge(s_done, h * 8 + i + 1)
                    v.tensor_tensor(s[:, i * P:(i + 1) * P], s[:, i * P:(i + 1) * P], mask[:], ALU.add).then_inc(masked, 1)
                    dve.wait_ge(masked, h * 8 + i + 1)
                    v.tensor_reduce(nmax[:, i:i + 1], s[:, 0:(i + 1) * P], AX.X, ALU.max, negate=True).then_inc(max_done, 1)

                def evac_odd(i):
                    for gi in groups(i):
                        if gi % 2:
                            dve.wait_ge(pt_done, h * 12 + gi + 1)
                            w = gw(i, gi)
                            v.tensor_copy(pT[:, gi % 4, 0:w], pT_ps[:, 1, 0:w]).then_inc(pt_dve, 1)
                softmax_max(0)
                softmax_max(1)
                for i in range(8):
                    evac_odd(i)
                    if i + 2 < 8:
                        softmax_max(i + 2)
                v.reciprocal(rinv[:], sums[:]).then_inc(rv2, 1)
                dve.wait_ge(rv2, h + 1)
                dve.wait_ge(o_done, h + 1)
                v.tensor_tensor(o_all[:, 0:8, bass.ds(h * VD, VD)], pO[:].rearrange("p (t c) -> p t c", c=VD), rinv[:].unsqueeze(2).broadcast_to([P, 8, VD]), ALU.mult).then_inc(o_ev, 1)

            dve.wait_ge(pro_act, 6 * HEADS)

            def sample_q(b, c):
                v.tensor_copy(qlat_b[:, c], qlat[:, bass.ds(b, 1)].rearrange("p a h q -> p (a h q)")).then_inc(q_b, 1)
                v.tensor_copy(qrs_b[0:32, c], qrs[0:32, bass.ds(b, 1)].rearrange("p a h q -> p (a h q)")).then_inc(q_b, 1)
                v.tensor_copy(krs_b[:, c], krsT[0:32, bass.ds(b * DQ, DQ)]).then_inc(q_b, 1)

            def sample(b, c, last=False):
                col = lambda i: st_s[:, c, i:i + 1]
                dve.wait_ge(ss_done, b + 1)
                v.tensor_tensor(s_new[:, c], s_new_ps[c], smask[:], ALU.add).then_inc(smax, 1)
                v.tensor_reduce(col(0), pS[0:HQ, 2 * c:2 * c + 2, :].rearrange("p a b -> p (a b)"), AX.X, ALU.max, negate=True).then_inc(smax, 1)
                dve.wait_ge(smax, b * 4 + 2)
                v.tensor_reduce(col(1), s_new[:, c], AX.X, ALU.max, negate=True).then_inc(smax, 1)
                dve.wait_ge(smax, b * 4 + 3)
                v.tensor_tensor(col(2), col(0), col(1), ALU.min).then_inc(smax, 1)
                dve.wait_ge(sexp, b * 2 + 2)
                v.tensor_tensor(col(5), col(3), col(4), ALU.add).then_inc(snorm, 1)
                dve.wait_ge(snorm, b * 3 + 1)
                v.reciprocal(col(6), col(5)).then_inc(snorm, 1)
                dve.wait_ge(snorm, b * 3 + 2)
                v.tensor_scalar(prob_s[:, c], prob_s[:, c], col(6), None, ALU.mult).then_inc(snorm, 1)
                dve.wait_ge(st_done, b + 1)
                v.tensor_copy(pTs[:, 0:8 * HQ], pT_ps[:, 0, 0:8 * HQ]).then_inc(st_ev, 1)
                v.tensor_copy(pTs[0:DQ, 8 * HQ:], pT_ps[0:DQ, 0, 8 * HQ:9 * HQ]).then_inc(st_ev, 1)
                if not last:
                    sample_q(b + 2, c)
                dve.wait_ge(ol_done, b + 1)
                v.tensor_copy(olat[:, :, bass.ds(b, 1), :], pO[:, 0:HQ].rearrange("p (h a q) -> p h a q", h=HEADS, a=1)).then_inc(ol_ev, 1)
            for c in range(2):
                sample_q(c, c)
            with dve.Fori(0, DB // 2 - 1) as r:
                for c in range(2):
                    sample(r * 2 + c, c)
            for c in range(2):
                sample(DB - 2 + c, c, last=True)
            dve.wait_ge(os_done, 1)
            v.tensor_copy(o_all[0:DB * DQ, 8, :], pS[0:DB * DQ, 0, :]).then_inc(os_ev, 1)

        @block.scalar
        def _(act):
            s_ = nc.scalar
            act.wait_ge(const_in, 16 * CONSTS)
            act.wait_ge(lat_in, 48)
            for t in range(NT):
                act.wait_ge(sq_ok, t)
                s_.activation(sq_q[:], cq[:, t, :], ACT.Square, accum_out=stat[:, 0, t:t + 1]).then_inc(sq_ok, 1)
            for g in range(12):
                arr, part = g // 3, g % 3
                w = 512 if part < 2 else P
                lo = part * 512
                act.wait_ge(lat_T, g + 1)
                src = pS[:, g % 4, 0:w]
                if arr < 2:
                    s_.activation(cqT[:, arr, lo:lo + w], src, ACT.Copy, scale=qg[:, arr:arr + 1]).then_inc(lat_ev, 1)
                elif arr == 2:
                    s_.copy(ckvT[:, lo:lo + w], src).then_inc(lat_ev, 1)
                elif part < 2:
                    s_.copy(kT[64:96, lo:lo + w], pS[64:96, g % 4, 0:w]).then_inc(lat_ev, 1)
                else:
                    s_.copy(krsT[0:32, :], pS[64:96, g % 4, 0:w]).then_inc(lat_ev, 1)

            with act.Fori(0, HEADS) as h:
                for g, (lo, w) in enumerate(QCH):
                    act.wait_ge(pro_mm, h * 7 + g + 1)
                    s_.activation(qT[0:64, lo:lo + w], pS[0:64, g, 0:w], ACT.Copy, scale=SCALE).then_inc(pro_act, 1)
                for g in range(2):
                    act.wait_ge(pro_mm, h * 7 + 4 + g)
                    s_.copy(kT[0:64, g * 512:(g + 1) * 512], pS[0:64, (3 + g) % 4, :]).then_inc(pro_act, 1)
                act.wait_ge(pro_mm, h * 7 + 7)
                s_.copy(qlat[:, :, bass.ds(h, 1), :], pS[:, 2, 0:DB * DQ].rearrange("p (b a q) -> p b a q", b=DB, a=1)).then_inc(pro_act, 1)

                def expo(i):
                    act.wait_ge(max_done, h * 8 + i + 1)
                    s = pS[:, 2 * (i % 2):2 * (i % 2) + 2, :].rearrange("p a b -> p (a b)")
                    s_.activation(prob[:, i % 2, 0:(i + 1) * P], s[:, 0:(i + 1) * P], ACT.Exp, bias=nmax[:, i:i + 1], accum_out=sums[:, i:i + 1]).then_inc(exp_done, 1)

                def evac_even(i):
                    for gi in groups(i):
                        if gi % 2 == 0:
                            act.wait_ge(pt_done, h * 12 + gi + 1)
                            w = gw(i, gi)
                            s_.copy(pT[:, gi % 4, 0:w], pT_ps[:, 0, 0:w]).then_inc(pt_act, 1)
                expo(0)
                for i in range(8):
                    if i + 1 < 8:
                        if i >= 1:
                            act.wait_ge(pt_done, h * 12 + groups(i - 1)[-1] + 1)
                        expo(i + 1)
                    evac_even(i)

            act.wait_ge(o_ev, HEADS)
            act.dma_start(o_mla[0:S].rearrange("(t p) c -> p t c", p=P), o_all[:, 0:8]).then_inc(o_out, 16)
            with act.Fori(0, DB // 2) as r:
                for c in range(2):
                    act.wait_ge(smax, r * 8 + 4 * c + 4)
                    s_.activation(prob_s[:, c, 0:S], pS[0:HQ, 2 * c:2 * c + 2, :].rearrange("p a b -> p (a b)"), ACT.Exp, bias=st_s[:, c, 2:3], accum_out=st_s[:, c, 3:4]).then_inc(sexp, 1)
                    s_.activation(prob_s[:, c, S:S + DQ], s_new[:, c], ACT.Exp, bias=st_s[:, c, 2:3], accum_out=st_s[:, c, 4:5]).then_inc(sexp, 1)

        @block.tensor
        def _(pe):
            t_ = nc.tensor
            pe.wait_ge(const_in, 16 * CONSTS)
            for g in range(12):
                arr, part = g // 3, g % 3
                if part == 0:
                    pe.wait_ge(lat_ready, (1, 1, 2, 3)[arr])
                if g >= 4:
                    pe.wait_ge(lat_ev, g - 3)
                for t in range(4 * part, min(4 * part + 4, NT)):
                    lo = (t - 4 * part) * P
                    src = cq[:, t, arr * P:(arr + 1) * P] if arr < 2 else ckv[:, t, :] if arr == 2 else krp[:, t, :]
                    rows = P if arr < 3 else 96
                    mm = t_.transpose(pS[0:rows, g % 4, lo:lo + P], src, ident[:])
                mm.then_inc(lat_T, 1)
            pe.wait_ge(lat_ev, 12)

            with pe.Fori(0, HEADS) as h:
                pe.wait_ge(w_ready, h * 48 + 48)
                pe.wait_ge(exp_done, h * 8)
                for g, (lo, w) in enumerate(QCH):
                    for k in range(2):
                        mm = t_.matmul(pS[:, g, 0:w], wq_h[:, k, :], cqT[:, k, lo:lo + w], start=k == 0, stop=k == 1)
                    mm.then_inc(pro_mm, 1)
                t_.matmul(pS[0:64, 3, :], wuk_h[:], ckvT[:, 0:512], start=True, stop=True).then_inc(pro_mm, 1)
                pe.wait_ge(pro_act, h * 6 + 1)
                pe.wait_ge(pro_dve, h * 5 + 1)
                t_.matmul(pS[0:64, 0, :], wuk_h[:], ckvT[:, 512:1024], start=True, stop=True).then_inc(pro_mm, 1)
                pe.wait_ge(pro_act, h * 6 + 2)
                pe.wait_ge(pro_dve, h * 5 + 2)
                for t in range(8):
                    mm = t_.matmul(pS[:, 1, t * VD:(t + 1) * VD], ckvT[:, t * P:(t + 1) * P], wuv[:, bass.ds(h * VD, VD)], start=True, stop=True)
                mm.then_inc(pro_mm, 1)
                pe.wait_ge(pro_act, h * 6 + 3)
                pe.wait_ge(pro_dve, h * 5 + 3)
                t_.matmul(pS[:, 2, 0:DB * DQ], wukT_h[:], qT[0:64, S:S + DB * DQ], start=True, stop=True).then_inc(pro_mm, 1)
                pe.wait_ge(pro_act, h * 6 + 6)
                pe.wait_ge(pro_dve, h * 5 + 5)

                def scores(i):
                    if i >= 2:
                        pe.wait_ge(exp_done, h * 8 + i - 1)
                    kw = (i + 1) * P
                    for c in range(0, kw, 512):
                        w = min(512, kw - c)
                        mm = t_.matmul(pS[:, 2 * (i % 2) + c // 512, 0:w], qT[0:96, i * P:(i + 1) * P], kT[0:96, c:c + w], start=True, stop=True)
                    mm.then_inc(s_done, 1)

                def turn(i):
                    pe.wait_ge(exp_done, h * 8 + i + 1)
                    for gi in groups(i):
                        pe.wait_ge(pt_dve if gi % 2 else pt_act, h * 6 + gi // 2)
                        b0 = 4 * (gi - groups(i)[0])
                        for b in range(gw(i, gi) // P):
                            mm = t_.transpose(pT_ps[:, gi % 2, b * P:(b + 1) * P], prob[:, i % 2, (b0 + b) * P:(b0 + b + 1) * P], ident[:])
                        mm.then_inc(pt_done, 1)

                def values(i):
                    if i == 0:
                        pe.wait_ge(o_ev, h)
                    for gi in groups(i):
                        pe.wait_ge(pt_dve if gi % 2 else pt_act, h * 6 + gi // 2 + 1)
                        b0 = 4 * (gi - groups(i)[0])
                        for b in range(gw(i, gi) // P):
                            mm = t_.matmul(pO[:, i * VD:(i + 1) * VD], pT[:, gi % 4, b * P:(b + 1) * P], v_h[:, b0 + b, :], start=b0 + b == 0, stop=b0 + b == i)
                    if i == 7:
                        mm.then_inc(o_done, 1)
                scores(0)
                scores(1)
                for i in range(8):
                    turn(i)
                    if i + 2 < 8:
                        scores(i + 2)
                    values(i)

            pe.wait_ge(exp_done, 64)
            pe.wait_ge(o_ev, 8)

            def sample_scores(b, c, r):
                pe.wait_ge(q_b, b * 3 + 3)
                if not isinstance(b, int) or b > 1:
                    pe.wait_ge(sexp, b * 2 - 2)
                pe.wait_ge(page_T_in[c], r * 256 + 256)
                for k in range(2):
                    out = pS[0:HQ, 2 * c + k, :]
                    t_.matmul(out, qlat_b[:, c], page_kvT[:, c, k * 512:(k + 1) * 512], start=True, stop=False)
                    t_.matmul(out, qrs_b[0:32, c], page_krT[0:32, c, k * 512:(k + 1) * 512], start=False, stop=True)
                out = s_new_ps[c]
                t_.matmul(out, qlat_b[:, c], ckvT[:, bass.ds(b * DQ + S, DQ)], start=True, stop=False)
                t_.matmul(out, qrs_b[0:32, c], krs_b[0:32, c], start=False, stop=True).then_inc(ss_done, 1)

            def sample_values(b, c, r):
                pe.wait_ge(snorm, b * 3 + 3)
                pe.sem_inc(passed, 1)
                for j in range(8):
                    t_.transpose(pT_ps[:, 0, j * HQ:(j + 1) * HQ], prob_s[:, c, j * P:(j + 1) * P], ident[0:HQ, 0:HQ])
                t_.transpose(pT_ps[0:DQ, 0, 8 * HQ:9 * HQ], prob_s[:, c, S:S + DQ], ident[0:HQ, 0:HQ]).then_inc(st_done, 1)
                pe.wait_ge(st_ev, b * 2 + 2)
                pe.wait_ge(ol_ev, b)
                pe.wait_ge(page_in[c], r * 144 + 144)
                for j in range(8):
                    t_.matmul(pO[:, 0:HQ], page_kv[:, c, j, :], pTs[:, j * HQ:(j + 1) * HQ], start=j == 0, stop=False)
                t_.matmul(pO[:, 0:HQ], new_kv[:, c, :], pTs[0:DQ, 8 * HQ:9 * HQ], start=False, stop=True).then_inc(ol_done, 1)
            sample_scores(0, 0, 0)
            sample_scores(1, 1, 0)
            sample_values(0, 0, 0)
            with pe.Fori(1, DB // 2) as r:
                sample_scores(r * 2, 0, r)
                sample_values(r * 2 - 1, 1, r - 1)
                sample_scores(r * 2 + 1, 1, r)
                sample_values(r * 2, 0, r)
            sample_values(DB - 1, 1, DB // 2 - 1)

            pe.wait_ge(ol_ev, DB)
            pe.wait_ge(sexp, 2 * DB)
            for h in range(HEADS):
                mm = t_.matmul(pS[0:DB * DQ, 0, h * VD:(h + 1) * VD], olat[:, h].rearrange("p b q -> p (b q)"), wuv[:, h * VD:(h + 1) * VD], start=True, stop=True)
            mm.then_inc(os_done, 1)


def retention(nc, passed, x_sb, gw_sb, gw_in, a, proj, retn, out_ret_p, out_ret_s):
    with ExitStack() as ctx:
        sb = lambda n, s, d=F32: ctx.enter_context(nc.sbuf_tensor("r_" + n, s, d))
        sem = lambda n: nc.alloc_semaphore("r_" + n)
        NS = DB * DQ
        ident = sb("ident", [P, P])
        raw_q = sb("raw_q", [P, NT, 512])
        raw_k = sb("raw_k", [P, NT, 512])
        raw_v = sb("raw_v", [P, NT, 512])
        rot = sb("rot", [P, 2, NT, 64])
        dmask = sb("dmask", [P, P])
        dmask_s = sb("dmask_s", [NS, NS])
        qdec = sb("qdec", [P, TOK])
        cols = sb("cols", [P, 11])
        st_in = sb("st_in", [P, DB, P])
        st_out = sb("st_out", [P, DB, P])
        tq = sb("tq", [P, 2, NT, 64])
        tk = sb("tk", [P, 2, NT, 64])
        qr = sb("qr", [P, NT, P])
        kr = sb("kr", [P, NT, P])
        kd = sb("kd", [P, 8, P])
        kds = sb("kds", [NS, DB, P])
        v_s = sb("v_s", [NS, P])
        qT = sb("qT", [P, TOK])
        kT = sb("kT", [P, TOK])
        qd = sb("qd", [P, TOK])
        attT = sb("attT", [P, 8, P])
        attT_s = sb("attT_s", [NS, NS])
        state = sb("state", [P, 9, P])
        oT_s = sb("oT_s", [P, NS])
        bst = sb("bst", [P, NT, 6])
        mv = sb("mv", [P, NT, 2])
        vare = sb("vare", [P, NT])
        mhalf = sb("mhalf", [P, NT])
        rstd = sb("rstd", [P, NT])
        nbias = sb("nbias", [P, NT])
        on = sb("on", [P, NT, P])
        g_out = sb("g_out", [P, 2, 3, FW])
        g_mm, g_ev, sto_ok = sem("g_mm"), sem("g_ev"), sem("sto_ok")
        g_stored = [sem(f"g_stored{c}") for c in range(2)]
        ps = [ctx.enter_context(nc.psum_tensor(f"r_ps{i}", [P, 512], F32)) for i in range(8)]
        const_in, rq_in, rk_in, rv_in, head_in, pl, dv, q_rot, k_rot, k_dec, turned, ev, qd_ok, att_mm, att_ok, kv_mm, kv_ok, o_mm, \
            os_mm, os_ev, os_T, var_ok, rstd_ok, nb_ok, norm_ok, out_s, state_out = [sem(n) for n in (
                "const_in rq_in rk_in rv_in head_in pl dv q_rot k_rot k_dec turned ev qd_ok att_mm att_ok kv_mm kv_ok o_mm "
                "os_mm os_ev os_T var_ok rstd_ok nb_ok norm_ok out_s state_out").split()]
        block = ctx.enter_context(nc.Block())
        pv = proj.rearrange("(t p) n -> p t n", p=P)
        rn = retn.rearrange("(t p) n -> p t n", p=P)
        R0 = QL + KVL + ROPE
        G0 = R0 + 3 * 512
        UNITS = 2 * NT
        CUT = (4, 6, 8, 9, 11, 13)

        @block.sync
        def _(sp):
            def head_consts(h):
                one = slice(h, h + 1) if isinstance(h, int) else bass.ds(h, 1)
                sp.dma_start(dmask[:], a["dmask"][one].rearrange("a p n -> p (a n)")).then_inc(head_in, 16)
                sp.dma_start(dmask_s[:], a["dmask_s"][one].rearrange("a p n -> p (a n)")).then_inc(head_in, 16)
                sp.dma_start(qdec[:], a["qdec"][one].rearrange("a p n -> p (a n)")).then_inc(head_in, 16)
                sp.dma_start(cols[:], a["ret_cols"][one].rearrange("a p n -> p (a n)")).then_inc(head_in, 16)
                sp.dma_start(st_in[:], a["state_ret"][:, one].rearrange("b a d v -> d b (a v)")).then_inc(head_in, 16)

            wv = a["w_in"].rearrange("(k p) n -> p k n", p=P)

            def gate_weights(q, at):
                at = slice(at, at + FW) if isinstance(at, int) else bass.ds(at, FW)
                sp.dma_start(gw_sb[:, q], wv[:, :, at]).then_inc(gw_in[q], 16)
            sp.dma_start(rot[:], a["rope64"].rearrange("s (t p) c -> p s t c", p=P)).then_inc(const_in, 16)
            sp.dma_start(ident[:], a["ident"]).then_inc(const_in, 16)
            for i, (x, ready) in enumerate(((raw_q, rq_in), (raw_k, rk_in), (raw_v, rv_in))):
                sp.dma_start(x[:], pv[:, :, R0 + 512 * i:R0 + 512 * (i + 1)]).then_inc(ready, 16)
                if i == 1:
                    head_consts(0)

            def stores(h, kv_n, st_n, norm_n, hc):
                sp.wait_ge(kv_ok, kv_n)
                sp.sem_inc(passed, 1)
                sp.wait_ge(sto_ok, st_n)
                sp.sem_inc(passed, 1)
                sp.dma_start(out_ret_p[bass.ds(h, 1)].rearrange("a d v -> d (a v)"), state[:, 8, :]).then_inc(state_out, 16)
                sp.dma_start(out_ret_s[:, bass.ds(h, 1)].rearrange("b a d v -> d b (a v)"), st_out[:]).then_inc(state_out, 16)
                sp.wait_ge(norm_ok, norm_n)
                sp.sem_inc(passed, 1)
                sp.dma_start(rn[:, :, bass.ds(hc, P)], on[:]).then_inc(out_s, 16)
            with sp.Fori(0, 3) as h:
                nxt, n8, n9, hc = sp.snap(h + 1), sp.snap(h * 8 + 8), sp.snap(h * 9 + 9), sp.snap(h * P)
                half, full = sp.snap(h * UNITS + 9), sp.snap(h * UNITS + UNITS)
                at = [sp.snap(h * (2 * FW) + (G0 + (2 + q) * FW)) for q in range(2)]
                sp.wait_ge(g_mm, half)
                sp.sem_inc(passed, 1)
                gate_weights(0, at[0])
                stores(h, n8, nxt, n9, hc)
                head_consts(nxt)
                sp.wait_ge(g_mm, full)
                sp.sem_inc(passed, 1)
                gate_weights(1, at[1])
            stores(3, 32, 4, 36, 3 * P)
            sp.wait_ge(state_out, 128)
            sp.wait_ge(out_s, 64)

        @block.gpsimd
        def _(pool):
            pool.memset(mhalf[:], -0.5).then_inc(pl, 1)
            pool.memset(on[:, 8, :], 0.0).then_inc(pl, 1)
            pool.memset(mv[:], 1.0).then_inc(pl, 1)
            pool.wait_ge(const_in, 32)
            pool.wait_ge(rk_in, 16)
            pool.wait_ge(pl, 3)
            cos, sin = rot[:, 0], rot[:, 1]
            with pool.Fori(0, 4) as h:
                x1, x2 = raw_k[:, :, bass.ds(h * P, 64)], raw_k[:, :, bass.ds(h * P + 64, 64)]
                g = nc.gpsimd
                g.tensor_tensor(tk[:, 0], x1, cos, ALU.mult).then_inc(k_rot, 1)
                g.tensor_tensor(tk[:, 1], x2, sin, ALU.mult).then_inc(k_rot, 1)
                pool.wait_ge(k_rot, h * 6 + 2)
                g.tensor_tensor(kr[:, :, 0:64], tk[:, 0], tk[:, 1], ALU.subtract).then_inc(k_rot, 1)
                pool.wait_ge(k_rot, h * 6 + 3)
                pool.sem_inc(passed, 1)
                g.tensor_tensor(tk[:, 0], x2, cos, ALU.mult).then_inc(k_rot, 1)
                g.tensor_tensor(tk[:, 1], x1, sin, ALU.mult).then_inc(k_rot, 1)
                pool.wait_ge(k_rot, h * 6 + 5)
                g.tensor_tensor(kr[:, :, 64:P], tk[:, 0], tk[:, 1], ALU.add).then_inc(k_rot, 1)
                pool.wait_ge(k_rot, h * 6 + 6)
                pool.sem_inc(passed, 1)
                pool.wait_ge(head_in, h * 80 + 80)
                pool.sem_inc(passed, 1)
                pool.wait_ge(rv_in, 16)
                g.tensor_scalar(kd[:], kr[:, 0:8, :], cols[:, 0:1], None, ALU.mult).then_inc(k_dec, 1)
                for b in range(DB):
                    g.tensor_scalar(kds[:, b, :], kr[0:NS, 8, :], cols[0:NS, 1 + b:2 + b], None, ALU.mult).then_inc(k_dec, 1)
                g.tensor_copy(v_s[:], raw_v[0:NS, 8, bass.ds(h * P, P)]).then_inc(k_dec, 1)
                pool.wait_ge(var_ok, h + 1)
                g.tensor_tensor(rstd[:], vare[:], mhalf[:], ALU.pow).then_inc(rstd_ok, 1)

        @block.vector
        def _(dve):
            v = nc.vector
            dve.wait_ge(const_in, 32)
            dve.wait_ge(rq_in, 16)
            dve.wait_ge(pl, 3)
            cos, sin = rot[:, 0], rot[:, 1]
            with dve.Fori(0, 4) as h:
                x1, x2 = raw_q[:, :, bass.ds(h * P, 64)], raw_q[:, :, bass.ds(h * P + 64, 64)]
                v.tensor_tensor(tq[:, 0], x1, cos, ALU.mult).then_inc(q_rot, 1)
                v.tensor_tensor(tq[:, 1], x2, sin, ALU.mult).then_inc(q_rot, 1)
                dve.wait_ge(q_rot, h * 6 + 2)
                v.tensor_tensor(qr[:, :, 0:64], tq[:, 0], tq[:, 1], ALU.subtract).then_inc(q_rot, 1)
                dve.wait_ge(q_rot, h * 6 + 3)
                v.tensor_tensor(tq[:, 0], x2, cos, ALU.mult).then_inc(q_rot, 1)
                v.tensor_tensor(tq[:, 1], x1, sin, ALU.mult).then_inc(q_rot, 1)
                dve.wait_ge(q_rot, h * 6 + 5)
                v.tensor_tensor(qr[:, :, 64:P], tq[:, 0], tq[:, 1], ALU.add).then_inc(q_rot, 1)
                dve.wait_ge(head_in, h * 80 + 80)
                dve.wait_ge(ev, h * 6 + 3)
                v.tensor_tensor(qd[:], qT[:], qdec[:], ALU.mult).then_inc(qd_ok, 1)
                for g in range(2):
                    dve.wait_ge(att_mm, h * 3 + g + 1)
                    v.tensor_tensor(attT[:, 4 * g:4 * g + 4, :], ps[2 + g][:].rearrange("p (c n) -> p c n", n=P), dmask[:].unsqueeze(1).broadcast_to([P, 4, P]), ALU.mult).then_inc(att_ok, 1)
                dve.wait_ge(att_mm, h * 3 + 3)
                v.tensor_tensor(attT_s[:], ps[4][0:NS, 0:NS], dmask_s[:], ALU.mult).then_inc(att_ok, 1)
                dve.wait_ge(state_out, h * 32)
                for n in range(8):
                    if n % 4 == 0:
                        dve.wait_ge(kv_mm, h * 4 + (1, 4)[n // 4])
                    kv = ps[5][:, (n % 4) * P:(n % 4 + 1) * P]
                    if n == 0:
                        v.tensor_copy(state[:, 1, :], kv).then_inc(kv_ok, 1)
                    else:
                        dve.wait_ge(kv_ok, h * 8 + n)
                        v.scalar_tensor_tensor(state[:, n + 1, :], state[:, n, :], cols[:, 9:10], kv, ALU.mult, ALU.add).then_inc(kv_ok, 1)
                    if n == 3:
                        for g in range(2):
                            dve.wait_ge(kv_mm, h * 4 + 2 + g)
                            ins = v.scalar_tensor_tensor(st_out[:, 4 * g:4 * g + 4, :].rearrange("p b n -> p (b n)"), st_in[:, 4 * g:4 * g + 4, :].rearrange("p b n -> p (b n)"), cols[:, 10:11], ps[g][:], ALU.mult, ALU.add)
                        ins.then_inc(sto_ok, 1)
                dve.wait_ge(os_mm, h + 1)
                v.tensor_copy(oT_s[:], ps[4][:, 64:64 + NS]).then_inc(os_ev, 1)
                for n in range(NT):
                    if n < 8:
                        if n % 4 == 0:
                            dve.wait_ge(o_mm, h * 2 + n // 4 + 1)
                        v.bn_stats(bst[:, n, :], ps[2 + n // 4][:, (n % 4) * P:(n % 4 + 1) * P]).then_inc(dv, 1)
                    else:
                        dve.wait_ge(os_T, h + 1)
                        v.bn_stats(bst[0:NS, n, :], ps[4][0:NS, P:2 * P]).then_inc(dv, 1)
                for n in range(NT):
                    rows = P if n < 8 else NS
                    dve.wait_ge(dv, h * 18 + n + 1)
                    dve.sem_inc(passed, 1)
                    v.bn_aggr(mv[0:rows, n, :], bst[0:rows, n, :]).then_inc(dv, 1)
                dve.wait_ge(dv, h * 18 + 18)
                v.tensor_scalar(vare[:], mv[:, :, 1], LN_EPS, None, ALU.add).then_inc(var_ok, 1)
                dve.wait_ge(rstd_ok, h + 1)
                v.scalar_tensor_tensor(nbias[:], mv[:, :, 0], -1.0, rstd[:], ALU.mult, ALU.mult).then_inc(nb_ok, 1)

        @block.scalar
        def _(act):
            s_ = nc.scalar
            act.sem_inc(g_ev, 1)
            with act.Fori(0, 4) as h:
                g_at = [act.snap(h * (2 * FW) + (G0 + q * FW)) for q in range(2)]
                g_done = [act.snap(h * UNITS + (3 * g + 4)) for g in range(6)]

                def gates(lo, hi):
                    for u in range(lo, hi):
                        g, i = u // 3, u % 3
                        if i == 0:
                            act.wait_ge(g_stored[g % 2], h * 48 + 16 * (g // 2))
                        act.wait_ge(g_mm, h * UNITS + u + 1)
                        s_.copy(g_out[:, g % 2, i, :], ps[6 + u % 2][:, 0:FW]).then_inc(g_ev, 1)
                        if i == 2:
                            act.wait_ge(g_ev, g_done[g])
                            act.sem_inc(passed, 1)
                            act.dma_start(pv[:, 3 * (g % 3):3 * (g % 3) + 3, bass.ds(g_at[g // 3], FW)], g_out[:, g % 2]).then_inc(g_stored[g % 2], 16)
                gates(0, CUT[0])
                for g in range(6):
                    dst, part = (qT, kT)[g // 3], g % 3
                    w = 512 if part < 2 else P
                    act.wait_ge(turned, h * 6 + g + 1)
                    s_.copy(dst[:, part * 512:part * 512 + w], ps[g % 2][:, 0:w]).then_inc(ev, 1)
                gates(CUT[0], CUT[5])
                act.wait_ge(nb_ok, h + 1)
                act.wait_ge(out_s, h * 16)
                for n in range(NT):
                    rows = P if n < 8 else NS
                    src = ps[2 + n // 4][:, (n % 4) * P:(n % 4 + 1) * P] if n < 8 else ps[4][0:NS, P:2 * P]
                    s_.activation(on[0:rows, n, :], src, ACT.Identity, bias=nbias[0:rows, n:n + 1], scale=rstd[0:rows, n:n + 1]).then_inc(norm_ok, 1)
                gates(CUT[5], UNITS)
            for c in range(2):
                act.wait_ge(g_stored[c], 4 * 48)

        @block.tensor
        def _(pe):
            t_ = nc.tensor
            with pe.Fori(0, 4) as h:
                def gates(lo, hi):
                    for u in range(lo, hi):
                        q, t = u // NT, u % NT
                        if t == 0:
                            pe.wait_ge(gw_in[q], h * 16 + 16)
                        pe.wait_ge(g_ev, h * UNITS + u)
                        for k in range(KD):
                            mm = t_.matmul(ps[6 + u % 2][:, 0:FW], x_sb[:, k, t * P:(t + 1) * P], gw_sb[:, q, k, :], start=k == 0, stop=k == KD - 1)
                        mm.then_inc(g_mm, 1)
                gates(0, CUT[0])
                for g in range(6):
                    src, part = (qr, kr)[g // 3], g % 3
                    if g == 0:
                        pe.wait_ge(const_in, 32)
                        pe.wait_ge(q_rot, h * 6 + 6)
                        pe.wait_ge(norm_ok, h * 9)
                    if g == 3:
                        pe.wait_ge(k_rot, h * 6 + 6)
                    if g >= 2:
                        pe.wait_ge(ev, h * 6 + g - 1)
                    for t in range(4 * part, min(4 * part + 4, NT)):
                        mm = t_.transpose(ps[g % 2][:, (t - 4 * part) * P:(t - 4 * part + 1) * P], src[:, t, :], ident[:])
                    mm.then_inc(turned, 1)
                gates(CUT[0], CUT[1])

                def keys_values(g):
                    for c in range(4):
                        n = 4 * g + c
                        mm = t_.matmul(ps[5][:, c * P:(c + 1) * P], kd[:, n, :], raw_v[:, n, bass.ds(h * P, P)], start=True, stop=True)
                    mm.then_inc(kv_mm, 1)
                pe.wait_ge(k_dec, h * 10 + 10)
                keys_values(0)
                pe.wait_ge(ev, h * 6 + 6)
                for g in range(2):
                    for c in range(4):
                        at = slice((4 * g + c) * P, (4 * g + c + 1) * P)
                        mm = t_.matmul(ps[2 + g][:, c * P:(c + 1) * P], kT[:, at], qT[:, at], start=True, stop=True)
                    mm.then_inc(att_mm, 1)
                t_.matmul(ps[4][0:NS, 0:NS], kT[:, S:S + NS], qT[:, S:S + NS], start=True, stop=True).then_inc(att_mm, 1)
                for g in range(2):
                    for c in range(4):
                        mm = t_.matmul(ps[g][:, c * P:(c + 1) * P], kds[:, 4 * g + c, :], raw_v[0:NS, 8, bass.ds(h * P, P)], start=True, stop=True)
                    mm.then_inc(kv_mm, 1)
                gates(CUT[1], CUT[2])
                pe.wait_ge(att_ok, h * 3 + 3)
                pe.wait_ge(qd_ok, h + 1)
                for b in range(DB):
                    out = ps[4][:, 64 + DQ * b:64 + DQ * (b + 1)]
                    t_.matmul(out, st_in[:, b, :], qd[:, S + DQ * b:S + DQ * (b + 1)], start=True, stop=False)
                    mm = t_.matmul(out, v_s[:], attT_s[:, DQ * b:DQ * (b + 1)], start=False, stop=True)
                mm.then_inc(os_mm, 1)

                def outputs(g):
                    for n in range(4 * g, 4 * g + 4):
                        if n:
                            pe.wait_ge(kv_ok, h * 8 + n)
                        out = ps[2 + g][:, (n % 4) * P:(n % 4 + 1) * P]
                        mm = t_.matmul(out, attT[:, n, :], raw_v[:, n, bass.ds(h * P, P)], start=True, stop=n == 0)
                        if n:
                            mm = t_.matmul(out, qd[:, n * P:(n + 1) * P], state[:, n, :], start=False, stop=True)
                    mm.then_inc(o_mm, 1)
                outputs(0)
                gates(CUT[2], CUT[3])
                pe.wait_ge(kv_ok, h * 8 + 4)
                keys_values(1)
                gates(CUT[3], CUT[4])
                outputs(1)
                pe.wait_ge(os_ev, h + 1)
                pe.sem_inc(passed, 1)
                t_.transpose(ps[4][0:NS, P:2 * P], oT_s[:], ident[:]).then_inc(os_T, 1)
                gates(CUT[4], UNITS)


def merge(nc, passed, a, proj, o_mla, retn, h_perm, base, tok_list, meta):
    with ExitStack() as ctx:
        sb = lambda n, s, d=F32: ctx.enter_context(nc.sbuf_tensor("m_" + n, s, d))
        sem = lambda n: ctx.enter_context(nc.semaphore("m_" + n))
        ident = sb("ident", [P, P])
        w_mo = sb("w_mo", [P, 4, D])
        w_ro = sb("w_ro", [P, 4, D])
        w_o = sb("w_o", [P, KD, D])
        w_gu = sb("w_gu", [P, KD, 512])
        w_sd = sb("w_sd", [P, 2, D])
        w_r = sb("w_r", [P, KD, NE])
        gn_g = sb("gn_g", [P, 512])
        g1 = sb("g1", [P, D])
        b1 = sb("b1", [P, D])
        gates = sb("gates", [P, 2560])
        o_in = sb("o_in", [P, 512])
        ret = sb("ret", [P, 512])
        srg = sb("srg", [P, 512])
        x_in = sb("x_in", [P, D])
        sg = sb("sg", [P, 2048])
        oT = sb("oT", [P, KD, P])
        mix = sb("mix", [P, D])
        tmp = sb("tmp", [P, D])
        mT = sb("mT", [P, KD, P])
        z = sb("z", [P, D])
        hp = sb("hp", [P, D])
        hT = sb("hT", [P, KD, P])
        sgg = sb("sgg", [P, 256])
        act_s = sb("act_s", [P, 256])
        aT = sb("aT", [P, 2, P])
        base_sb = sb("base_sb", [P, D])
        bst = sb("bst", [P, 2, 6])
        mv = sb("mv", [P, 2])
        col = sb("col", [P, 4])
        bias = sb("bias", [P, NE])
        tri = sb("tri", [P, P])
        ones = sb("ones", [P, P])
        iota = sb("iota", [P, NE + 1])
        ebase = sb("ebase", [P, NE])
        pid = sb("pid", [P, 1])
        valid = sb("valid", [P, NT])
        dump = sb("dump", [P, NT, TOPK])
        tid = sb("tid", [P, NT], U32)
        sc = sb("sc", [P, NE])
        sel = sb("sel", [P, NE])
        top2 = sb("top2", [P, 8, 8])
        gs = sb("gs", [P, 8])
        m8 = sb("m8", [P, 8])
        i8 = sb("i8", [P, 8], U32)
        f8 = sb("f8", [P, 8])
        gm = sb("gm", [P, 8])
        oh = sb("oh", [P, TOPK, NE])
        prod = sb("prod", [P, TOPK, NE])
        cnt = sb("cnt", [P, NE])
        carry = sb("carry", [P, NE])
        rank = sb("rank", [P, NE])
        w6 = sb("w6", [P, TOPK])
        wsum = sb("wsum", [P, 2])
        slot = sb("slot", [P, TOPK])
        slot_c = sb("slot_c", [P, TOPK], U32)
        entry = sb("entry", [P, TOPK, 2], U32)
        nb_i = sb("nb_i", [P, NE], I32)
        pre = sb("pre", [P, 2, NE + 1])
        eqk = sb("eqk", [P, NE])
        bt = sb("bt", [P, 8])
        meta_i = sb("meta_i", [P, 2], I32)
        nblk_i = sb("nblk_i", [P, 1], I32)

        T = [ctx.enter_context(nc.psum_tensor(f"m_T{i}", [P, 512], F32)) for i in range(2)]
        Y = ctx.enter_context(nc.psum_tensor("m_Y", [P, 4, 512], F32))
        GU = ctx.enter_context(nc.psum_tensor("m_GU", [P, 512], F32))
        R = ctx.enter_context(nc.psum_tensor("m_R", [P, 512], F32))
        (mo_in, ro_in, wo_in, id_in, w_in_s, c_in, gates_in, o_in_s, ret_in, x_in_s, pl, sig_ok, ret_ok, turned, tev, y_done, m_ok, w_done, z_ok,
         st, var_ok, rstd_ok, zn_ok, hg, h_ok, h_out, gu_done, sgg_ok, a1_ok, act_ok, r_done, sc_ok, p_done,
         rank_ok, d_done, base_ok, base_out, slot_ok, listed, rt, t12, t12b, filled, bk, meta_out) = [sem(n) for n in (
            "mo_in ro_in wo_in id_in w_in_s c_in gates_in o_in_s ret_in x_in_s pl sig_ok ret_ok turned tev y_done m_ok w_done z_ok "
            "st var_ok rstd_ok zn_ok hg h_ok h_out gu_done sgg_ok a1_ok act_ok r_done sc_ok p_done "
            "rank_ok d_done base_ok base_out slot_ok listed rt t12 t12b filled bk meta_out").split()]
        block = ctx.enter_context(nc.Block())
        G0 = QL + KVL + ROPE + 3 * 512
        NCONST = 12

        def rows(t, dram):
            return dram[t * P:(t + 1) * P, :] if isinstance(t, int) else dram[bass.ds(t * P, P), :]

        def wait_alone(eng, s, value):
            eng.wait_ge(s, value)
            eng.sem_inc(passed, 1)

        @block.sync
        def _(sp):
            def loads(t):
                n = [t, t, t, t] if isinstance(t, int) else [sp.snap(t) for _ in range(4)]
                r0 = t * P if isinstance(t, int) else sp.snap(t * P)
                t3 = t * 3 if isinstance(t, int) else sp.snap(t * 3)
                turned_o, turned_r = (t * 2 - 1, t * 2) if isinstance(t, int) else (sp.snap(t * 2 - 1), sp.snap(t * 2))
                later = not isinstance(t, int) or t > 0
                at = bass.ds(r0, P)
                if later:
                    wait_alone(sp, sig_ok, n[0])
                    wait_alone(sp, ret_ok, t3)
                sp.dma_start(gates[:], proj[at, G0:G0 + GATE_W]).then_inc(gates_in, 16)
                if later:
                    wait_alone(sp, y_done, turned_o)
                sp.dma_start(o_in[:], o_mla[at, :]).then_inc(o_in_s, 16)
                if later:
                    wait_alone(sp, y_done, turned_r)
                sp.dma_start(ret[:], retn[at, :]).then_inc(ret_in, 16)
                if later:
                    wait_alone(sp, z_ok, n[0])
                sp.dma_start(x_in[:], a["x"][at, :]).then_inc(x_in_s, 16)

            loads(0)
            sp.dma_start(ident[:], a["ident"]).then_inc(id_in, 16)
            sp.dma_start(w_mo[:], a["w_mla_o"].rearrange("(k p) n -> p k n", p=P)).then_inc(mo_in, 16)
            for dst, src in ((gn_g[:], a["ret_gn_g"].partition_broadcast(P)), (g1[:], a["ln1_g"].partition_broadcast(P)),
                             (b1[:], a["ln1_b"].partition_broadcast(P)), (bias[:], a["router_bias"].partition_broadcast(P)),
                             (tri[:], a["tri"]), (iota[:], a["iota"]), (ebase[:], a["ebase"]), (pid[:], a["pid"]),
                             (valid[:], a["valid"]), (dump[:], a["dump"]), (tid[:], a["tid"]), (ones[:], a["ones"])):
                sp.dma_start(dst, src).then_inc(c_in, 16)
            for dst, src, ready in ((w_ro[:], a["w_ret_o"].rearrange("(k p) n -> p k n", p=P), ro_in),
                                    (w_o[:], a["w_out"].rearrange("(k p) n -> p k n", p=P), wo_in),
                                    (w_gu[:, :, 0:256], a["w_sh_gate"].rearrange("(p k) n -> p k n", p=P), w_in_s),
                                    (w_gu[:, :, 256:512], a["w_sh_up"].rearrange("(p k) n -> p k n", p=P), w_in_s),
                                    (w_sd[:], a["w_sh_down"].rearrange("(k p) n -> p k n", p=P), w_in_s),
                                    (w_r[:], a["w_router"].rearrange("(p k) n -> p k n", p=P), w_in_s)):
                sp.dma_start(dst, src).then_inc(ready, 16)
            loads(1)
            with sp.Fori(2, NT) as t:
                loads(t)
            sp.wait_ge(bk, BK_STEPS)
            sp.dma_start(meta[0:P, :], meta_i[:]).then_inc(meta_out, 16)
            sp.dma_start(meta[P:P + 1, 0:1], nblk_i[0:1, :]).then_inc(meta_out, 16)
            sp.wait_ge(meta_out, 32)

        @block.gpsimd
        def _(pool):
            g = nc.gpsimd
            g.memset(col[:, 3:4], -0.5).then_inc(pl, 1)
            g.memset(carry[:], 0.0).then_inc(pl, 1)
            pool.wait_ge(c_in, 16 * NCONST)

            def branch(t):
                pool.wait_ge(sig_ok, t + 1)
                pool.wait_ge(ret_in, t * 16 + 16)
                g.tensor_tensor(srg[:], srg[:], gates[:, 0:512], ALU.mult).then_inc(ret_ok, 1)
                g.tensor_tensor(ret[:], ret[:], gn_g[:], ALU.mult).then_inc(ret_ok, 1)
                pool.wait_ge(ret_ok, t * 3 + 2)
                g.tensor_tensor(ret[:], ret[:], srg[:], ALU.mult).then_inc(ret_ok, 1)

            def norm(t):
                pool.wait_ge(var_ok, t + 1)
                g.tensor_tensor(col[:, 1:2], col[:, 0:1], col[:, 3:4], ALU.pow).then_inc(rstd_ok, 1)
                pool.wait_ge(zn_ok, t + 1)
                g.tensor_tensor(z[:], z[:], g1[:], ALU.mult).then_inc(hg, 1)
                pool.wait_ge(hg, t + 1)
                pool.wait_ge(h_out, t * 16)
                pool.wait_ge(base_ok, t)
                g.tensor_tensor(hp[:].rearrange("p (k q) -> p q k", k=KD), z[:].rearrange("p (q k) -> p q k", k=KD), b1[:].rearrange("p (q k) -> p q k", k=KD), ALU.add).then_inc(h_ok, 1)
                wait_alone(pool, h_ok, t + 1)
                pool.dma_start(rows(t, h_perm), hp[:]).then_inc(h_out, 16)

            def scatter(t):
                wait_alone(pool, slot_ok, t + 1)
                for k in range(TOPK):
                    idx = slot_c[:, k:k + 1]
                    g.indirect_dma_start(tok_list, bass.IndirectOffsetOnAxis(ap=idx, axis=0), entry[:, k, :], None).then_inc(listed, 16)

            branch(0)
            pool.dma_start(tok_list, a["list_fill"]).then_inc(filled, 16)
            pool.dma_start(h_perm[TOK:TOK + P, :], a["zero_rows"]).then_inc(filled, 16)
            pool.dma_start(base[TOK:TOK + P, :], a["zero_rows"]).then_inc(filled, 16)
            branch(1)
            norm(0)
            pool.wait_ge(filled, 48)
            with pool.Fori(1, NT - 1) as t:
                branch(t + 1)
                norm(t)
                scatter(t - 1)
            norm(NT - 1)
            scatter(NT - 2)
            scatter(NT - 1)
            pool.wait_ge(listed, 16 * TOPK * NT)
            pool.wait_ge(h_out, 16 * NT)

        @block.scalar
        def _(act):
            s_ = nc.scalar

            def sigmoids(t):
                act.wait_ge(gates_in, t * 16 + 16)
                act.wait_ge(ret_ok, t * 3)
                act.wait_ge(m_ok, t)
                s_.activation(srg[:], gates[:, 0:512], ACT.Sigmoid).then_inc(t12, 1)
                s_.activation(sg[:], gates[:, 512:2560], ACT.Sigmoid).then_inc(sig_ok, 1)

            def evac(dst, bank, n):
                act.wait_ge(turned, n + 1)
                s_.copy(dst, T[bank][:, 0:dst.free_size()]).then_inc(tev, 1)

            def body(t, first=False, last=False):
                n0 = 0 if first else t * 7 - 3
                evac(oT[:, 0:4, :].rearrange("p k n -> p (k n)"), 0, n0)
                evac(oT[:, 4:8, :].rearrange("p k n -> p (k n)"), 1, n0 + 1)
                if not first:
                    evac(hT[:, 0:4, :].rearrange("p k n -> p (k n)"), 0, n0 + 2)
                    evac(hT[:, 4:8, :].rearrange("p k n -> p (k n)"), 1, n0 + 3)
                    act.wait_ge(gu_done, t)
                    s_.activation(sgg[:], GU[:, 0:256], ACT.Sigmoid).then_inc(sgg_ok, 1)
                nm = n0 + (2 if first else 4)
                evac(mT[:, 0:4, :].rearrange("p k n -> p (k n)"), 0, nm)
                evac(mT[:, 4:8, :].rearrange("p k n -> p (k n)"), 1, nm + 1)
                if not first:
                    act.wait_ge(r_done, t)
                    act.wait_ge(rank_ok, t - 1)
                    s_.activation(sc[:], R[:, 0:NE], ACT.Sigmoid).then_inc(sc_ok, 1)
                if not last:
                    sigmoids(t + 1)
                if not first:
                    evac(aT[:].rearrange("p k n -> p (k n)"), 0, n0 + 6)
                    wait_alone(act, base_ok, t)
                    act.dma_start(rows(t - 1, base), base_sb[:]).then_inc(base_out, 16)
            sigmoids(0)
            body(0, first=True)
            with act.Fori(1, NT - 1) as t:
                body(t)
            body(NT - 1, last=True)
            n0 = NT * 7 - 3
            evac(hT[:, 0:4, :].rearrange("p k n -> p (k n)"), 0, n0)
            evac(hT[:, 4:8, :].rearrange("p k n -> p (k n)"), 1, n0 + 1)
            act.wait_ge(gu_done, NT)
            s_.activation(sgg[:], GU[:, 0:256], ACT.Sigmoid).then_inc(sgg_ok, 1)
            act.wait_ge(r_done, NT)
            act.wait_ge(rank_ok, NT - 1)
            s_.activation(sc[:], R[:, 0:NE], ACT.Sigmoid).then_inc(sc_ok, 1)
            evac(aT[:].rearrange("p k n -> p (k n)"), 0, n0 + 2)
            act.wait_ge(base_ok, NT)
            act.dma_start(rows(NT - 1, base), base_sb[:]).then_inc(base_out, 16)
            act.wait_ge(base_out, 16 * NT)

        @block.vector
        def _(dve):
            v = nc.vector

            def mixing(t):
                dve.wait_ge(y_done, t * 2 + 1)
                dve.wait_ge(sig_ok, t + 1)
                v.tensor_tensor(mix[:], sg[:, 0:D], Y[:, 0:2, :].rearrange("p a b -> p (a b)"), ALU.mult).then_inc(t12b, 1)
                dve.wait_ge(y_done, t * 2 + 2)
                v.tensor_tensor(tmp[:], sg[:, D:2 * D], Y[:, 2:4, :].rearrange("p a b -> p (a b)"), ALU.mult).then_inc(t12b, 1)
                dve.wait_ge(t12b, t * 2 + 2)
                v.tensor_tensor(mix[:], mix[:], tmp[:], ALU.add).then_inc(m_ok, 1)

            def shared_act(u):
                dve.wait_ge(sgg_ok, u + 1)
                v.tensor_tensor(act_s[:], sgg[:], GU[:, 0:256], ALU.mult).then_inc(a1_ok, 1)
                dve.wait_ge(a1_ok, u + 1)
                v.tensor_tensor(act_s[:], act_s[:], GU[:, 256:512], ALU.mult).then_inc(act_ok, 1)

            def layer_norm_1(t):
                dve.wait_ge(w_done, t + 1)
                dve.wait_ge(x_in_s, t * 16 + 16)
                dve.wait_ge(h_ok, t)
                v.scalar_tensor_tensor(z[:], x_in[:], ALPHA, Y[:, 0:2, :].rearrange("p a b -> p (a b)"), ALU.mult, ALU.add).then_inc(z_ok, 1)
                dve.wait_ge(z_ok, t + 1)
                v.bn_stats(bst[:, 0, :], z[:, 0:512]).then_inc(st, 1)
                v.bn_stats(bst[:, 1, :], z[:, 512:D]).then_inc(st, 1)
                wait_alone(dve, st, t * 3 + 2)
                v.bn_aggr(mv[:], bst[:].rearrange("p a b -> p (a b)")).then_inc(st, 1)
                dve.wait_ge(st, t * 3 + 3)
                v.tensor_scalar(col[:, 0:1], mv[:, 1:2], LN_EPS, None, ALU.add).then_inc(var_ok, 1)
                dve.wait_ge(rstd_ok, t + 1)
                v.tensor_scalar(z[:], z[:], mv[:, 0:1], col[:, 1:2], ALU.subtract, ALU.mult).then_inc(zn_ok, 1)

            def shared_out(u):
                dve.wait_ge(d_done, u + 1)
                dve.wait_ge(base_out, u * 16)
                v.scalar_tensor_tensor(base_sb[:].rearrange("p (q k) -> p q k", k=KD), hp[:].rearrange("p (k q) -> p q k", k=KD), ALPHA,
                                       Y[:, 2:4, :].rearrange("p a (q k) -> p (a q) k", k=KD), ALU.mult, ALU.add).then_inc(base_ok, 1)

            RSTEPS = 29

            def choose(u):
                n = [0]

                def link(ins, alone=False):
                    n[0] += 1
                    ins.then_inc(rt, 1)
                    dve.wait_ge(rt, u * RSTEPS + n[0])
                    if alone:
                        dve.sem_inc(passed, 1)
                dve.wait_ge(sc_ok, u + 1)
                link(v.tensor_tensor(sel[:], sc[:], bias[:], ALU.add), True)
                for q in range(8):
                    ins = v.max(top2[:, q, :], sel[:, 8 * q:8 * q + 8])
                link(ins)
                link(v.tensor_tensor(gs[:], top2[:, :, 0], top2[:, :, 1], ALU.add), True)
                link(v.max(m8[:], gs[:]), True)
                link(v.max_index(i8[:], m8[:], gs[:]))
                link(v.tensor_copy(f8[:], i8[:]))
                link(v.tensor_tensor(prod[:, 0, 0:32].rearrange("p (g k) -> p g k", k=4), iota[:, 0:8].unsqueeze(2).broadcast_to([P, 8, 4]),
                                     f8[:, 0:4].unsqueeze(1).broadcast_to([P, 8, 4]), ALU.is_equal))
                link(v.tensor_reduce(gm[:], prod[:, 0, 0:32].rearrange("p (g k) -> p g k", k=4), AX.X, ALU.add))
                sel3 = sel[:].rearrange("p (g k) -> p g k", k=8)
                link(v.tensor_tensor(sel3, sel3, gm[:].unsqueeze(2).broadcast_to([P, 8, 8]), ALU.mult))
                link(v.tensor_scalar(gm[:], gm[:], 1.0, 1e30, ALU.subtract, ALU.mult))
                link(v.tensor_tensor(sel3, sel3, gm[:].unsqueeze(2).broadcast_to([P, 8, 8]), ALU.add), True)
                link(v.max(m8[:], sel[:]), True)
                link(v.max_index(i8[:], m8[:], sel[:]))
                link(v.tensor_copy(f8[:], i8[:]))
                link(v.tensor_tensor(oh[:], iota[:, 0:NE].unsqueeze(1).broadcast_to([P, TOPK, NE]),
                                     f8[:, 0:TOPK].unsqueeze(2).broadcast_to([P, TOPK, NE]), ALU.is_equal))
                link(v.tensor_reduce(cnt[:], oh[:].rearrange("p k e -> p e k"), AX.X, ALU.add))
                link(v.tensor_scalar(cnt[:], cnt[:], at(valid, u), None, ALU.mult))
                link(v.tensor_tensor(prod[:], oh[:], sc[:].unsqueeze(1).broadcast_to([P, TOPK, NE]), ALU.mult))
                link(v.tensor_reduce(w6[:], prod[:], AX.X, ALU.add))
                link(v.tensor_reduce(wsum[:, 0:1], w6[:], AX.X, ALU.add))
                link(v.reciprocal(wsum[:, 1:2], wsum[:, 0:1]))
                link(v.tensor_scalar(w6[:], w6[:], wsum[:, 1:2], ROUTED_SCALE, ALU.mult, ALU.mult))
                assert n[0] == 22, n

            def place(u):
                n = [22]

                def link(ins):
                    n[0] += 1
                    ins.then_inc(rt, 1)
                    dve.wait_ge(rt, u * RSTEPS + n[0])
                dve.wait_ge(p_done, u + 1)
                link(v.tensor_tensor(rank[:], carry[:], R[:, 64:128], ALU.add))
                v.tensor_tensor(carry[:], carry[:], R[:, 128:192], ALU.add).then_inc(rank_ok, 1)
                link(v.tensor_tensor(rank[:], rank[:], ebase[:], ALU.add))
                link(v.tensor_tensor(prod[:], oh[:], rank[:].unsqueeze(1).broadcast_to([P, TOPK, NE]), ALU.mult))
                link(v.tensor_reduce(slot[:], prod[:], AX.X, ALU.add))
                link(v.scalar_tensor_tensor(slot[:].unsqueeze(1), slot[:].unsqueeze(1), at(valid, u), at(dump, u), ALU.mult, ALU.add))
                dve.wait_ge(listed, u * (16 * TOPK))
                link(v.tensor_copy(entry[:, :, 0], at(tid, u).broadcast_to([P, TOPK])))
                link(v.tensor_copy(entry[:, :, 1].bitcast(F32), w6[:]))
                v.tensor_copy(slot_c[:], slot[:]).then_inc(slot_ok, 1)
                assert n[0] == RSTEPS, n

            def at(x, u):
                return x[:, u:u + 1] if isinstance(u, int) else x[:, bass.ds(u, 1)]

            dve.wait_ge(c_in, 16 * NCONST)
            dve.wait_ge(pl, 2)
            mixing(0)
            layer_norm_1(0)
            with dve.Fori(1, NT) as t:
                mixing(t)
                shared_act(t - 1)
                choose(t - 1)
                layer_norm_1(t)
                shared_out(t - 1)
                place(t - 1)
            shared_act(NT - 1)
            choose(NT - 1)
            shared_out(NT - 1)
            place(NT - 1)

            n = [0]

            def link(ins):
                n[0] += 1
                ins.then_inc(bk, 1)
                dve.wait_ge(bk, n[0])
            dve.wait_ge(rank_ok, NT)
            link(v.tensor_scalar(rank[:], carry[:], P - 1.0, None, ALU.add))
            link(v.tensor_copy(nb_i[:], rank[:]))
            link(v.tensor_scalar(nb_i[:], nb_i[:], 7, None, ALU.logical_shift_right))
            link(v.memset(pre[:], 0.0))
            link(v.tensor_copy(pre[:, 0, 1:], nb_i[:]))
            s, c = 1, 0
            while s <= NE:
                link(v.tensor_copy(pre[:, 1 - c, 0:s], pre[:, c, 0:s]))
                link(v.tensor_tensor(pre[:, 1 - c, s:], pre[:, c, s:], pre[:, c, 0:NE + 1 - s], ALU.add))
                s, c = 2 * s, 1 - c
            start = pre[:, c, :]
            link(v.tensor_scalar(eqk[:], start[:, 1:], pid[:, 0:1], None, ALU.is_le))
            link(v.tensor_reduce(bt[:, 0:1], eqk[:], AX.X, ALU.add))
            other = pre[:, 1 - c, :]
            link(v.tensor_scalar(other, iota[:], bt[:, 0:1], None, ALU.is_equal))
            link(v.tensor_tensor(other, other, start, ALU.mult))
            link(v.tensor_reduce(bt[:, 1:2], other, AX.X, ALU.add))
            link(v.tensor_tensor(bt[:, 2:3], pid[:], bt[:, 1:2], ALU.subtract))
            link(v.tensor_scalar(bt[:, 3:4], bt[:, 0:1], float(TOK), None, ALU.mult))
            link(v.scalar_tensor_tensor(bt[:, 4:5], bt[:, 2:3], float(P), bt[:, 3:4], ALU.mult, ALU.add))
            link(v.tensor_scalar(bt[:, 5:6], bt[:, 0:1], NE - 1.0, None, ALU.min))
            link(v.tensor_scalar(bt[:, 4:5], bt[:, 4:5], float(LIST - P), None, ALU.min))
            link(v.tensor_copy(meta_i[:, 0:1], bt[:, 5:6]))
            link(v.tensor_copy(meta_i[:, 1:2], bt[:, 4:5]))
            link(v.tensor_scalar(bt[:, 6:7], start[:, NE:], 1.0, None, ALU.subtract))
            link(v.tensor_copy(nblk_i[:], bt[:, 6:7]))
            link(v.tensor_scalar(nblk_i[:], nblk_i[:], 1, None, ALU.logical_shift_right))
            assert n[0] == BK_STEPS, n

        @block.tensor
        def _(pe):
            t_ = nc.tensor

            def turn(srcs, bank, n, free):
                pe.wait_ge(tev, free)
                for i, src in enumerate(srcs):
                    mm = t_.transpose(T[bank][:, i * P:(i + 1) * P], src, ident[:])
                mm.then_inc(turned, 1)

            def project_out(out, xT_, w, k0, nk):
                for c in range(2):
                    for k in range(nk):
                        mm = t_.matmul(out[:, c, :], xT_[:, k0 + k, :], w[:, k, c * 512:(c + 1) * 512], start=k == 0, stop=k == nk - 1)
                return mm

            def cols_of(x, lo=0, n=4):
                return [x[:, (lo + i) * P:(lo + i + 1) * P] for i in range(n)]

            def front(t, n0):
                pe.wait_ge(o_in_s, t * 16 + 16)
                turn(cols_of(o_in), 0, n0, n0)
                pe.wait_ge(tev, n0 + 1)
                pe.wait_ge(z_ok, t)
                if isinstance(t, int):
                    pe.wait_ge(mo_in, 16)
                project_out(Y[:, 0:2, :], oT, w_mo, 0, 4).then_inc(y_done, 1)
                pe.wait_ge(ret_ok, t * 3 + 3)
                turn(cols_of(ret), 1, n0 + 1, n0)
                pe.wait_ge(tev, n0 + 2)
                if not isinstance(t, int) or t > 0:
                    pe.wait_ge(base_ok, t - 1)
                if isinstance(t, int):
                    pe.wait_ge(ro_in, 16)
                project_out(Y[:, 2:4, :], oT, w_ro, 4, 4).then_inc(y_done, 1)

            def shared_up(u, n):
                pe.wait_ge(h_ok, u + 1)
                turn(cols_of(hp), 0, n, n - 1)
                turn(cols_of(hp, 4), 1, n + 1, n)
                pe.wait_ge(tev, n + 2)
                pe.wait_ge(act_ok, u)
                for k in range(KD):
                    mm = t_.matmul(GU[:], hT[:, k, :], w_gu[:, k, :], start=k == 0, stop=k == KD - 1)
                mm.then_inc(gu_done, 1)

            def mixed_out(t, n):
                pe.wait_ge(m_ok, t + 1)
                turn(cols_of(mix), 0, n, n - 1)
                turn(cols_of(mix, 4), 1, n + 1, n)

            def router(u):
                pe.wait_ge(rank_ok, u)
                for k in range(KD):
                    mm = t_.matmul(R[:, 0:NE], hT[:, k, :], w_r[:, k, :], start=k == 0, stop=k == KD - 1)
                mm.then_inc(r_done, 1)

            def out_proj(t, n):
                pe.wait_ge(tev, n)
                project_out(Y[:, 0:2, :], mT, w_o, 0, KD).then_inc(w_done, 1)

            def shared_down(u, n):
                pe.wait_ge(act_ok, u + 1)
                turn(cols_of(act_s, 0, 2), 0, n, n - 1)
                pe.wait_ge(tev, n + 1)
                project_out(Y[:, 2:4, :], aT, w_sd, 0, 2).then_inc(d_done, 1)

            def prefix(u):
                pe.wait_ge(rt, u * 29 + 17)
                pe.wait_ge(sc_ok, u + 1)
                t_.matmul(R[:, 64:128], tri[:], cnt[:], start=True, stop=True)
                t_.matmul(R[:, 128:192], ones[:], cnt[:], start=True, stop=True).then_inc(p_done, 1)

            pe.wait_ge(id_in, 16)
            front(0, 0)
            mixed_out(0, 2)
            pe.wait_ge(wo_in, 16)
            out_proj(0, 4)
            pe.wait_ge(c_in, 16 * NCONST)
            pe.wait_ge(w_in_s, 16 * 4)
            with pe.Fori(1, NT) as t:
                n0 = t * 7 - 3
                front(t, n0)
                shared_up(t - 1, n0 + 2)
                mixed_out(t, n0 + 4)
                router(t - 1)
                out_proj(t, n0 + 6)
                shared_down(t - 1, n0 + 6)
                prefix(t - 1)
            n0 = NT * 7 - 3
            shared_up(NT - 1, n0)
            router(NT - 1)
            shared_down(NT - 1, n0 + 2)
            prefix(NT - 1)


def experts(nc, passed, a, h_perm, tok_list, meta, base):
    with ExitStack() as ctx:
        sb = lambda n, s, d=F32: ctx.enter_context(nc.sbuf_tensor("e_" + n, s, d))
        sem = lambda n: ctx.enter_context(nc.semaphore("e_" + n))
        ident = sb("ident", [P, P])
        w_gu = sb("w_gu", [P, 2, KD, 2, FF])
        w_d = sb("w_d", [P, 2, 2, D])
        idx = [sb(f"idx{c}", [P, 2], U32) for c in range(2)]
        s_idx = [sb(f"s_idx{c}", [P, 2], U32) for c in range(2)]
        xg = [sb(f"xg{c}", [P, D]) for c in range(2)]
        xT = sb("xT", [P, 2, KD, P])
        sig = sb("sig", [P, 2, FF])
        act_s = sb("act_s", [P, 2, FF])
        aT = sb("aT", [P, 2, 2, P])
        y_sb = sb("y_sb", [P, 2, D])
        T = [ctx.enter_context(nc.psum_tensor(f"e_T{i}", [P, 512], F32)) for i in range(2)]
        G = [ctx.enter_context(nc.psum_tensor(f"e_G{i}", [P, 512], F32)) for i in range(2)]
        A = ctx.enter_context(nc.psum_tensor("e_A", [P, 512], F32))
        Y = [ctx.enter_context(nc.psum_tensor(f"e_Y{i}", [P, 512], F32)) for i in range(2)]
        c_in = sem("c_in")
        gu_in, d_in, idx_in, s_in, x_in, y_out = [[sem(f"{n}{c}") for c in range(2)] for n in "gu_in d_in idx_in s_in x_in y_out".split()]
        (x_turned, xT_act, xT_dve, gu_done, sig_ok, a1_ok, act_ok, a_turned, aT_ok, d_done, y_act, y_dve) = [sem(n) for n in
            "x_turned xT_act xT_dve gu_done sig_ok a1_ok act_ok a_turned aT_ok d_done y_act y_dve".split()]
        block = ctx.enter_context(nc.Block())

        def wait_alone(eng, s, value):
            eng.wait_ge(s, value)
            eng.sem_inc(passed, 1)

        def pairs(eng):
            return eng.value_load(meta[P:P + 1, 0:1], min_val=(S + DB * DQ) * TOPK // P // 2 - 1, max_val=BLOCKS // 2)

        def number(eng, b, field, top):
            src = meta[b:b + 1, field:field + 1] if isinstance(b, int) else meta[bass.ds(b, 1), field:field + 1]
            return eng.value_load(src, min_val=0, max_val=top)

        @block.sync
        def _(sp):
            sp.dma_start(ident[:], a["ident"]).then_inc(c_in, 16)
            more = pairs(sp)

            def gate_up(e, c, used=None):
                if used is not None:
                    wait_alone(sp, gu_done, used)
                for q, w in enumerate(("w_exp_gate", "w_exp_up")):
                    sp.dma_start(w_gu[:, c, :, q, :], a[w][bass.ds(e, 1)].rearrange("a (p k) n -> p (a k) n", p=P)).then_inc(gu_in[c], 16)

            def down(e, c, used=None):
                if used is not None:
                    wait_alone(sp, d_done, used)
                sp.dma_start(w_d[:, c], a["w_exp_down"][bass.ds(e, 1)].rearrange("a (p k) n -> p (a k) n", p=P)).then_inc(d_in[c], 16)

            expert = lambda b: number(sp, b, 0, NE - 1)
            e0, e1 = expert(0), expert(1)
            gate_up(e0, 0)
            sp.wait_ge(x_in[0], 16)
            gate_up(e1, 1)
            down(e0, 0)
            with sp.Fori(1, more + 1) as r:
                e_last, e0, e1 = [expert(b) for b in (sp.snap(r * 2 - 1), sp.snap(r * 2), sp.snap(r * 2 + 1))]
                n_last, n0, n1 = sp.snap(r * 2 - 2), sp.snap(r * 2 - 1), sp.snap(r * 2)
                gate_up(e0, 0, n0)
                down(e_last, 1, n_last)
                gate_up(e1, 1, n1)
                down(e0, 0, n0)
            down(expert(sp.snap(more * 2 + 1)), 1, sp.snap(more * 2))
            sp.wait_ge(c_in, 16)

        @block.gpsimd
        def _(pool):
            g = nc.gpsimd
            more = pairs(pool)

            def gather(c, n_list, turned=None):
                wait_alone(pool, idx_in[c], n_list)
                if turned is not None:
                    wait_alone(pool, x_turned, turned)
                g.indirect_dma_start(xg[c][:], None, h_perm, bass.IndirectOffsetOnAxis(ap=idx[c][:, 0:1], axis=0)).then_inc(x_in[c], 16)

            def add_rows(b, c, n_before=None):
                pool.wait_ge(y_act, b + 1)
                wait_alone(pool, y_dve, b + 1)
                if n_before is not None:
                    wait_alone(pool, y_out[1 - c], n_before)
                g.indirect_dma_start(base, bass.IndirectOffsetOnAxis(ap=s_idx[c][:, 0:1], axis=0), y_sb[:, c, :], None, compute_op=ALU.add).then_inc(y_out[c], 16)
            gather(0, 16)
            gather(1, 16)
            gather(0, 32, 2)
            gather(1, 32, 4)
            add_rows(0, 0)
            with pool.Fori(2, more + 1) as r:
                gather(0, pool.snap(r * 16 + 16), pool.snap(r * 4 - 2))
                add_rows(pool.snap(r * 2 - 3), 1, pool.snap(r * 16 - 16))
                gather(1, pool.snap(r * 16 + 16), pool.snap(r * 4))
                add_rows(pool.snap(r * 2 - 2), 0, pool.snap(r * 16 - 16))
            add_rows(pool.snap(more * 2 - 1), 1, pool.snap(more * 16))
            add_rows(pool.snap(more * 2), 0, pool.snap(more * 16))
            add_rows(pool.snap(more * 2 + 1), 1, pool.snap(more * 16 + 16))
            wait_alone(pool, y_out[1], pool.snap(more * 16 + 16))

        @block.scalar
        def _(act):
            s_ = nc.scalar
            more = pairs(act)

            entry = lambda b: number(act, b, 1, LIST - P)

            def gather_list(lb, c, gathered=None):
                if gathered is not None:
                    wait_alone(act, x_in[c], gathered)
                act.dma_start(idx[c][:], tok_list[bass.ds(lb, P), :]).then_inc(idx_in[c], 16)

            def add_list(lb, c, added=None):
                if added is not None:
                    wait_alone(act, y_out[c], added)
                act.dma_start(s_idx[c][:], tok_list[bass.ds(lb, P), :]).then_inc(s_in[c], 16)

            def turned(b, c):
                act.wait_ge(x_turned, b * 2 + 1)
                s_.copy(xT[:, c, 0:4, :].rearrange("p k n -> p (k n)"), T[0][:]).then_inc(xT_act, 1)

            def gate(b, c):
                act.wait_ge(gu_done, b + 1)
                s_.activation(sig[:, c, :], G[c][:, 0:FF], ACT.Sigmoid).then_inc(sig_ok, 1)

            def turned_act(b, c):
                act.wait_ge(a_turned, b + 1)
                s_.copy(aT[:, c].rearrange("p k n -> p (k n)"), A[:, 0:2 * P]).then_inc(aT_ok, 1)

            def weigh(b, c, r):
                act.wait_ge(d_done, b + 1)
                act.wait_ge(s_in[c], r * 16 + 16)
                s_.activation(y_sb[:, c, 0:512], Y[0][:], ACT.Copy, scale=s_idx[c][:, 1:2].bitcast(F32)).then_inc(y_act, 1)
            l0, l1, l2 = entry(0), entry(1), entry(2)
            gather_list(l0, 0)
            gather_list(l1, 1)
            add_list(l0, 0)
            turned(0, 0)
            gather_list(l2, 0, 16)
            gate(0, 0)
            turned(1, 1)
            turned_act(0, 0)
            with act.Fori(1, more + 1) as r:
                s1, s0, g1, g0 = [entry(b) for b in (act.snap(r * 2 - 1), act.snap(r * 2), act.snap(r * 2 + 1), act.snap(r * 2 + 2))]
                n_row, n_next, n_last = act.snap(r * 16), act.snap(r * 16 + 16), act.snap(r * 16 - 16)
                gate(r * 2 - 1, 1)
                gather_list(g1, 1, n_row)
                turned(r * 2, 0)
                turned_act(r * 2 - 1, 1)
                add_list(s1, 1, n_last)
                weigh(r * 2 - 2, 0, r - 1)
                gate(r * 2, 0)
                gather_list(g0, 0, n_next)
                turned(r * 2 + 1, 1)
                turned_act(r * 2, 0)
                add_list(s0, 0, n_row)
                weigh(r * 2 - 1, 1, r - 1)
            last = act.snap(more * 2 + 1)
            l1 = entry(last)
            gate(last, 1)
            turned_act(last, 1)
            add_list(l1, 1, act.snap(more * 16))
            weigh(act.snap(more * 2), 0, act.snap(more + 0))
            weigh(last, 1, act.snap(more + 0))
            act.wait_ge(idx_in[0], act.snap(more * 16 + 32))
            act.sem_inc(passed, 1)

        @block.vector
        def _(dve):
            v = nc.vector
            more = pairs(dve)

            def turned(b, c):
                dve.wait_ge(x_turned, b * 2 + 2)
                v.tensor_copy(xT[:, c, 4:8, :].rearrange("p k n -> p (k n)"), T[1][:]).then_inc(xT_dve, 1)

            def gated(b, c):
                dve.wait_ge(sig_ok, b + 1)
                v.tensor_tensor(sig[:, c, :], sig[:, c, :], G[c][:, 0:FF], ALU.mult).then_inc(a1_ok, 1)
                dve.wait_ge(a1_ok, b + 1)
                v.tensor_tensor(act_s[:, c, :].rearrange("p (k q) -> p q k", k=2), sig[:, c, :].rearrange("p (q k) -> p q k", k=2),
                                G[c][:, FF:2 * FF].rearrange("p (q k) -> p q k", k=2), ALU.mult).then_inc(act_ok, 1)

            def weigh(b, c, r):
                dve.wait_ge(d_done, b + 1)
                dve.wait_ge(s_in[c], r * 16 + 16)
                v.tensor_scalar(y_sb[:, c, 512:D], Y[1][:], s_idx[c][:, 1:2].bitcast(F32), None, ALU.mult).then_inc(y_dve, 1)
            turned(0, 0)
            gated(0, 0)
            turned(1, 1)
            with dve.Fori(1, more + 1) as r:
                gated(r * 2 - 1, 1)
                turned(r * 2, 0)
                weigh(r * 2 - 2, 0, r - 1)
                gated(r * 2, 0)
                turned(r * 2 + 1, 1)
                weigh(r * 2 - 1, 1, r - 1)
            gated(dve.snap(more * 2 + 1), 1)
            weigh(dve.snap(more * 2), 0, dve.snap(more + 0))
            weigh(dve.snap(more * 2 + 1), 1, dve.snap(more + 0))

        @block.tensor
        def _(pe):
            t_ = nc.tensor
            more = pairs(pe)

            def turn(b, c, r):
                pe.wait_ge(x_in[c], r * 16 + 16)
                for q in range(2):
                    pe.wait_ge((xT_act, xT_dve)[q], b)
                    for k in range(4):
                        mm = t_.transpose(T[q][:, k * P:(k + 1) * P], xg[c][:, (4 * q + k) * P:(4 * q + k + 1) * P], ident[:])
                    mm.then_inc(x_turned, 1)

            def gate_up(b, c, r):
                pe.wait_ge(gu_in[c], r * 32 + 32)
                pe.wait_ge(xT_act, b + 1)
                for k in range(KD):
                    if k == 4:
                        pe.wait_ge(xT_dve, b + 1)
                    mm = t_.matmul(G[c][:], xT[:, c, k, :], w_gu[:, c, k, :, :].rearrange("p q n -> p (q n)"), start=k == 0, stop=k == KD - 1)
                mm.then_inc(gu_done, 1)

            def turn_act(b, c):
                pe.wait_ge(act_ok, b + 1)
                pe.wait_ge(aT_ok, b)
                for k in range(2):
                    mm = t_.transpose(A[:, k * P:(k + 1) * P], act_s[:, c, k * P:(k + 1) * P], ident[:])
                mm.then_inc(a_turned, 1)

            def down(b, c, r):
                pe.wait_ge(d_in[c], r * 16 + 16)
                pe.wait_ge(aT_ok, b + 1)
                pe.wait_ge(y_act, b)
                pe.wait_ge(y_dve, b)
                for q in range(2):
                    for k in range(2):
                        mm = t_.matmul(Y[q][:], aT[:, c, k, :], w_d[:, c, k, q * 512:(q + 1) * 512], start=k == 0, stop=k == 1)
                mm.then_inc(d_done, 1)
            pe.wait_ge(c_in, 16)
            turn(0, 0, 0)
            gate_up(0, 0, 0)
            turn(1, 1, 0)
            turn_act(0, 0)
            with pe.Fori(1, more + 1) as r:
                gate_up(r * 2 - 1, 1, r - 1)
                turn(r * 2, 0, r)
                turn_act(r * 2 - 1, 1)
                down(r * 2 - 2, 0, r - 1)
                gate_up(r * 2, 0, r)
                turn(r * 2 + 1, 1, r)
                turn_act(r * 2, 0)
                down(r * 2 - 1, 1, r - 1)
            gate_up(pe.snap(more * 2 + 1), 1, pe.snap(more + 0))
            turn_act(pe.snap(more * 2 + 1), 1)
            down(pe.snap(more * 2), 0, pe.snap(more + 0))
            down(pe.snap(more * 2 + 1), 1, pe.snap(more + 0))


def finish(nc, a, base, out_p, out_s):
    with ExitStack() as ctx:
        sb = lambda n, s, d=F32: ctx.enter_context(nc.sbuf_tensor("c_" + n, s, d))
        sem = lambda n: ctx.enter_context(nc.semaphore("c_" + n))
        g2 = sb("g2", [P, D])
        b2 = sb("b2", [P, D])
        acc = sb("acc", [P, NT, D])
        bst = sb("bst", [P, NT, 12])
        mv = sb("mv", [P, NT, 2])
        col = sb("col", [P, NT, 2])
        mhalf = sb("mhalf", [P, 1])
        nbias = sb("nbias", [P, NT])
        nb_ok = sem("nb_ok")
        c_in, pl, st, var_ok, rstd_ok, zn, gained, out_ok, o_out = [sem(n) for n in "c_in pl st var_ok rstd_ok zn gained out_ok o_out".split()]
        acc_in = [sem(f"acc_in{t}") for t in range(NT)]
        block = ctx.enter_context(nc.Block())

        @block.sync
        def _(sp):
            for t in range(NT):
                sp.dma_start(acc[:, t, :], base[t * P:(t + 1) * P, :]).then_inc(acc_in[t], 16)
                if t == 1:
                    sp.dma_start(g2[:], a["ln2_g"].partition_broadcast(P)).then_inc(c_in, 16)
                    sp.dma_start(b2[:], a["ln2_b"].partition_broadcast(P)).then_inc(c_in, 16)
            for t in range(NT):
                sp.wait_ge(out_ok, t + 1)
                if t < NT - 1:
                    sp.dma_start(out_p[t * P:(t + 1) * P, :], acc[:, t, :]).then_inc(o_out, 16)
                else:
                    sp.dma_start(out_s, acc[0:DB * DQ, t, :]).then_inc(o_out, 16)
            sp.wait_ge(o_out, 16 * NT)

        @block.gpsimd
        def _(pool):
            nc.gpsimd.memset(mhalf[:], -0.5).then_inc(pl, 1)
            pool.wait_ge(pl, 1)

            def gain(t):
                pool.wait_ge(c_in, 32)
                pool.wait_ge(zn, t + 1)
                nc.gpsimd.tensor_tensor(acc[:, t, :], acc[:, t, :], g2[:], ALU.mult).then_inc(gained, 1)
            for t in range(NT):
                pool.wait_ge(var_ok, t + 1)
                nc.gpsimd.tensor_tensor(col[:, t, 1:2], col[:, t, 0:1], mhalf[:], ALU.pow).then_inc(rstd_ok, 1)
                if t:
                    gain(t - 1)
            gain(NT - 1)

        @block.vector
        def _(dve):
            v = nc.vector

            def statistics(t):
                x = acc[:, t, :]
                dve.wait_ge(acc_in[t], 16)
                v.bn_stats(bst[:, t, 0:6], x[:, 0:512]).then_inc(st, 1)
                v.bn_stats(bst[:, t, 6:12], x[:, 512:D]).then_inc(st, 1)
                dve.wait_ge(st, 3 * t + 2)
                v.bn_aggr(mv[:, t, :], bst[:, t, :]).then_inc(st, 1)
                dve.wait_ge(st, 3 * t + 3)
                v.tensor_scalar(col[:, t, 0:1], mv[:, t, 1:2], LN_EPS, None, ALU.add).then_inc(var_ok, 1)

            def shifted(t):
                dve.wait_ge(gained, t + 1)
                v.tensor_tensor(acc[:, t, :], acc[:, t, :], b2[:], ALU.add).then_inc(out_ok, 1)
            statistics(0)
            dve.wait_ge(c_in, 32)
            for t in range(NT):
                if t + 1 < NT:
                    statistics(t + 1)
                dve.wait_ge(rstd_ok, t + 1)
                v.scalar_tensor_tensor(nbias[:, t:t + 1], mv[:, t, 0:1], -1.0, col[:, t, 1:2], ALU.mult, ALU.mult).then_inc(nb_ok, 1)
                if t > 1:
                    shifted(t - 2)
            shifted(NT - 2)
            shifted(NT - 1)

        @block.scalar
        def _(act):
            for t in range(NT):
                act.wait_ge(nb_ok, t + 1)
                nc.scalar.activation(acc[:, t, :], acc[:, t, :], ACT.Identity, bias=nbias[:, t:t + 1], scale=col[:, t, 1:2]).then_inc(zn, 1)


def program(nc, a, o):
    def dram(name, shape, dt=F32):
        return nc.dram_tensor("d_" + name, shape, dt).ap()
    proj = dram("proj", (TOK, IN_W))
    retn = dram("retn", (TOK, 512))
    o_mla = dram("o_mla", (TOK, 512))
    h_perm = dram("h_perm", (TOK + P, D))
    base = dram("base", (TOK + P, D))
    tok_list = dram("tok_list", (LIST, 2), U32)
    meta = dram("meta", (P + 1, 2), I32)
    with nc.semaphore("passed") as passed:
        with (nc.sbuf_tensor("x_sb", [P, KD, TOK], F32) as x_sb, nc.sbuf_tensor("gw_sb", [P, 2, KD, FW], F32) as gw_sb,
              nc.semaphore("gw_in0") as gw_in0, nc.semaphore("gw_in1") as gw_in1):
            gw_in = (gw_in0, gw_in1)
            project(nc, passed, x_sb, gw_sb, gw_in, a["xT"], a["w_in"], proj)
            with nc.cleanup_on_exit():
                retention(nc, passed, x_sb, gw_sb, gw_in, a, proj, retn, o["ret_p"], o["ret_s"])
        attention(nc, passed, a, proj, o_mla, o["ckv_p"], o["ckv_s"], o["kr_p"], o["kr_s"])
        merge(nc, passed, a, proj, o_mla, retn, h_perm, base, tok_list, meta)
        experts(nc, passed, a, h_perm, tok_list, meta, base)
        finish(nc, a, base, o["y_p"], o["y_s"])


def host_arrays(i):
    import numpy as np
    f = np.float32
    x = np.concatenate([i["x_prompt"].reshape(1024, D), i["x_sample"].reshape(32, D), np.zeros((96, D), f)])
    pos = np.concatenate([np.arange(S), np.tile(PAST + np.arange(DQ), DB), np.zeros(96)]).astype(f)

    def angles(half):
        inv = f(10000.0) ** (-np.arange(half, dtype=f) / f(half))
        ang = pos[:, None] * inv[None, :]
        return np.cos(ang).astype(f), np.sin(ang).astype(f)
    c16, s16 = angles(HALF)
    wq = i["w_q_up"].reshape(QL, HEADS, NOPE + ROPE)
    wq = np.concatenate([wq, wq[:, :, NOPE + HALF:], wq[:, :, NOPE:NOPE + HALF]], axis=2)
    c64, s64 = angles(64)
    kscale = f(128 ** -0.5)
    lg = np.log(f(1.0) - f(2.0) ** (-5 - np.arange(4, dtype=f)))
    idx = np.arange(P, dtype=f)
    diff = idx[None, :] - idx[:, None]

    def decay_mask(m):
        return np.where(m >= 0, np.exp(np.maximum(m, 0)[None] * lg[:, None, None]), 0).astype(f)
    same = np.kron(np.eye(DB), np.ones((DQ, DQ)))
    d_s = np.where(same > 0, np.tile(diff[0:DQ, 0:DQ], (DB, DB)), -1)
    q_idx = np.concatenate([np.tile(idx, 8), np.tile(idx[0:DQ], DB), np.zeros(96, f)])
    qdec = np.exp((q_idx[None, :] + 1) * lg[:, None]).astype(f)
    cols = np.zeros((4, P, 11), f)
    cols[:, :, 0] = np.exp((P - 1 - idx)[None, :] * lg[:, None])
    for b in range(DB):
        cols[:, DQ * b:DQ * (b + 1), 1 + b] = np.exp((DQ - 1 - idx[0:DQ])[None, :] * lg[:, None])
    cols *= kscale
    cols[:, :, 9] = np.exp(P * lg)[:, None]
    cols[:, :, 10] = np.exp(DQ * lg)[:, None]
    real = (np.arange(TOK) < S + DB * DQ).astype(f).reshape(NT, P).T
    tri = np.where(np.arange(P)[None, :] <= np.arange(P)[:, None], 0, -1e30).astype(f)
    h = {
        "xT": x.T, "x": x, "w_in": i["w_in"], "ident": np.eye(P, dtype=f),
        "kv_norm_g": i["kv_norm_g"], "q_norm_gT": i["q_norm_g"].reshape(2, P).T,
        "rope16": np.stack([c16, s16]),
        "rope_q": np.concatenate([c16.T, c16.T, -s16.T, s16.T]) * f(SCALE),
        "causal": tri, "causal_s": np.tile(tri[0:DQ, 0:DQ], (HEADS, 1)),
        "w_uv": i["w_uv"],
        "rope64": np.stack([c64, s64]),
        "dmask": decay_mask(diff) * kscale, "dmask_s": decay_mask(d_s) * kscale,
        "qdec": np.repeat(qdec[:, None, :], P, axis=1), "ret_cols": cols,
        "state_ret": i["state_ret"],
        "tri": (np.arange(P)[:, None] < np.arange(P)[None, :]).astype(f), "ones": np.ones((P, P), f),
        "iota": np.tile(np.arange(NE + 1, dtype=f), (P, 1)), "ebase": np.tile(np.arange(NE, dtype=f) * TOK, (P, 1)),
        "pid": np.arange(P, dtype=f)[:, None], "valid": real,
        "dump": ((1 - real)[:, :, None] * (NE * TOK + P * np.arange(TOPK)[None, None, :] + np.arange(P)[:, None, None])).astype(f),
        "list_fill": np.stack([TOK + np.arange(LIST) % P, np.zeros(LIST)], axis=1).astype(np.uint32), "zero_rows": np.zeros((P, D), f),
        "tid": (np.arange(NT)[None, :] * P + np.arange(P)[:, None]).astype(np.uint32),
        **{k: i[k] for k in ("ret_gn_g", "ln1_g", "ln1_b", "ln2_g", "ln2_b", "router_bias", "w_mla_o", "w_ret_o", "w_out", "w_router",
                             "w_sh_gate", "w_sh_up", "w_sh_down", "w_exp_gate", "w_exp_up", "w_exp_down")},
        "w_q_ext": wq.transpose(1, 0, 2),
        "w_uk_h": i["w_uk"].reshape(KVL, HEADS, NOPE).transpose(1, 0, 2),
        "w_ukT_h": i["w_uk"].reshape(KVL, HEADS, NOPE).transpose(1, 2, 0),
        "page_table": i["page_table"], "cache_ckv": i["cache_ckv"],
        "cache_ckvT": i["cache_ckv"].transpose(0, 2, 1), "cache_kropeT": i["cache_krope"].transpose(0, 2, 1),
    }
    return {k: np.ascontiguousarray(v) for k, v in h.items()}


OUTS = {"y_p": (1024, 1024), "y_s": (32, 1024), "ckv_p": (1024, 128), "ckv_s": (32, 128), "kr_p": (1024, 32), "kr_s": (32, 32), "ret_p": (4, 128, 128), "ret_s": (8, 4, 128, 128)}


RETURNED = {"y_p": (1, S, D), "y_s": (DB, DQ, D), "ckv_p": (1, S, KVL), "kr_p": (1, S, ROPE), "ret_p": (1, 4, 128, 128),
            "ckv_s": (DB, DQ, KVL), "kr_s": (DB, DQ, ROPE), "ret_s": (DB, 4, 128, 128)}


def kernel(**inputs):
    import concourse.bacc as bacc
    from concourse.bass_utils import run_bass_kernel_spmd as run
    nc = bacc.Bacc("TRN2", target_bir_lowering=False, num_devices=1)
    host = host_arrays(inputs)
    a = {k: nc.dram_tensor("in_" + k, v.shape, mybir.dt.from_np(v.dtype), kind="ExternalInput").ap() for k, v in host.items()}
    o = {k: nc.dram_tensor("out_" + k, s, F32, kind="ExternalOutput").ap() for k, s in OUTS.items()}
    program(nc, a, o)
    r = run(nc, [{"in_" + k: v for k, v in host.items()}], core_ids=[0])
    got = r.results[0]
    return tuple(got["out_" + k].reshape(s) for k, s in RETURNED.items())
```
